# Optimizing a Trainium2 kernel written in Bass

```python
import math
import jax, jax.numpy as jnp
from jax import lax
import numpy as np

D_MODEL = 1024
BATCH = 1
SEQ = 256
DEPTH = 1

HG_HEADS = 4
HG_KDIM = 128
HG_VDIM = 128
HG_KWIDTH = HG_HEADS * HG_KDIM
HG_WIDTH = HG_HEADS * HG_VDIM
DA_HEADS = 4
DA_HEAD_DIM = 64
DA_WIDTH = DA_HEADS * 2 * DA_HEAD_DIM
MIX_WIDTH = HG_WIDTH + DA_WIDTH
IN_SIZES = (HG_KWIDTH, HG_KWIDTH, HG_WIDTH, HG_WIDTH, DA_WIDTH, DA_WIDTH, DA_WIDTH)
IN_WIDTH = sum(IN_SIZES)
D_FF = -(-8 * D_MODEL // (3 * 256)) * 256
CHUNK = 64
Q_BLOCK = 128
EPS = 1e-6
N_MOD = 6


def rmsnorm(x, w):
    x32 = x.astype(jnp.float32)
    y = x32 * lax.rsqrt(jnp.mean(x32 * x32, axis=-1, keepdims=True) + EPS)
    return (y * w.astype(jnp.float32)).astype(x.dtype)

def alibi_slopes(n):
    return jnp.asarray(np.array([2.0 ** (-8.0 * (h + 1) / n) for h in range(n)], dtype=np.float32))

def hgrn2(q, f_logit, i, g, lb, gnorm_w):
    B, T, _ = q.shape
    n = T // CHUNK
    f = lb + (1.0 - lb) * jax.nn.sigmoid(f_logit.astype(jnp.float32))
    logf = jnp.log(f)
    k = 1.0 - f

    def heads(t, d):
        return t.reshape(B, n, CHUNK, HG_HEADS, d).transpose(1, 0, 3, 2, 4)

    qc = heads(q.astype(jnp.float32), HG_KDIM)
    kc = heads(k, HG_KDIM)
    vc = heads(i.astype(jnp.float32), HG_VDIM)
    bc = jnp.cumsum(heads(logf, HG_KDIM), axis=3)
    causal = jnp.tril(jnp.ones((CHUNK, CHUNK), dtype=bool))[:, :, None]

    def step(S, inp):
        qb, kb, vb, bb = inp
        o_inter = jnp.einsum('bhtk,bhkv->bhtv', qb * jnp.exp(bb), S)
        rel = bb[:, :, :, None, :] - bb[:, :, None, :, :]
        decay = jnp.exp(jnp.where(causal, rel, -jnp.inf))
        A = jnp.einsum('bhtk,bhsk,bhtsk->bhts', qb, kb, decay)
        o = o_inter + jnp.einsum('bhts,bhsv->bhtv', A, vb)
        blast = bb[:, :, -1:, :]
        S_new = jnp.exp(blast[:, :, 0, :])[..., None] * S + jnp.einsum('bhsk,bhsv->bhkv', kb * jnp.exp(blast - bb), vb)
        return S_new, o

    S0 = jnp.zeros((B, HG_HEADS, HG_KDIM, HG_VDIM), jnp.float32)
    _, o = lax.scan(step, S0, (qc, kc, vc, bc))
    o = o.transpose(1, 0, 3, 2, 4).reshape(B, T, HG_HEADS, HG_VDIM)
    o = rmsnorm(o, gnorm_w) * jax.nn.silu(g.reshape(B, T, HG_HEADS, HG_VDIM).astype(jnp.float32))
    return o.reshape(B, T, HG_WIDTH).astype(q.dtype)

def diff_attention(q, k, v, lam, lambda_init, subln_w):
    B, T, _ = q.shape
    d = DA_HEAD_DIM
    q = q.reshape(B, T, DA_HEADS, 2, d).transpose(0, 2, 3, 1, 4)
    k = k.reshape(B, T, DA_HEADS, 2, d).transpose(0, 2, 3, 1, 4)
    v = v.reshape(B, T, DA_HEADS, 2 * d).transpose(0, 2, 1, 3)
    scale = d ** -0.5
    slopes = alibi_slopes(DA_HEADS)
    pos = jnp.arange(T)
    outs = []
    for blk in range(T // Q_BLOCK):
        lo, hi = blk * Q_BLOCK, (blk + 1) * Q_BLOCK
        qb, kb, vb = q[:, :, :, lo:hi], k[:, :, :, :hi], v[:, :, :hi]
        s = jnp.einsum('bhmqd,bhmkd->bhmqk', qb, kb).astype(jnp.float32) * scale
        dist = (pos[lo:hi, None] - pos[None, :hi]).astype(jnp.float32)
        s = s - (slopes[:, None, None] * dist)[None, :, None]
        s = jnp.where(dist >= 0, s, -jnp.inf)
        p = jax.nn.softmax(s, axis=-1)
        w = p[:, :, 0] - lam * p[:, :, 1]
        outs.append(jnp.einsum('bhqk,bhkv->bhqv', w.astype(v.dtype), vb))
    o = jnp.concatenate(outs, axis=2)
    o = rmsnorm(o, subln_w) * (1.0 - lambda_init)
    return o.transpose(0, 2, 1, 3).reshape(B, T, DA_WIDTH)

def first_inputs(seed: int = 0) -> dict:
    key = jax.random.key(seed)
    ks = jax.random.split(key, 20)
    f32 = jnp.float32
    nrm = lambda k, shape, s: jax.random.normal(k, shape, f32) * s
    return {
        "x": nrm(ks[0], (BATCH, SEQ, D_MODEL), 1.0),
        "c": nrm(ks[1], (BATCH, D_MODEL), 1.0),
        "w_ada": nrm(ks[2], (DEPTH, D_MODEL, N_MOD * D_MODEL), 0.5 * D_MODEL ** -0.5),
        "b_ada": nrm(ks[3], (DEPTH, N_MOD * D_MODEL), 0.01),
        "norm1_w": 1.0 + nrm(ks[4], (DEPTH, D_MODEL), 0.02),
        "w_in": nrm(ks[5], (DEPTH, D_MODEL, IN_WIDTH), D_MODEL ** -0.5),
        "hgrn_lb_logits": nrm(ks[6], (DEPTH + 1, HG_KWIDTH), 0.5),
        "hgrn_gnorm_w": 1.0 + nrm(ks[7], (DEPTH, HG_VDIM), 0.02),
        "diff_lambda_q1": nrm(ks[8], (DEPTH, DA_HEAD_DIM), 0.1),
        "diff_lambda_k1": nrm(ks[9], (DEPTH, DA_HEAD_DIM), 0.1),
        "diff_lambda_q2": nrm(ks[10], (DEPTH, DA_HEAD_DIM), 0.1),
        "diff_lambda_k2": nrm(ks[11], (DEPTH, DA_HEAD_DIM), 0.1),
        "diff_subln_w": 1.0 + nrm(ks[12], (DEPTH, 2 * DA_HEAD_DIM), 0.02),
        "w_out": nrm(ks[13], (DEPTH, MIX_WIDTH, D_MODEL), MIX_WIDTH ** -0.5),
        "norm2_w": 1.0 + nrm(ks[14], (DEPTH, D_MODEL), 0.02),
        "w_ffn_gate": nrm(ks[15], (DEPTH, D_MODEL, D_FF), D_MODEL ** -0.5),
        "w_ffn_up": nrm(ks[16], (DEPTH, D_MODEL, D_FF), D_MODEL ** -0.5),
        "w_ffn_down": nrm(ks[17], (DEPTH, D_FF, D_MODEL), D_FF ** -0.5),
        "final_norm_w": 1.0 + nrm(ks[18], (D_MODEL,), 0.02),
    }

def first_block(x, c, w_ada, b_ada, norm1_w, w_in, hgrn_lb_logits, hgrn_gnorm_w,
              diff_lambda_q1, diff_lambda_k1, diff_lambda_q2, diff_lambda_k2, diff_subln_w,
              w_out, norm2_w, w_ffn_gate, w_ffn_up, w_ffn_down, final_norm_w):
    offs = np.cumsum(IN_SIZES)[:-1].tolist()
    lower_bounds = jnp.cumsum(jax.nn.softmax(hgrn_lb_logits.astype(jnp.float32), axis=0), axis=0)
    h = x
    for l in range(DEPTH):
        mod = jax.nn.silu(c) @ w_ada[l] + b_ada[l]
        sh1, sc1, g1, sh2, sc2, g2 = jnp.split(mod[:, None, :], N_MOD, axis=-1)
        u = rmsnorm(h, norm1_w[l]) * (1.0 + sc1) + sh1
        proj = u @ w_in[l]
        hq, hf, hi, hg, aq, ak, av = jnp.split(proj, offs, axis=-1)
        o_hg = hgrn2(hq, hf, hi, hg, lower_bounds[l], hgrn_gnorm_w[l])
        lambda_init = 0.8 - 0.6 * math.exp(-0.3 * l)
        lam = (jnp.exp(jnp.sum(diff_lambda_q1[l].astype(jnp.float32) * diff_lambda_k1[l].astype(jnp.float32)))
               - jnp.exp(jnp.sum(diff_lambda_q2[l].astype(jnp.float32) * diff_lambda_k2[l].astype(jnp.float32)))
               + lambda_init)
        o_da = diff_attention(aq, ak, av, lam, lambda_init, diff_subln_w[l])
        mix = jnp.concatenate([o_hg, o_da.astype(o_hg.dtype)], axis=-1) @ w_out[l]
        h = h + g1 * mix
        u = rmsnorm(h, norm2_w[l]) * (1.0 + sc2) + sh2
        ff = (jax.nn.silu(u @ w_ffn_gate[l]) * (u @ w_ffn_up[l])) @ w_ffn_down[l]
        h = h + g2 * ff
    return rmsnorm(h, final_norm_w)


GLA_HEADS = 4
GLA_DK = 128
GLA_DV = 256
GLA_QK = GLA_HEADS * GLA_DK
GLA_V = GLA_HEADS * GLA_DV
GLA_GATE_RANK = 16
GLA_GATE_TEMP = 16.0
RET_HEADS = 4
RET_DK = 256
RET_DV = 512
RET_QK = RET_HEADS * RET_DK
RET_V = RET_HEADS * RET_DV
ROPE_BASE = 10000.0
IN_SPLITS = (GLA_QK, GLA_QK, GLA_V, GLA_V, GLA_GATE_RANK, RET_QK, RET_QK, RET_V, RET_V, D_MODEL, D_MODEL)
D_IN = sum(IN_SPLITS)
N_GROUPS = 4
EXPERTS_PER_GROUP = 8
N_EXPERTS = N_GROUPS * EXPERTS_PER_GROUP
TOP_K_IN_GROUP = 2
EXPERT_HIDDEN = 512
EXPERT_BLOCK = 128


def _rmsnorm(x, w):
    x32 = x.astype(jnp.float32)
    y = x32 * lax.rsqrt(jnp.mean(x32 * x32, axis=-1, keepdims=True) + EPS)
    return (y * w.astype(jnp.float32)).astype(x.dtype)

def _group_norm(o, w):
    mu = jnp.mean(o, axis=-1, keepdims=True)
    var = jnp.mean(jnp.square(o - mu), axis=-1, keepdims=True)
    y = ((o - mu) * lax.rsqrt(var + EPS)).reshape(o.shape[0], o.shape[1], -1)
    return y * w.astype(jnp.float32)

def _to_chunks(t):
    b, h, s, d = t.shape
    return t.reshape(b, h, s // CHUNK, CHUNK, d).transpose(2, 0, 1, 3, 4)

def _from_chunks(t):
    n, b, h, c, d = t.shape
    return t.transpose(1, 0, 3, 2, 4).reshape(b, n * c, h, d)

def _gla_chunked(q, k, v, log_a):
    b, h, _, dk = q.shape
    dv = v.shape[-1]
    causal = jnp.tril(jnp.ones((CHUNK, CHUNK), dtype=bool))[:, :, None]

    def step(state, inp):
        qi, ki, vi, ai = inp
        cum = jnp.cumsum(ai, axis=-2)
        diff = cum[..., :, None, :] - cum[..., None, :, :]
        decay = jnp.exp(jnp.where(causal, diff, -jnp.inf))
        scores = jnp.einsum("bhid,bhijd,bhjd->bhij", qi, decay, ki)
        o = (jnp.einsum("bhij,bhjv->bhiv", scores, vi)
             + jnp.einsum("bhid,bhdv->bhiv", qi * jnp.exp(cum), state))
        last = cum[..., -1:, :]
        state = (jnp.exp(last[..., 0, :])[..., None] * state
                 + jnp.einsum("bhjd,bhjv->bhdv", ki * jnp.exp(last - cum), vi))
        return state, o

    init = jnp.zeros((b, h, dk, dv), jnp.float32)
    xs = tuple(_to_chunks(t.astype(jnp.float32)) for t in (q, k, v, log_a))
    _, out = lax.scan(step, init, xs)
    return _from_chunks(out)

def _retention_chunked(q, k, v):
    b, h, _, dk = q.shape
    dv = v.shape[-1]
    log_gamma = jnp.log(1.0 - 2.0 ** (-5.0 - jnp.arange(h, dtype=jnp.float32)))
    idx = jnp.arange(CHUNK, dtype=jnp.float32)
    rel = idx[:, None] - idx[None, :]
    intra = jnp.where(rel >= 0, jnp.exp(log_gamma[:, None, None] * jnp.maximum(rel, 0.0)), 0.0)
    q_dec = jnp.exp(log_gamma[:, None] * (idx + 1.0))[:, :, None]
    k_dec = jnp.exp(log_gamma[:, None] * (CHUNK - 1.0 - idx))[:, :, None]
    chunk_dec = jnp.exp(log_gamma * CHUNK)[:, None, None]

    def step(state, inp):
        qi, ki, vi = inp
        scores = jnp.einsum("bhid,bhjd->bhij", qi, ki) * intra
        o = (jnp.einsum("bhij,bhjv->bhiv", scores, vi)
             + jnp.einsum("bhid,bhdv->bhiv", qi * q_dec, state))
        state = chunk_dec * state + jnp.einsum("bhjd,bhjv->bhdv", ki * k_dec, vi)
        return state, o

    init = jnp.zeros((b, h, dk, dv), jnp.float32)
    xs = tuple(_to_chunks(t.astype(jnp.float32)) for t in (q, k, v))
    _, out = lax.scan(step, init, xs)
    return _from_chunks(out)

def _rotary(t, positions):
    dk = t.shape[-1]
    theta = 1.0 / (ROPE_BASE ** jnp.linspace(0.0, 1.0, dk // 2, dtype=jnp.float32))
    theta = jnp.repeat(theta, 2)
    ang = positions.astype(jnp.float32)[:, :, None, None] * theta
    t32 = t.astype(jnp.float32)
    rot = jnp.stack([-t32[..., 1::2], t32[..., 0::2]], axis=-1).reshape(t.shape)
    return t32 * jnp.cos(ang) + rot * jnp.sin(ang)

def _hybrid_mixer(u, positions, w_in, gk_up, gk_bias, gla_norm_w, w_br_gla, ret_norm_w, w_br_ret, w_out):
    B, S, _ = u.shape
    proj = u @ w_in
    splits = np.cumsum(IN_SPLITS)[:-1].tolist()
    gq, gk, gv, gg, gdown, rq, rk, rv, rg, mga, mgb = jnp.split(proj, splits, axis=-1)

    def heads(t, h):
        return t.reshape(B, S, h, -1).transpose(0, 2, 1, 3)

    log_a = jax.nn.log_sigmoid((gdown @ gk_up + gk_bias).astype(jnp.float32)) / GLA_GATE_TEMP
    o_gla = _gla_chunked(heads(gq * (GLA_DK ** -0.5), GLA_HEADS), heads(gk, GLA_HEADS),
                         heads(gv, GLA_HEADS), heads(log_a, GLA_HEADS))
    o_gla = _rmsnorm(o_gla, gla_norm_w).reshape(B, S, GLA_V) * jax.nn.silu(gg.astype(jnp.float32))

    q_r = _rotary(rq.reshape(B, S, RET_HEADS, RET_DK), positions).transpose(0, 2, 1, 3)
    k_r = (_rotary(rk.reshape(B, S, RET_HEADS, RET_DK), positions) * (RET_DK ** -0.5)).transpose(0, 2, 1, 3)
    o_ret = _retention_chunked(q_r, k_r, heads(rv, RET_HEADS))
    o_ret = _group_norm(o_ret, ret_norm_w) * jax.nn.silu(rg.astype(jnp.float32))

    y_a = o_gla.astype(u.dtype) @ w_br_gla
    y_b = o_ret.astype(u.dtype) @ w_br_ret
    merged = (jax.nn.sigmoid(mga.astype(jnp.float32)) * y_a.astype(jnp.float32)
              + jax.nn.sigmoid(mgb.astype(jnp.float32)) * y_b.astype(jnp.float32))
    return merged.astype(u.dtype) @ w_out

def _hierarchical_moe(u, rg_w, rg_b, re_w, re_b, wg, wu, wd):
    B, S, D = u.shape
    t = u.reshape(-1, D)
    n = t.shape[0]
    g_logits = (t @ rg_w + rg_b).astype(jnp.float32)
    g_prob = jax.nn.softmax(g_logits, axis=-1)
    g_idx = jnp.argmax(g_logits, axis=-1)
    g_w = jnp.take_along_axis(g_prob, g_idx[:, None], axis=-1)
    e_all = (jnp.einsum("nd,gde->nge", t, re_w) + re_b).astype(jnp.float32)
    e_logits = jnp.take_along_axis(e_all, g_idx[:, None, None], axis=1)[:, 0]
    top_v, top_i = lax.top_k(e_logits, TOP_K_IN_GROUP)
    weights = g_w * jax.nn.softmax(top_v, axis=-1)
    expert_ids = g_idx[:, None] * EXPERTS_PER_GROUP + top_i

    n_assign = n * TOP_K_IN_GROUP
    flat_e = expert_ids.reshape(-1)
    flat_w = weights.reshape(-1)
    flat_tok = jnp.repeat(jnp.arange(n, dtype=jnp.int32), TOP_K_IN_GROUP)
    order = jnp.argsort(flat_e)
    sorted_e = flat_e[order]
    counts = jnp.bincount(flat_e, length=N_EXPERTS)
    padded = ((counts + EXPERT_BLOCK - 1) // EXPERT_BLOCK) * EXPERT_BLOCK
    pad_end = jnp.cumsum(padded)
    pad_start = pad_end - padded
    start = jnp.cumsum(counts) - counts
    dest = pad_start[sorted_e] + (jnp.arange(n_assign) - start[sorted_e])
    n_slots = ((n_assign + N_EXPERTS * (EXPERT_BLOCK - 1) + EXPERT_BLOCK - 1) // EXPERT_BLOCK) * EXPERT_BLOCK
    n_blocks = n_slots // EXPERT_BLOCK
    slot_tok = jnp.zeros((n_slots,), jnp.int32).at[dest].set(flat_tok[order])
    slot_w = jnp.zeros((n_slots,), jnp.float32).at[dest].set(flat_w[order])
    block_start = jnp.arange(n_blocks) * EXPERT_BLOCK
    block_expert = jnp.minimum(jnp.searchsorted(pad_end, block_start, side="right"), N_EXPERTS - 1)

    def run_block(args):
        e, tok, w = args
        xb = t[tok]
        hid = jax.nn.silu(xb @ wg[e]) * (xb @ wu[e])
        return ((hid @ wd[e]).astype(jnp.float32) * w[:, None])

    outs = lax.map(run_block, (block_expert, slot_tok.reshape(n_blocks, EXPERT_BLOCK),
                               slot_w.reshape(n_blocks, EXPERT_BLOCK)))
    y = jnp.zeros((n, D), jnp.float32).at[slot_tok].add(outs.reshape(n_slots, D))
    return y.reshape(B, S, D).astype(u.dtype)

def second_inputs(seed: int = 0) -> dict:
    key = jax.random.key(seed)
    ks = jax.random.split(key, 24)
    f32 = jnp.float32

    def nrm(k, shape, scale):
        return jax.random.normal(k, shape, f32) * scale

    x = jax.random.normal(ks[0], (BATCH, SEQ, D_MODEL), f32)
    offsets = jax.random.randint(ks[1], (BATCH, 1), 0, 512)
    positions = (jnp.arange(SEQ, dtype=jnp.int32)[None, :] + offsets).astype(jnp.int32)
    return {
        "x": x,
        "positions": positions,
        "norm_mix_w": 1.0 + nrm(ks[2], (DEPTH, D_MODEL), 0.02),
        "w_in": nrm(ks[3], (DEPTH, D_MODEL, D_IN), D_MODEL ** -0.5),
        "gla_gk_up": nrm(ks[4], (DEPTH, GLA_GATE_RANK, GLA_QK), GLA_GATE_RANK ** -0.5),
        "gla_gk_bias": nrm(ks[5], (DEPTH, GLA_QK), 0.1),
        "gla_norm_w": 1.0 + nrm(ks[6], (DEPTH, GLA_DV), 0.02),
        "w_branch_gla": nrm(ks[7], (DEPTH, GLA_V, D_MODEL), GLA_V ** -0.5),
        "ret_norm_w": 1.0 + nrm(ks[8], (DEPTH, RET_V), 0.02),
        "w_branch_ret": nrm(ks[9], (DEPTH, RET_V, D_MODEL), RET_V ** -0.5),
        "w_out": nrm(ks[10], (DEPTH, D_MODEL, D_MODEL), D_MODEL ** -0.5),
        "norm_ffn_w": 1.0 + nrm(ks[11], (DEPTH, D_MODEL), 0.02),
        "router_group_w": nrm(ks[12], (DEPTH, D_MODEL, N_GROUPS), D_MODEL ** -0.5),
        "router_group_b": nrm(ks[13], (DEPTH, N_GROUPS), 0.01),
        "router_expert_w": nrm(ks[14], (DEPTH, N_GROUPS, D_MODEL, EXPERTS_PER_GROUP), D_MODEL ** -0.5),
        "router_expert_b": nrm(ks[15], (DEPTH, N_GROUPS, EXPERTS_PER_GROUP), 0.01),
        "expert_w_gate": nrm(ks[16], (DEPTH, N_EXPERTS, D_MODEL, EXPERT_HIDDEN), D_MODEL ** -0.5),
        "expert_w_up": nrm(ks[17], (DEPTH, N_EXPERTS, D_MODEL, EXPERT_HIDDEN), D_MODEL ** -0.5),
        "expert_w_down": nrm(ks[18], (DEPTH, N_EXPERTS, EXPERT_HIDDEN, D_MODEL), EXPERT_HIDDEN ** -0.5),
        "norm_final_w": 1.0 + nrm(ks[19], (D_MODEL,), 0.02),
    }

def second_block(x, positions, norm_mix_w, w_in, gla_gk_up, gla_gk_bias, gla_norm_w, w_branch_gla,
              ret_norm_w, w_branch_ret, w_out, norm_ffn_w, router_group_w, router_group_b,
              router_expert_w, router_expert_b, expert_w_gate, expert_w_up, expert_w_down, norm_final_w):
    h = x
    for l in range(DEPTH):
        mix = _hybrid_mixer(_rmsnorm(h, norm_mix_w[l]), positions, w_in[l], gla_gk_up[l], gla_gk_bias[l],
                            gla_norm_w[l], w_branch_gla[l], ret_norm_w[l], w_branch_ret[l], w_out[l])
        h = h + mix.astype(h.dtype)
        ffn = _hierarchical_moe(_rmsnorm(h, norm_ffn_w[l]), router_group_w[l], router_group_b[l],
                                router_expert_w[l], router_expert_b[l], expert_w_gate[l],
                                expert_w_up[l], expert_w_down[l])
        h = h + ffn.astype(h.dtype)
    return _rmsnorm(h, norm_final_w)


def setup_inputs(seed=0):
    out = dict(first_inputs(seed))
    for name, value in second_inputs(seed + 1).items():
        if name != "x":
            out[name + "_2"] = value
    return out


def reference(
    x, c, w_ada, b_ada, norm1_w, w_in, hgrn_lb_logits, hgrn_gnorm_w, diff_lambda_q1,
    diff_lambda_k1, diff_lambda_q2, diff_lambda_k2, diff_subln_w, w_out, norm2_w, w_ffn_gate,
    w_ffn_up, w_ffn_down, final_norm_w, positions_2, norm_mix_w_2, w_in_2, gla_gk_up_2,
    gla_gk_bias_2, gla_norm_w_2, w_branch_gla_2, ret_norm_w_2, w_branch_ret_2, w_out_2,
    norm_ffn_w_2, router_group_w_2, router_group_b_2, router_expert_w_2, router_expert_b_2,
    expert_w_gate_2, expert_w_up_2, expert_w_down_2, norm_final_w_2,
):
    x = first_block(
        x, c, w_ada, b_ada, norm1_w, w_in, hgrn_lb_logits, hgrn_gnorm_w, diff_lambda_q1,
        diff_lambda_k1, diff_lambda_q2, diff_lambda_k2, diff_subln_w, w_out, norm2_w,
        w_ffn_gate, w_ffn_up, w_ffn_down, final_norm_w,
    )
    return second_block(
        x, positions_2, norm_mix_w_2, w_in_2, gla_gk_up_2, gla_gk_bias_2, gla_norm_w_2,
        w_branch_gla_2, ret_norm_w_2, w_branch_ret_2, w_out_2, norm_ffn_w_2, router_group_w_2,
        router_group_b_2, router_expert_w_2, router_expert_b_2, expert_w_gate_2, expert_w_up_2,
        expert_w_down_2, norm_final_w_2,
    )


_drawn_inputs = setup_inputs


def setup_inputs(seed=0):
    import zlib

    import numpy as np

    out = dict(_drawn_inputs(seed))
    spreads = {}
    factors = {'hgrn_gnorm_w': 3.169,
     'diff_lambda_k1': 5.668,
     'diff_lambda_q2': 5.68,
     'diff_subln_w': 7.13,
     'norm2_w': 5.772,
     'gla_norm_w_2': 11.398,
     'ret_norm_w_2': 11.847,
     'router_group_b_2': 9.086,
     'norm_ffn_w_2': 3.438,
     'router_expert_b_2': 8.0}
    for name, (base, spread) in spreads.items():
        noise = np.random.default_rng([zlib.crc32(name.encode()), seed]).standard_normal(out[name].shape)
        drawn = base * np.exp(spread * noise) if base else spread * noise
        out[name] = __import__('jax').numpy.asarray(drawn.astype(out[name].dtype))
    for name, factor in factors.items():
        out[name] = (out[name] * factor).astype(out[name].dtype)
    return out
```

```python
import numpy as np
from contextlib import ExitStack

import concourse.bass as bass
from concourse import mybir
from concourse.alu_op_type import AluOpType as ALU

F32 = mybir.dt.float32
I32 = mybir.dt.int32
U32 = mybir.dt.uint32
ACT = mybir.ActivationFunctionType
AXX = mybir.AxisListType.X

P = 128
T = 256
TT = T // P
D = 1024
KC = D // P
EPS = 1e-6
HEADS = 4
CH = 64
LEVELS = [1, 2, 4, 8, 16, 32, 64, 128]
FF = 2816
FFC = FF // P
NE, NGRP, EPG, HID = 32, 4, 8, 512
CAP = 64
NPAIR = NE // 2
NSLOT = NE * CAP
RING = 5
ARENA = 23824
LAMBDA_INIT = 0.2
ROWS = dict(b_ada=0, norm1=48, norm2=56, mixn=64, ffnn=72, fin1=80, lb0=88, lb1=92, gn=96,
            subln=97, gkb=98, glan=102, retn=104, c=120)


class Queue:

    def __init__(self, name, sem):
        self.name, self.sem, self.count, self.items = name, sem, 0, []

    def do(self, fn, *after):
        self.count += 1
        self.items.append((after, fn, (self.sem, 1)))
        return (self.sem, self.count)

    def quiet(self, fn, *after):
        self.items.append((after, fn, None))

    def last(self):
        return (self.sem, self.count)

    def emit(self, eng):
        met = {}

        def wait(after):
            for a in after:
                if a is None:
                    continue
                if len(a) == 2 and isinstance(a[1], int):
                    if a[1] > met.get(a[0].num, 0):
                        eng.wait_ge(a[0], a[1])
                        met[a[0].num] = a[1]
                else:
                    wait(a)

        for after, fn, inc in self.items:
            wait(after)
            ins = fn(eng)
            if inc:
                ins.then_inc(inc[0], inc[1])


def build(nc, a, out):
    ctx = ExitStack()
    with ctx:
        arena = [None]

        class Region:

            def __init__(self, start=0):
                self.at = start

            def close(self):
                pass

        def sb(name, shape, dt=F32, stack=None):
            if stack is None:
                return ctx.enter_context(nc.sbuf_tensor(name, shape, dt))
            n = int(np.prod(shape[1:]))
            v = arena[0][0:shape[0], stack.at:stack.at + n]
            stack.at += n
            assert stack.at <= ARENA, (name, stack.at)
            if dt != F32:
                v = v.bitcast(dt)
            if len(shape) == 3:
                v = v.rearrange("p (a b) -> p a b", a=shape[1])
            elif len(shape) == 4:
                v = v.rearrange("p (a b c) -> p a b c", a=shape[1], b=shape[2])
            return v

        def sem(name):
            return ctx.enter_context(nc.semaphore(name))

        PE, AC, VE, PO, SP = (Queue(n, sem("s_" + n)) for n in ("pe", "act", "dve", "pool", "sp"))

        def load(q, name, dst, src, *after):
            s = sem("d_" + name)
            q.items.append((after, lambda e: e.dma_start(dst, src), (s, 16)))
            return (s, 16)

        def fence():
            return [PE.last(), AC.last(), VE.last(), PO.last()]

        arena[0] = ctx.enter_context(nc.sbuf_tensor("arena", [P, ARENA], F32))
        ring = [sb(f"weights{i}", [P, KC * 512]) for i in range(RING)]
        ring_sem = [sem(f"s_weights{i}") for i in range(RING)]
        ring_free = [None] * RING
        ring_n = [0]
        ident = sb("ident", [P, P])
        ones = sb("ones", [P, P])
        pcol = sb("pcol", [P, P])
        hT = sb("hT", [P, KC, T])
        uT = sb("uT", [P, KC, T])
        small = sb("small", [P, 64])
        rstd = sb("rstd", [P, T])
        epsc = sb("epsc", [P, 1])
        banks = [ctx.enter_context(nc.psum_tensor(f"bank{i}", [P, 512], F32)) for i in range(8)]
        bank_free = [None] * 8
        gemm_n, side_n = [0], [0]

        def take(kind):
            n = gemm_n if kind == "gemm" else side_n
            i = n[0] % 4 + (0 if kind == "gemm" else 4)
            n[0] += 1
            return i, bank_free[i]

        def stream(src, kc=KC, cols=512):
            i = ring_n[0] % RING
            use = ring_n[0] // RING
            ring_n[0] += 1
            dst = ring[i][:, 0:kc * cols].rearrange("p (k n) -> p k n", k=kc)
            s = src.rearrange("(k p) n -> p k n", p=P)
            SP.items.append(([ring_free[i]], lambda e: e.dma_start(dst, s), (ring_sem[i], 16)))
            return i, dst, (ring_sem[i], 16 * (use + 1))

        early = Region()
        prow = sb("prow", [P, P], stack=early)
        xtok = sb("xtok", [P, TT, D], stack=early)
        t_id = load(AC, "ident", ident[:, :], a["ident"])
        t_x = load(AC, "x", xtok[:, :, :], a["x"][0].rearrange("(i p) d -> p i d", p=P))
        t_rows = []
        for name, src, n in [("b_ada", a["b_ada"], 48), ("norm1", a["norm1_w"], 8), ("norm2", a["norm2_w"], 8),
                             ("mixn", a["norm_mix_w_2"], 8), ("ffnn", a["norm_ffn_w_2"], 8),
                             ("fin1", a["final_norm_w"].rearrange("(o n) -> o n", o=1), 8),
                             ("lb0", a["hgrn_lb_logits"][0:1], 4), ("lb1", a["hgrn_lb_logits"][1:2], 4),
                             ("gn", a["hgrn_gnorm_w"], 1), ("subln", a["diff_subln_w"], 1),
                             ("gkb", a["gla_gk_bias_2"], 4), ("glan", a["gla_norm_w_2"], 2),
                             ("retn", a["ret_norm_w_2"], 16), ("c", a["c"], 8)]:
            r = ROWS[name]
            t_rows.append(load(AC if r < 90 else PO, "row_" + name, prow[r:r + n, :],
                               src.rearrange("o (r p) -> (o r) p", p=P)))
        t_ones = VE.do(lambda e: e.memset(ones[:, :], 1.0))
        t_eps = VE.do(lambda e: e.memset(epsc[:, :], EPS))
        bi, bf = take("side")
        t = PE.do(lambda e: e.transpose(banks[bi][:, 0:P], prow[:, :], ident[:, :]), t_rows, t_id)
        t_pcol = VE.do(lambda e: e.tensor_copy(pcol[:, :], banks[bi][:, 0:P]), t)
        bank_free[bi] = t_pcol

        def col(name, k=0):
            r = ROWS[name] + k
            return pcol[:, r:r + 1]

        cT = small[:, 0:8]
        t_cT = AC.do(lambda e: e.activation(cT, pcol[:, ROWS["c"]:ROWS["c"] + 8], ACT.Silu), t_pcol)

        def to_features(src, dst, *after):
            t = None
            for k in range(KC):
                i, fr = take("side")
                for j in range(TT):
                    f = lambda e, i=i, j=j, k=k: e.transpose(banks[i][:, j * P:(j + 1) * P],
                                                             src[:, j, k * P:(k + 1) * P], ident[:, :])
                    t = (PE.do if j == TT - 1 else PE.quiet)(f, after, fr)
                q = VE if k % 2 else AC
                g = ((lambda e, i=i, k=k: e.tensor_copy(dst[:, k, :], banks[i][:, 0:T])) if k % 2 else
                     (lambda e, i=i, k=k: e.activation(dst[:, k, :], banks[i][:, 0:T], ACT.Copy)))
                t = q.do(g, t)
                bank_free[i] = t
            return [AC.last(), VE.last()]

        def to_tokens(src, dst, *after):
            for j in range(TT):
                for k0 in range(0, KC, 4):
                    i, fr = take("side")
                    for k in range(4):
                        f = lambda e, i=i, j=j, k=k, k0=k0: e.transpose(
                            banks[i][:, k * P:(k + 1) * P], src[:, k0 + k, j * P:(j + 1) * P], ident[:, :])
                        t = (PE.do if k == 3 else PE.quiet)(f, after, fr)
                    t = AC.do(lambda e, i=i, j=j, k0=k0: e.activation(
                        dst[:, j, k0 * P:(k0 + 4) * P], banks[i][:, :], ACT.Copy), t)
                    bank_free[i] = t
            return t

        t_h = to_features(xtok, hT, t_x, t_id)

        def rms_scale(src, sq, n, *after):
            t = AC.do(lambda e: e.activation(sq[:, 0:n, :], src[:, 0:n, :], ACT.Square), after)
            i, fr = take("side")
            for k in range(n):
                f = lambda e, k=k: e.matmul(banks[i][:, 0:T], ones[:, :], sq[:, k, :], start=k == 0, stop=k == n - 1)
                t = (PE.do if k == n - 1 else PE.quiet)(f, t, fr, t_ones)
            t = AC.do(lambda e: e.activation(rstd[:, :], banks[i][:, 0:T], ACT.Sqrt, bias=epsc[:, 0:1],
                                             scale=1.0 / (n * P)), t, t_eps, VE.last())
            bank_free[i] = t
            return VE.do(lambda e: e.reciprocal(rstd[:, :], rstd[:, :]), t)

        def norm(src, dst, weight, shift, *after):
            t = rms_scale(src, dst, KC, after, fence())
            for k in range(KC):
                t2 = VE.do(lambda e, k=k: e.scalar_tensor_tensor(
                    out=dst[:, k, :], in0=src[:, k, :], scalar=weight(k), in1=rstd[:, :],
                    op0=ALU.mult, op1=ALU.mult), t)
                if shift:
                    t2 = AC.do(lambda e, k=k: e.activation(dst[:, k, :], dst[:, k, :], ACT.Identity,
                                                           bias=shift(k)), t2)
            return t2

        def project_T(src, xT, evac, *after, kc=KC, cols=512, parts=1, part=0, hold=None, step=1):
            i, w, t_w = stream(src, kc, cols)
            nb = (cols + 255) // 256
            if part == 0:
                got = [take("gemm") for _ in range(nb)]
                if hold is not None:
                    hold.extend(got)
            else:
                got = hold
            for b in range(nb):
                bk, fr = got[b]
                nch = min(2, cols // P - 2 * b)
                for c in range(nch):
                    ch = 2 * b + c
                    for k in range(kc):
                        if step == 2:
                            lw = w[:, k, 256 * b + c:256 * b + 256:2]
                        else:
                            lw = w[:, k, ch * P:(ch + 1) * P]
                        st = (part == 0 and k == 0 and (c == 0 or parts == 1))
                        f = lambda e, bk=bk, c=c, k=k, lw=lw, st=st: e.matmul(
                            banks[bk][:, c * T:(c + 1) * T], lw, xT(k), start=st,
                            stop=(part == parts - 1 and k == kc - 1), skip_group_check=parts > 1)
                        lastmm = k == kc - 1 and c == nch - 1
                        t = (PE.do if lastmm else PE.quiet)(f, t_w, fr if part == 0 else None, after)
                if part == parts - 1:
                    bank_free[bk] = evac(bk, 2 * b, nch, t)
            ring_free[i] = t

        def project_tok(src, xT, evac, *after, cols=512):
            i, w, t_w = stream(src, KC, cols)
            for j in range(TT):
                bk, fr = take("gemm")
                for k in range(KC):
                    f = lambda e, bk=bk, j=j, k=k: e.matmul(banks[bk][:, 0:cols], xT(k)[:, j * P:(j + 1) * P],
                                                            w[:, k, :], start=k == 0, stop=k == KC - 1)
                    t = (PE.do if k == KC - 1 else PE.quiet)(f, t_w, fr, after)
                bank_free[bk] = evac(bk, j, t)
            ring_free[i] = t

        def copy_T(dst, base=0, scale=1.0, func=ACT.Copy, wait=None):
            def evac(bk, ch, n, t):
                o = dst[:, base + ch:base + ch + n, :]
                return AC.do(lambda e: e.activation(o, banks[bk][:, 0:n * T].rearrange("p (c t) -> p c t", c=n),
                                                    func, scale=scale), t, wait)
            return evac

        def copy_tok(dst, c0, wait=None):
            def evac(bk, j, t):
                return VE.do(lambda e: e.tensor_copy(dst[:, j, c0:c0 + 512], banks[bk][:, :]), t, wait)
            return evac

        uX = lambda k: uT[:, k, :]

        modc = sb("modc", [P, 48])
        rowbuf = sb("rowbuf", [P, 512])
        modrow = sb("modrow", [16, P])
        state = {"modrow": None}

        def modulation(g):
            blocks = [stream(a["w_ada"][0][:, (4 * g + j) * 512:(4 * g + j + 1) * 512]) for j in range(4)]
            bk, fr = take("gemm")
            for k in range(KC):
                for j in range(4):
                    f = lambda e, j=j, k=k: e.matmul(banks[bk][32 * j:32 * j + 1, :], cT[:, k:k + 1],
                                                     blocks[j][1][:, k, :], start=k == 0, stop=k == KC - 1)
                    t = (PE.do if (k == KC - 1) else PE.quiet)(f, blocks[j][2], fr, t_cT)
                    ring_free[blocks[j][0]] = t
            for j in range(4):
                t2 = VE.do(lambda e, j=j: e.tensor_copy(rowbuf[32 * j:32 * j + 1, :], banks[bk][32 * j:32 * j + 1, :]),
                           t, state["modrow"])
            bank_free[bk] = t2
            ts = [load(PO, f"mod{g}_{j}", modrow[4 * j:4 * j + 4, :],
                       rowbuf[32 * j:32 * j + 1, :].rearrange("o (r p) -> o r p", p=P), t2, state["modrow"])
                  for j in range(4)]
            i, fr = take("side")
            t = PE.do(lambda e: e.transpose(banks[i][:, 0:16], modrow[:, :], ident[0:16, 0:16]), ts, fr)
            state["modrow"] = [t] + ts
            t = VE.do(lambda e: e.tensor_tensor(modc[:, 16 * g:16 * g + 16], banks[i][:, 0:16],
                                                pcol[:, 16 * g:16 * g + 16], ALU.add), t)
            bank_free[i] = t
            return t

        scl = sb("scl", [P, 16])
        t_mod0 = modulation(0)
        t_scl1 = VE.do(lambda e: e.scalar_tensor_tensor(
            out=scl[:, 0:8], in0=modc[:, 8:16], scalar=1.0, in1=pcol[:, ROWS["norm1"]:ROWS["norm1"] + 8],
            op0=ALU.add, op1=ALU.mult), t_mod0)

        lbc = small[:, 8:12]
        oml = small[:, 12:16]
        l0 = pcol[:, ROWS["lb0"]:ROWS["lb0"] + 4]
        l1 = pcol[:, ROWS["lb1"]:ROWS["lb1"] + 4]
        mx, e0, e1 = small[:, 16:20], small[:, 20:24], small[:, 24:28]
        t = VE.do(lambda e: e.tensor_tensor(mx, l0, l1, ALU.max), t_pcol)
        VE.do(lambda e: e.tensor_tensor(e0, l0, mx, ALU.subtract), t)
        t = VE.do(lambda e: e.tensor_tensor(e1, l1, mx, ALU.subtract), t)
        t = AC.do(lambda e: e.activation(small[:, 20:28], small[:, 20:28], ACT.Exp), t)
        t = VE.do(lambda e: e.tensor_tensor(mx, e0, e1, ALU.add), t)
        t = VE.do(lambda e: e.reciprocal(mx, mx), t)
        VE.do(lambda e: e.tensor_tensor(lbc, e0, mx, ALU.mult), t)
        t_lb = VE.do(lambda e: e.tensor_tensor(oml, e1, mx, ALU.mult), t)

        lamrow = sb("lamrow", [1, 4, 64])
        lams = sb("lams", [1, 8])
        t_l = [load(PO, "lam" + n, lamrow[:, i, :], a["diff_lambda_" + n]) for i, n in enumerate(["q1", "k1", "q2", "k2"])]
        t = VE.do(lambda e: e.tensor_tensor(lamrow[:, 0::2, :], lamrow[:, 0::2, :], lamrow[:, 1::2, :], ALU.mult), t_l)
        t = VE.do(lambda e: e.tensor_reduce(lams[:, 0:2], lamrow[:, 0::2, :], AXX, ALU.add), t)
        t = AC.do(lambda e: e.activation(lams[:, 2:4], lams[:, 0:2], ACT.Exp), t)
        t = VE.do(lambda e: e.tensor_tensor(lams[:, 4:5], lams[:, 3:4], lams[:, 2:3], ALU.subtract), t)
        t = VE.do(lambda e: e.tensor_scalar(lams[:, 5:6], lams[:, 4:5], -LAMBDA_INIT, None, ALU.add), t)
        i_l, fr = take("side")
        t = PE.do(lambda e: e.matmul(banks[i_l][:, 0:1], ones[0:1, :], lams[0:1, 5:6], start=True, stop=True),
                  t, t_ones, fr)
        neglam = small[:, 28:29]
        t_lam = VE.do(lambda e: e.tensor_copy(neglam, banks[i_l][:, 0:1]), t)
        bank_free[i_l] = t_lam

        chainm = sb("chainm", [P, HEADS * T])
        t = PO.do(lambda e: e.memset(chainm[:, :], 1.0))
        t_chain = PO.do(lambda e: e.memset(chainm[:, 0:HEADS * T:CH], 0.0), t)
        masks = sb("masks", [P, len(LEVELS), P], U32)
        t_masks = load(PO, "masks", masks[:, :, :], a["masks"].bitcast(U32))

        t_u = norm(hT, uT, lambda k: scl[:, k:k + 1], lambda k: modc[:, k:k + 1], t_h, t_scl1, t_mod0)
        f0 = fence()

        def gated(name, stack, q, k, v, b, dv, escale, oT, ready, ztok):
            lev = [[sb(f"{name}_{x}{i}", [P, HEADS, T], stack=stack) for x in ("e", "q", "k")] for i in range(2)]
            A0 = sb(name + "_A0", [P, HEADS, T], stack=stack)
            A1 = sb(name + "_A1", [P, HEADS, P], stack=stack)
            bl = sb(name + "_bl", [P, HEADS, 1], stack=stack)
            NV = dv // P
            tz = PO.do(lambda e: e.memset(A0[:, :, 0:P], 0.0), ztok)
            tz = PO.do(lambda e: e.memset(A1[:, :, :], 0.0), tz)
            for i in range(2):
                PO.do(lambda e, i=i: e.memset(lev[i][1][:, :, :], 0.0), ztok)
                tz = PO.do(lambda e, i=i: e.memset(lev[i][2][:, :, :], 0.0), ztok)
            free = [tz, tz]
            for li, m in enumerate(LEVELS + [256]):
                E, Q, K = lev[li % 2]
                if m == 1:
                    Qs, Ks, tq = q, k, [ready]
                else:
                    g = HEADS * T // m
                    vw = lambda x: x[:, :, :].rearrange("p h (g m) -> p (h g) m", m=m)
                    B, Ev, Qv, Kv = vw(b), vw(E), vw(Q), vw(K)
                    qq, kk = vw(q), vw(k)
                    half = m // 2
                    fr = free[li % 2]
                    if m <= CH:
                        ref = B[:, :, half - 1:half].broadcast_to([P, g, half])
                        VE.do(lambda e, B=B, Ev=Ev, ref=ref, half=half: e.tensor_tensor(
                            Ev[:, :, half:], B[:, :, half:], ref, ALU.subtract), ready, fr)
                        t = VE.do(lambda e, B=B, Ev=Ev, ref=ref, half=half: e.tensor_tensor(
                            Ev[:, :, 0:half], ref, B[:, :, 0:half], ALU.subtract), ready, fr)
                    elif m == 128:
                        ref = B[:, :, half - 1:half].broadcast_to([P, g, half])
                        VE.do(lambda e, B=B, Ev=Ev: e.tensor_copy(Ev[:, :, 64:], B[:, :, 64:]), ready, fr)
                        t = VE.do(lambda e, B=B, Ev=Ev, ref=ref: e.tensor_tensor(
                            Ev[:, :, 0:64], ref, B[:, :, 0:64], ALU.subtract), ready, fr)
                    else:
                        t0 = VE.do(lambda e: e.tensor_tensor(bl[:, :, :], b[:, :, 63:64], b[:, :, 127:128], ALU.add),
                                   ready, fr)
                        VE.do(lambda e, E=E: e.tensor_copy(E[:, :, 128:192], b[:, :, 128:192]), ready, fr)
                        VE.do(lambda e, E=E: e.tensor_tensor(
                            E[:, :, 192:256], b[:, :, 192:256], b[:, :, 191:192].broadcast_to([P, HEADS, 64]),
                            ALU.add), ready, fr)
                        VE.do(lambda e, E=E: e.tensor_tensor(
                            E[:, :, 64:128], b[:, :, 127:128].broadcast_to([P, HEADS, 64]), b[:, :, 64:128],
                            ALU.subtract), ready, fr)
                        t = VE.do(lambda e, E=E: e.tensor_tensor(
                            E[:, :, 0:64], bl[:, :, :].broadcast_to([P, HEADS, 64]), b[:, :, 0:64],
                            ALU.subtract), t0, fr)
                    t = AC.do(lambda e, E=E: e.activation(E[:, :, :], E[:, :, :], ACT.Exp, scale=escale), t)
                    tk = PO.do(lambda e, Kv=Kv, kk=kk, Ev=Ev, half=half: e.tensor_tensor(
                        Kv[:, :, 0:half], kk[:, :, 0:half], Ev[:, :, 0:half], ALU.mult), t, fr, ready)
                    tq = VE.do(lambda e, Qv=Qv, qq=qq, Ev=Ev, half=half: e.tensor_tensor(
                        Qv[:, :, half:], qq[:, :, half:], Ev[:, :, half:], ALU.mult), t, fr, ready)
                    Qs, Ks, tq = Q, K, [tk, tq]
                tiles = [(0, 0), (1, 1)] if m <= P else [(0, 1)]
                done = []
                for si, ti in tiles:
                    i, fr = take("side")
                    for h in range(HEADS):
                        f = lambda e, i=i, h=h, si=si, ti=ti, Qs=Qs, Ks=Ks: e.matmul(
                            banks[i][:, h * P:(h + 1) * P], Ks[:, h, si * P:(si + 1) * P],
                            Qs[:, h, ti * P:(ti + 1) * P], start=True, stop=True)
                        t = (PE.do if h == HEADS - 1 else PE.quiet)(f, tq, fr)
                    ps = banks[i][:, :].rearrange("p (h t) -> p h t", h=HEADS)
                    if m > P:
                        t2 = VE.do(lambda e, ps=ps: e.tensor_copy(A0[:, :, P:T], ps), t, ztok)
                    else:
                        dst = A0[:, :, 0:P] if si == 0 else A1[:, :, :]
                        mk = masks[:, li:li + 1, :].broadcast_to([P, HEADS, P])
                        t2 = VE.do(lambda e, dst=dst, mk=mk, ps=ps: e.copy_predicated(dst, mk, ps), t, tz, t_masks,
                                   VE.last())
                    bank_free[i] = t2
                    done.append(t)
                if m > 1:
                    free[li % 2] = done[-1]
                yield
            tA = VE.last()
            for h in range(HEADS):
                for c0 in range(0, NV, 2):
                    n = min(2, NV - c0)
                    i, fr = take("side")
                    for c in range(n):
                        vs = lambda j, h=h, c=c, c0=c0: v[:, j, h * dv + (c0 + c) * P:h * dv + (c0 + c + 1) * P]
                        PE.quiet(lambda e, i=i, c=c, h=h, vs=vs: e.matmul(
                            banks[i][:, c * T:(c + 1) * T], vs(0), A0[:, h, :], start=True, stop=False,
                            skip_group_check=True), tA, fr)
                        t = PE.do(lambda e, i=i, c=c, h=h, vs=vs: e.matmul(
                            banks[i][:, c * T + P:(c + 1) * T], vs(1), A1[:, h, :], start=False, stop=True,
                            skip_group_check=True), tA, fr)
                    o = oT[:, h * NV + c0:h * NV + c0 + n, :]
                    t = AC.do(lambda e, i=i, o=o, n=n: e.activation(
                        o, banks[i][:, 0:n * T].rearrange("p (c t) -> p c t", c=n), ACT.Copy), t, ztok)
                    bank_free[i] = t
            yield
            sq = lev[0][0] if NV == 1 else None
            rs = lev[1][0]
            tr = []
            for h in range(HEADS):
                i, fr = take("side")
                sqh = lev[0][0][:, 0:NV, :]
                t1 = AC.do(lambda e, h=h, sqh=sqh: e.activation(sqh, oT[:, h * NV:(h + 1) * NV, :], ACT.Square),
                           AC.last(), PE.last())
                for c in range(NV):
                    f = lambda e, i=i, c=c: e.matmul(banks[i][:, 0:T], ones[:, :], lev[0][0][:, c, :],
                                                     start=c == 0, stop=c == NV - 1)
                    t = (PE.do if c == NV - 1 else PE.quiet)(f, t1, fr)
                t = AC.do(lambda e, i=i, h=h: e.activation(rs[:, h, :], banks[i][:, 0:T], ACT.Sqrt,
                                                           bias=epsc[:, 0:1], scale=1.0 / dv), t)
                bank_free[i] = t
            t = VE.do(lambda e: e.reciprocal(rs[:, :, :], rs[:, :, :]), t)
            yield (rs, t)

        def run(gen):
            r = None
            for x in gen:
                r = x if x is not None else r
            return r

        def interleave(main, *gens):
            res = []
            live = list(gens)
            for step in main:
                step()
                if live:
                    try:
                        x = next(live[0])
                        if x is not None:
                            res.append(x)
                    except StopIteration:
                        live.pop(0)
            for g in live:
                for x in g:
                    if x is not None:
                        res.append(x)
            return res

        early.close()
        b1 = Region()
        hq = sb("hq", [P, HEADS, T], stack=b1)
        hk = sb("hk", [P, HEADS, T], stack=b1)
        hb = sb("hb", [P, HEADS, T], stack=b1)
        hv = sb("hv", [P, TT, 512], stack=b1)
        hg = sb("hg", [P, HEADS, T], stack=b1)
        hf = sb("hf", [P, HEADS, T], stack=b1)
        aq = sb("aq", [P, HEADS, T], stack=b1)
        ak = sb("ak", [P, HEADS, T], stack=b1)
        av = sb("av", [P, TT, 512], stack=b1)
        mixT = sb("mixT", [P, KC, T], stack=b1)
        distc = sb("distc", [P, 384], stack=b1)
        t_dist = load(PO, "dist", distc[:, :], a["dist"], f0)
        win = lambda i: a["w_in"][0][:, i * 512:(i + 1) * 512]
        project_T(win(1), uX, copy_T(hf, func=ACT.Sigmoid, wait=f0), t_u)
        t = AC.last()
        for h in range(HEADS):
            t2 = VE.do(lambda e, h=h: e.tensor_scalar(hf[:, h, :], hf[:, h, :], oml[:, h:h + 1], lbc[:, h:h + 1],
                                                      ALU.mult, ALU.add), t, t_lb)
        t2 = VE.do(lambda e: e.tensor_scalar(hf[:, :, :], hf[:, :, :], 1e-18, None, ALU.max), t2)
        VE.do(lambda e: e.tensor_scalar(hk[:, :, :], hf[:, :, :], -1.0, 1.0, ALU.mult, ALU.add), t2, f0)
        t = AC.do(lambda e: e.activation(hf[:, :, :], hf[:, :, :], ACT.Ln), VE.last())
        t_hb = VE.do(lambda e: e.tensor_tensor_scan(
            hb[:, :, :].rearrange("p h t -> p (h t)"), chainm[:, :], hf[:, :, :].rearrange("p h t -> p (h t)"),
            0.0, ALU.mult, ALU.add), t, t_chain, f0)
        project_T(win(0), uX, copy_T(hq, wait=f0), t_u)
        t_hready = [t_hb, AC.last()]
        project_tok(win(2), uX, copy_tok(hv, 0, f0), t_u)
        t_hv = VE.last()
        hst = Region(b1.at)
        gen_h = gated("hg", hst, hq, hk, hv, hb, P, 1.0, mixT, t_hready, f0)

        def diff_attention():
            S = [[sb(f"S{i}{m}", [P, 384], stack=hst) for m in range(2)] for i in range(2)]
            W = [sb(f"W{i}", [P, 384], stack=hst) for i in range(2)]
            WT = [sb(f"WT{i}", [P, 384], stack=hst) for i in range(2)]
            st = sb("dstat", [P, HEADS, 12], stack=hst)
            t_in = [AC.last(), VE.last()]
            span = [(0, P), (P, 384)]
            sfree = [None, None]
            for h in range(HEADS):
                slope = 2.0 ** (-8.0 * (h + 1) / HEADS)
                Sh, Wh, WTh = S[h % 2], W[h % 2], WT[h % 2]
                tb = []
                for m in range(2):
                    i, fr = take("side")
                    for j in range(TT):
                        a0, a1 = span[j]
                        f = lambda e, i=i, m=m, j=j, a0=a0, a1=a1, h=h: e.matmul(
                            banks[i][:, a0:a1], aq[64 * m:64 * m + 64, h, j * P:(j + 1) * P],
                            ak[64 * m:64 * m + 64, h, 0:a1 - a0], start=True, stop=True)
                        t = (PE.do if j == 1 else PE.quiet)(f, t_in, fr)
                    t = VE.do(lambda e, i=i, m=m, Sh=Sh, slope=slope: e.scalar_tensor_tensor(
                        out=Sh[m][:, :], in0=distc[:, :], scalar=-slope, in1=banks[i][:, 0:384],
                        op0=ALU.mult, op1=ALU.add), t, t_dist, sfree[h % 2])
                    bank_free[i] = t
                    for j in range(TT):
                        a0, a1 = span[j]
                        tr = VE.do(lambda e, m=m, j=j, a0=a0, a1=a1, h=h, Sh=Sh: e.tensor_reduce(
                            st[:, h, 2 * m + j:2 * m + j + 1], Sh[m][:, a0:a1], AXX, ALU.max), t)
                t = VE.do(lambda e, h=h: e.tensor_scalar(st[:, h, 0:4], st[:, h, 0:4], -1.0, None, ALU.mult), tr)
                for m in range(2):
                    for j in range(TT):
                        a0, a1 = span[j]
                        c = 2 * m + j
                        te = AC.do(lambda e, m=m, c=c, a0=a0, a1=a1, h=h, Sh=Sh: e.activation(
                            Sh[m][:, a0:a1], Sh[m][:, a0:a1], ACT.Exp, bias=st[:, h, c:c + 1],
                            accum_out=st[:, h, 4 + c:5 + c]), t)
                t = VE.do(lambda e, h=h: e.reciprocal(st[:, h, 8:12], st[:, h, 4:8]), te)
                t = VE.do(lambda e, h=h: e.tensor_scalar(st[:, h, 10:12], st[:, h, 10:12], neglam, None, ALU.mult),
                          t, t_lam)
                for j in range(TT):
                    a0, a1 = span[j]
                    t1 = VE.do(lambda e, j=j, a0=a0, a1=a1, h=h, Sh=Sh, Wh=Wh: e.tensor_scalar(
                        Wh[:, a0:a1], Sh[0][:, a0:a1], st[:, h, 8 + j:9 + j], None, ALU.mult), t, sfree[h % 2])
                    t1 = VE.do(lambda e, j=j, a0=a0, a1=a1, h=h, Sh=Sh, Wh=Wh: e.scalar_tensor_tensor(
                        out=Wh[:, a0:a1], in0=Sh[1][:, a0:a1], scalar=st[:, h, 10 + j:11 + j], in1=Wh[:, a0:a1],
                        op0=ALU.mult, op1=ALU.add), t1)
                yield
                i, fr = take("side")
                for c in range(3):
                    f = lambda e, i=i, c=c, Wh=Wh: e.transpose(banks[i][:, c * P:(c + 1) * P],
                                                               Wh[:, c * P:(c + 1) * P], ident[:, :])
                    t = (PE.do if c == 2 else PE.quiet)(f, t1, fr)
                t = AC.do(lambda e, i=i, WTh=WTh: e.activation(WTh[:, :], banks[i][:, 0:384], ACT.Copy), t,
                          sfree[h % 2])
                bank_free[i] = t
                yield
                i, fr = take("side")
                PE.quiet(lambda e, i=i, h=h, WTh=WTh: e.matmul(
                    banks[i][:, 0:T], av[:, 0, h * P:(h + 1) * P], WTh[:, 0:T], start=True, stop=False,
                    skip_group_check=True), t, fr)
                t = PE.do(lambda e, i=i, h=h, WTh=WTh: e.matmul(
                    banks[i][:, P:T], av[:, 1, h * P:(h + 1) * P], WTh[:, T:384], start=False, stop=True,
                    skip_group_check=True), t, fr)
                sfree[h % 2] = t
                t = AC.do(lambda e, i=i, h=h: e.activation(mixT[:, 4 + h, :], banks[i][:, 0:T], ACT.Copy), t, f0)
                bank_free[i] = t
            yield
            t = AC.do(lambda e: e.activation(aq[:, :, :], mixT[:, 4:8, :], ACT.Square), t, PE.last())
            for h in range(HEADS):
                i, fr = take("side")
                t1 = PE.do(lambda e, i=i, h=h: e.matmul(banks[i][:, 0:T], ones[:, :], aq[:, h, :],
                                                        start=True, stop=True), t, fr)
                t1 = AC.do(lambda e, i=i, h=h: e.activation(ak[:, h, :], banks[i][:, 0:T], ACT.Sqrt,
                                                            bias=epsc[:, 0:1], scale=1.0 / P), t1)
                bank_free[i] = t1
            t1 = VE.do(lambda e: e.reciprocal(ak[:, :, :], ak[:, :, :]), t1)
            subs = small[:, 29:30]
            t2 = VE.do(lambda e: e.tensor_scalar(subs, col("subln"), 1.0 - LAMBDA_INIT, None, ALU.mult))
            t1 = VE.do(lambda e: e.scalar_tensor_tensor(
                out=mixT[:, 4:8, :], in0=mixT[:, 4:8, :], scalar=subs, in1=ak[:, :, :],
                op0=ALU.mult, op1=ALU.mult), t1, t2)
            yield

        res = interleave([
            lambda: project_T(win(3), uX, copy_T(hg, func=ACT.Silu, wait=f0), t_u),
            lambda: project_T(win(4), uX, copy_T(aq, scale=0.125, wait=f0), t_u),
            lambda: project_T(win(5), uX, copy_T(ak, wait=f0), t_u),
            lambda: project_tok(win(6), uX, copy_tok(av, 0, f0), t_u),
            lambda: modulation(1),
            lambda: modulation(2)], gen_h, diff_attention())
        rs, t = res[0]
        t = VE.do(lambda e, rs=rs: e.scalar_tensor_tensor(out=mixT[:, 0:4, :], in0=mixT[:, 0:4, :], scalar=col("gn"),
                                                   in1=rs[:, :, :], op0=ALU.mult, op1=ALU.mult), t)
        t = VE.do(lambda e: e.tensor_tensor(mixT[:, 0:4, :], mixT[:, 0:4, :], hg[:, :, :], ALU.mult), t)
        t_mod = VE.last()
        t_scl2 = VE.do(lambda e: e.scalar_tensor_tensor(
            out=scl[:, 8:16], in0=modc[:, 32:40], scalar=1.0, in1=pcol[:, ROWS["norm2"]:ROWS["norm2"] + 8],
            op0=ALU.add, op1=ALU.mult), t_mod)

        def residual(gate, base):
            def evac(bk, ch, n, t):
                for c in range(n):
                    k = base + ch + c
                    t2 = VE.do(lambda e, bk=bk, c=c, k=k: e.scalar_tensor_tensor(
                        out=hT[:, k, :], in0=banks[bk][:, c * T:(c + 1) * T], scalar=modc[:, gate + k:gate + k + 1],
                        in1=hT[:, k, :], op0=ALU.mult, op1=ALU.add), t, t_mod)
                return t2
            return evac

        mX = lambda k: mixT[:, k, :]
        for c in range(2):
            project_T(a["w_out"][0][:, c * 512:(c + 1) * 512], mX, residual(16, 4 * c), VE.last() if c == 0 else None)
        t_u = norm(hT, uT, lambda k: scl[:, 8 + k:9 + k], lambda k: modc[:, 24 + k:25 + k], VE.last())
        f1 = fence()
        hst.close()
        b1.close()

        b2 = Region()
        hid = sb("hid", [P, FFC, T], stack=b2)
        c0 = 0
        while c0 < FF:
            n = min(512, FF - c0)
            project_T(a["w_ffn_gate"][0][:, c0:c0 + n], uX, copy_T(hid, c0 // P, func=ACT.Silu, wait=f1), t_u, cols=n)
            t_g = AC.last()

            def evac_up(bk, ch, m, t, c0=c0, t_g=t_g):
                o = hid[:, c0 // P + ch:c0 // P + ch + m, :]
                return VE.do(lambda e: e.tensor_tensor(
                    o, banks[bk][:, 0:m * T].rearrange("p (c t) -> p c t", c=m), o, ALU.mult), t, t_g)
            project_T(a["w_ffn_up"][0][:, c0:c0 + n], uX, evac_up, t_u, cols=n)
            c0 += n
        t_hid = VE.last()
        for c in range(2):
            hold = []
            parts = [(0, 8), (8, 8), (16, 6)]
            for pi, (k0, kn) in enumerate(parts):
                project_T(a["w_ffn_down"][0][k0 * P:(k0 + kn) * P, c * 512:(c + 1) * 512],
                          lambda k, k0=k0: hid[:, k0 + k, :], residual(40, 4 * c), t_hid, kc=kn,
                          parts=3, part=pi, hold=hold)
        t = rms_scale(hT, uT, KC, VE.last(), PE.last())
        for k in range(KC):
            t_h = VE.do(lambda e, k=k: e.scalar_tensor_tensor(
                out=hT[:, k, :], in0=hT[:, k, :], scalar=col("fin1", k), in1=rstd[:, :],
                op0=ALU.mult, op1=ALU.mult), t)
        t_u = norm(hT, uT, lambda k: col("mixn", k), None, t_h)
        f2 = fence()
        b2.close()

        outer = Region()
        w2 = a["w_in_2"][0]
        rq = sb("rq", [P, 8, T], stack=outer)
        rk = sb("rk", [P, 8, T], stack=outer)
        rv = sb("rv", [P, TT, 2048], stack=outer)
        b3 = Region(outer.at)
        gq = sb("gq", [P, HEADS, T], stack=b3)
        gk = sb("gk", [P, HEADS, T], stack=b3)
        gb = sb("gb", [P, HEADS, T], stack=b3)
        gv = sb("gv", [P, TT, 1024], stack=b3)
        gd = sb("gd", [16, T], stack=b3)
        gup = sb("gup", [16, 512], stack=b3)
        oG = sb("oG", [P, 8, T], stack=b3)
        z = oG[:, 0:4, :]
        t_gup = load(PO, "gup", gup[:, :], a["gla_gk_up_2"][0], f2)

        i, w, t_w = stream(w2[:, 3072:3088], KC, 16)
        bk, fr = take("gemm")
        for k in range(KC):
            f = lambda e, k=k, w=w, bk=bk: e.matmul(banks[bk][0:16, 0:T], w[:, k, :], uT[:, k, :],
                                                    start=k == 0, stop=k == KC - 1)
            t = (PE.do if k == KC - 1 else PE.quiet)(f, t_w, fr, t_u)
        ring_free[i] = t
        t = AC.do(lambda e, bk=bk: e.activation(gd[:, :], banks[bk][0:16, 0:T], ACT.Copy), t, f2)
        bank_free[bk] = t
        t_gd = t
        project_T(w2[:, 0:512], uX, copy_T(gq, scale=float(P) ** -0.5, wait=f2), t_u)
        gbf = [None] * 2
        for hh in range(2):
            i, fr = take("side")
            for c in range(2):
                h = 2 * hh + c
                t = PE.do(lambda e, i=i, c=c, h=h: e.matmul(banks[i][:, c * T:(c + 1) * T],
                                                            gup[:, h * P:(h + 1) * P], gd[:, :], start=True,
                                                            stop=True), t_gd, t_gup, fr)
            for c in range(2):
                h = 2 * hh + c
                t2 = AC.do(lambda e, i=i, c=c, h=h: e.activation(z[:, h, :], banks[i][:, c * T:(c + 1) * T],
                                                                 ACT.Identity, bias=col("gkb", h)), t, f2)
            bank_free[i] = t2
        t = AC.do(lambda e: e.activation(gb[:, :, :], z[:, :, :], ACT.Abs), t2, f2)
        t = AC.do(lambda e: e.activation(gb[:, :, :], gb[:, :, :], ACT.Exp, scale=-1.0), t)
        t = AC.do(lambda e: e.activation(gb[:, :, :], gb[:, :, :], ACT.Ln, bias=ones[:, 0:1]), t)
        t = VE.do(lambda e: e.scalar_tensor_tensor(out=z[:, :, :], in0=z[:, :, :], scalar=0.0, in1=gb[:, :, :],
                                                   op0=ALU.min, op1=ALU.subtract), t)
        t_gb = VE.do(lambda e: e.tensor_tensor_scan(
            gb[:, :, :].rearrange("p h t -> p (h t)"), chainm[:, :], z[:, :, :].rearrange("p h t -> p (h t)"),
            0.0, ALU.mult, ALU.add), t)
        project_T(w2[:, 512:1024], uX, copy_T(gk, wait=f2), t_u)
        t_gready = [t_gb, AC.last()]
        for c in range(2):
            project_tok(w2[:, 1024 + c * 512:1536 + c * 512], uX, copy_tok(gv, c * 512, f2), t_u)
        gst = Region(b3.at)
        gen_g = gated("gl", gst, gq, gk, gv, gb, 256, 1.0 / 16.0, oG, t_gready, f2)
        RQ, RK, RV, RG, MA, MB = 3088, 4112, 5136, 7184, 9232, 10256
        mains = []
        for c in range(2):
            mains.append(lambda c=c: project_T(w2[:, RQ + c * 512:RQ + (c + 1) * 512], uX,
                                               copy_T(rq, 4 * c, wait=f2), t_u, step=2))
        for c in range(2):
            mains.append(lambda c=c: project_T(w2[:, RK + c * 512:RK + (c + 1) * 512], uX,
                                               copy_T(rk, 4 * c, scale=1.0 / 16.0, wait=f2), t_u, step=2))
        for c in range(4):
            mains.append(lambda c=c: project_tok(w2[:, RV + c * 512:RV + (c + 1) * 512], uX,
                                                 copy_tok(rv, c * 512, f2), t_u))
        GG = 2048
        res = interleave(mains, gen_g)
        rs, t = res[0]
        for c in range(2):
            t = VE.do(lambda e, c=c: e.scalar_tensor_tensor(
                out=oG[:, c::2, :], in0=oG[:, c::2, :], scalar=col("glan", c), in1=rs[:, :, :],
                op0=ALU.mult, op1=ALU.mult), t)

        def evac_gate(dst, base, t_in, tmp, func):
            def evac(bk, ch, n, t):
                j = (ch // 2) % 2
                t = AC.do(lambda e: e.activation(tmp[j], banks[bk][:, 0:n * T], func), t, tmpfree[j])
                o = dst[:, base + ch:base + ch + n, :]
                tmpfree[j] = VE.do(lambda e: e.tensor_tensor(o, o, tmp[j].rearrange("p (c t) -> p c t", c=n),
                                                             ALU.mult), t, t_in)
                return t
            return evac
        fg = fence()
        gst = Region(b3.at)
        merged = sb("merged", [P, KC, T], stack=Region(ARENA - KC * T))
        gtmp = [sb(f"gtmp{i}", [P, 512], stack=gst) for i in range(2)]
        tmpfree = [fg, fg]
        tm = [gtmp[0][:, :], gtmp[1][:, :]]
        for c in range(2):
            project_T(w2[:, GG + c * 512:GG + (c + 1) * 512], uX, evac_gate(oG, 4 * c, t, tm, ACT.Silu), t_u)
        t_oG = VE.last()
        gX = lambda k: oG[:, k, :]
        for c in range(2):
            project_T(w2[:, MA + c * 512:MA + (c + 1) * 512], uX, copy_T(merged, 4 * c, func=ACT.Sigmoid, wait=fg), t_u)
        t_mga = AC.last()

        def evac_ya(base):
            def evac(bk, ch, n, t):
                o = merged[:, base + ch:base + ch + n, :]
                return VE.do(lambda e: e.tensor_tensor(o, banks[bk][:, 0:n * T].rearrange("p (c t) -> p c t", c=n),
                                                       o, ALU.mult), t, t_mga)
            return evac
        for c in range(2):
            project_T(a["w_branch_gla_2"][0][:, c * 512:(c + 1) * 512], gX, evac_ya(4 * c), t_oG)
        f3 = fence()
        gst.close()
        b3.close()

        b4 = Region(outer.at)
        rtmp = [sb(f"rtmp{i}", [P, 512], stack=b4)[:, :] for i in range(2)]
        cosT = sb("cosT", [P, T], stack=b4)
        sinT = sb("sinT", [P, T], stack=b4)
        posi = sb("posi", [P, T], I32, stack=b4)
        ang = sb("ang", [P, T], stack=b4)
        rot = [sb(f"rot{i}", [P, HEADS, T], stack=b4) for i in range(2)]
        dec = sb("dec", [P, HEADS, 384], stack=b4)
        theta = sb("theta", [P, 1], stack=b4)
        oR = sb("oR", [P, 16, T], stack=b4)
        t_pos = load(PO, "pos", posi[:, :], a["positions_2"].partition_broadcast(P).rearrange("p o t -> p (o t)"), f3)
        t_th = load(PO, "theta", theta[:, :], a["theta"], f3)
        t_dec = load(PO, "dec", dec[:, :, :], a["decay"], f3)
        t = VE.do(lambda e: e.tensor_copy(ang[:, :], posi[:, :]), t_pos, f3)
        t = VE.do(lambda e: e.tensor_scalar(ang[:, :], ang[:, :], theta[:, 0:1], None, ALU.mult), t, t_th)
        t_ang = t
        MAGIC = 12582912.0
        for dst, shift in ((sinT, 0.0), (cosT, 0.25)):
            kt = rot[0][:, 0, :]
            t = VE.do(lambda e, kt=kt, shift=shift: e.tensor_scalar(
                kt, ang[:, :], float(1.0 / (2 * np.pi)), shift, ALU.mult, ALU.add), t_ang, t, f3)
            t = VE.do(lambda e, kt=kt: e.tensor_scalar(kt, kt, MAGIC, None, ALU.add), t)
            t = VE.do(lambda e, kt=kt: e.tensor_scalar(kt, kt, -MAGIC, None, ALU.add), t)
            src = ang
            for part in TWO_PI_PARTS:
                t = VE.do(lambda e, kt=kt, part=part, src=src, dst=dst: e.scalar_tensor_tensor(
                    out=dst[:, :], in0=kt, scalar=-part, in1=src[:, :], op0=ALU.mult, op1=ALU.add), t)
                src = dst
            t = VE.do(lambda e, dst=dst, shift=shift: e.tensor_scalar(
                dst[:, :], dst[:, :], float(2 * np.pi * shift), None, ALU.add), t)
            t = VE.do(lambda e, dst=dst: e.tensor_scalar(
                dst[:, :], dst[:, :], 3.1415925, -3.1415925, ALU.min, ALU.max), t)
            t = AC.do(lambda e, dst=dst: e.activation(dst[:, :], dst[:, :], ACT.Sin), t)
        t_cs = t
        cb = cosT[:, :].unsqueeze(1).broadcast_to([P, HEADS, T])
        sbb = sinT[:, :].unsqueeze(1).broadcast_to([P, HEADS, T])
        tr = None
        for x in (rq, rk):
            ev, od = x[:, 0::2, :], x[:, 1::2, :]
            t1 = VE.do(lambda e, ev=ev: e.tensor_tensor(rot[0][:, :, :], ev, sbb, ALU.mult), t_cs, VE.last())
            t2 = PO.do(lambda e, od=od: e.tensor_tensor(rot[1][:, :, :], od, sbb, ALU.mult), t_cs, tr, f3)
            t3 = VE.do(lambda e, ev=ev: e.tensor_tensor(ev, ev, cb, ALU.mult), t1, AC.last())
            t4 = VE.do(lambda e, od=od: e.tensor_tensor(od, od, cb, ALU.mult), t2)
            VE.do(lambda e, ev=ev: e.tensor_tensor(ev, ev, rot[1][:, :, :], ALU.subtract), t3, t2)
            tr = VE.do(lambda e, od=od: e.tensor_tensor(od, od, rot[0][:, :, :], ALU.add), t4, t1)
        t_rot = tr


        def retention():
            AT = [sb(f"ret_A{i}", [P, 384], stack=b4) for i in range(2)]
            mean = sb("ret_mean", [P, T], stack=b4)
            sq = rot[1]
            afree = [None, None]
            sqf = None
            for h in range(HEADS):
                i, fr = take("side")
                for c in range(2):
                    PE.quiet(lambda e, i=i, c=c, h=h: e.matmul(
                        banks[i][:, 0:T], rk[:, 2 * h + c, 0:P], rq[:, 2 * h + c, :], start=c == 0, stop=c == 1),
                        t_rot, fr)
                for c in range(2):
                    t = (PE.do if c else PE.quiet)(lambda e, i=i, c=c, h=h: e.matmul(
                        banks[i][:, T:384], rk[:, 2 * h + c, P:T], rq[:, 2 * h + c, P:T], start=c == 0, stop=c == 1))
                A = AT[h % 2]
                t = VE.do(lambda e, i=i, h=h, A=A: e.tensor_tensor(A[:, :], banks[i][:, 0:384], dec[:, h, :], ALU.mult),
                          t, t_dec, afree[h % 2])
                bank_free[i] = t
                yield
                for c0 in range(0, 4, 2):
                    i, fr = take("side")
                    for c in range(2):
                        vc = slice(h * 512 + (c0 + c) * P, h * 512 + (c0 + c + 1) * P)
                        PE.quiet(lambda e, i=i, c=c, vc=vc, A=A: e.matmul(
                            banks[i][:, c * T:(c + 1) * T], rv[:, 0, vc], A[:, 0:T], start=True, stop=False,
                            skip_group_check=True), t, fr)
                        t2 = PE.do(lambda e, i=i, c=c, vc=vc, A=A: e.matmul(
                            banks[i][:, c * T + P:(c + 1) * T], rv[:, 1, vc], A[:, T:384], start=False, stop=True,
                            skip_group_check=True))
                    t2 = AC.do(lambda e, i=i, c0=c0, h=h: e.activation(
                        oR[:, 4 * h + c0:4 * h + c0 + 2, :], banks[i][:, :].rearrange("p (c t) -> p c t", c=2),
                        ACT.Copy), t2, f3)
                    bank_free[i] = t2
                afree[h % 2] = PE.last()
                yield
                o = oR[:, 4 * h:4 * h + 4, :]
                i, fr = take("side")
                for c in range(4):
                    t = (PE.do if c == 3 else PE.quiet)(lambda e, i=i, c=c, h=h: e.matmul(
                        banks[i][:, 0:T], ones[:, :], oR[:, 4 * h + c, :], start=c == 0, stop=c == 3), t2, fr)
                t = AC.do(lambda e, i=i: e.activation(mean[:, :], banks[i][:, 0:T], ACT.Copy, scale=1.0 / 512), t,
                          VE.last())
                bank_free[i] = t
                t = VE.do(lambda e, o=o: e.tensor_tensor(
                    o, o, mean[:, :].unsqueeze(1).broadcast_to([P, 4, T]), ALU.subtract), t)
                t2 = AC.do(lambda e, o=o: e.activation(sq[:, :, :], o, ACT.Square), t, PE.last(), t_rot)
                i, fr = take("side")
                for c in range(4):
                    t = (PE.do if c == 3 else PE.quiet)(lambda e, i=i, c=c: e.matmul(
                        banks[i][:, 0:T], ones[:, :], sq[:, c, :], start=c == 0, stop=c == 3), t2, fr)
                yield
                t = AC.do(lambda e, i=i: e.activation(mean[:, :], banks[i][:, 0:T], ACT.Sqrt, bias=epsc[:, 0:1],
                                                      scale=1.0 / 512), t)
                bank_free[i] = t
                t = VE.do(lambda e: e.reciprocal(mean[:, :], mean[:, :]), t)
                for c in range(4):
                    t2 = VE.do(lambda e, c=c, h=h: e.scalar_tensor_tensor(
                        out=oR[:, 4 * h + c, :], in0=oR[:, 4 * h + c, :], scalar=col("retn", 4 * h + c),
                        in1=mean[:, :], op0=ALU.mult, op1=ALU.mult), t)
                rdone[h] = t2
                yield
        rdone = {}
        mgb = sb("mgb", [P, KC, T], stack=b4)
        interleave([lambda c=c: project_T(w2[:, MB + c * 512:MB + (c + 1) * 512], uX,
                                          copy_T(mgb, 4 * c, func=ACT.Sigmoid, wait=f3), t_u) for c in range(2)],
                   retention())
        tmpfree[:] = [f3, f3]
        for c in range(4):
            project_T(w2[:, RG + c * 512:RG + (c + 1) * 512], uX, evac_gate(oR, 4 * c, rdone[c], rtmp, ACT.Silu), t_u)
        t_oR = VE.last()
        t_mgb = AC.last()
        xtok2 = sb("xtok2", [P, TT, D], stack=Region())

        def evac_yb(base):
            def evac(bk, ch, n, t):
                o = merged[:, base + ch:base + ch + n, :]
                g = mgb[:, base + ch:base + ch + n, :]
                t = VE.do(lambda e: e.tensor_tensor(g, banks[bk][:, 0:n * T].rearrange("p (c t) -> p c t", c=n),
                                                    g, ALU.mult), t, t_mgb)
                t2 = VE.do(lambda e: e.tensor_tensor(o, o, g, ALU.add), t)
                return t
            return evac
        t_x2 = to_tokens(hT, xtok2, t_h, f3, PE.last())
        for c in range(2):
            hold = []
            for part in range(2):
                project_T(a["w_branch_ret_2"][0][part * D:(part + 1) * D, c * 512:(c + 1) * 512],
                          lambda k, part=part: oR[:, 8 * part + k, :], evac_yb(4 * c), t_oR, parts=2, part=part,
                          hold=hold)
        t_merged = VE.last()

        def evac_res(c):
            def evac(bk, j, t):
                o = xtok2[:, j, c * 512:(c + 1) * 512]
                return VE.do(lambda e: e.tensor_tensor(o, banks[bk][:, :], o, ALU.add), t, t_x2)
            return evac
        for c in range(2):
            project_tok(a["w_out_2"][0][:, c * 512:(c + 1) * 512], lambda k: merged[:, k, :], evac_res(c), t_merged)
        t_h2 = VE.last()
        f4 = fence()
        b4.close()
        outer.close()

        b5 = Region(TT * D)
        rw = sb("rw", [P, KC, 36], stack=b5)
        rb = sb("rb", [P, 36], stack=b5)
        wrow = sb("wrow", [P, D], stack=b5)
        frow = sb("frow", [P, D], stack=b5)
        utok = sb("utok", [P, TT, D], stack=b5)
        lg = sb("lg", [P, TT, 36], stack=b5)
        tri = sb("tri", [P, P], stack=b5)
        ecol = sb("ecol", [P, 64], stack=b5)
        toki = sb("toki", [P, TT, 2, 2], I32, stack=b5)
        rt = sb("rt", [P, TT, 256], stack=b5)
        slots = sb("slots", [P, TT, 2], I32, stack=b5)
        tab = sb("tab", [P, NPAIR, 2], I32, stack=b5)
        t_rw = [load(PO, f"rw{g}", rw[:, :, 4 + 8 * g:12 + 8 * g], a["router_expert_w_2"][0, g].rearrange(
            "(k p) e -> p k e", p=P), f4) for g in range(NGRP)]
        t_rw.append(load(PO, "rwg", rw[:, :, 0:4], a["router_group_w_2"][0].rearrange("(k p) e -> p k e", p=P), f4))
        t_rb = [load(PO, "rbg", rb[:, 0:4], a["router_group_b_2"].partition_broadcast(P).rearrange("p o e -> p (o e)"), f4),
                load(PO, "rbe", rb[:, 4:36], a["router_expert_b_2"].rearrange("o g e -> o (g e)").partition_broadcast(
                    P).rearrange("p o e -> p (o e)"), f4)]
        t_wr = load(PO, "wrow", wrow[:, :], a["norm_ffn_w_2"].partition_broadcast(P).rearrange("p o e -> p (o e)"), f4)
        t_fr = load(PO, "frow", frow[:, :], a["norm_final_w_2"].rearrange("(o e) -> o e", o=1).partition_broadcast(
            P).rearrange("p o e -> p (o e)"), f4)
        t_tri = load(PO, "tri", tri[:, :], a["tri"], f4)
        t_ec = load(PO, "ecol", ecol[:, :], a["ecol"], f4)
        t_tk = load(PO, "toki", toki[:, :, :, :], a["toki"], f4)
        t_ti = load(PO, "tabinit", a["slot_table"].rearrange("(p q) c -> p (q c)", p=P), a["tab0"], f4)
        zero = uT[:, :, :].rearrange("p k t -> p (k t)")
        tz = PO.do(lambda e: e.memset(zero, 0.0), f4)
        t_zr = [load(PO, f"zrows{i}", a["rows"][i * 256:(i + 1) * 256, :].rearrange("(p q) d -> p (q d)", p=P), zero, tz)
                for i in range(2)]

        ss = small[:, 32:34]
        for j in range(TT):
            t = AC.do(lambda e, j=j: e.activation(utok[:, j, :], xtok2[:, j, :], ACT.Square,
                                                  accum_out=ss[:, j:j + 1]), t_h2, f4)
        t = AC.do(lambda e: e.activation(ss, ss, ACT.Sqrt, bias=epsc[:, 0:1], scale=1.0 / D), t)
        t = VE.do(lambda e: e.reciprocal(ss, ss), t)
        t_rows2 = []
        for j in range(TT):
            t2 = VE.do(lambda e, j=j: e.scalar_tensor_tensor(
                out=utok[:, j, :], in0=xtok2[:, j, :], scalar=ss[:, j:j + 1], in1=wrow[:, :],
                op0=ALU.mult, op1=ALU.mult), t, t_wr)
            t_rows2.append(load(PO, f"urows{j}", a["urows"][j * P:(j + 1) * P, :], utok[:, j, :], t2))
        uTe = hT
        t_ut = to_features(utok, uTe, t2)
        for j in range(TT):
            i, fr = take("side")
            for k in range(KC):
                f = lambda e, i=i, j=j, k=k: e.matmul(banks[i][:, 0:36], uTe[:, k, j * P:(j + 1) * P], rw[:, k, :],
                                                      start=k == 0, stop=k == KC - 1)
                t = (PE.do if k == KC - 1 else PE.quiet)(f, t_ut, t_rw, fr)
            t = VE.do(lambda e, i=i, j=j: e.tensor_tensor(lg[:, j, :], banks[i][:, 0:36], rb[:, :], ALU.add), t, t_rb)
            bank_free[i] = t

        def first_max(src, n, onehot, mxo, tmp, after):
            t = VE.do(lambda e: e.tensor_reduce(mxo, src, AXX, ALU.max), after)
            t = VE.do(lambda e: e.tensor_tensor(onehot, src, mxo.broadcast_to([P, TT, n]), ALU.is_lt), t)
            t = VE.do(lambda e: e.scalar_tensor_tensor(
                out=onehot, in0=onehot, scalar=1000.0, in1=ecol[:, 0:n].unsqueeze(1).broadcast_to([P, TT, n]),
                op0=ALU.mult, op1=ALU.add), t, t_ec)
            t = VE.do(lambda e: e.tensor_reduce(tmp, onehot, AXX, ALU.min), t)
            return VE.do(lambda e: e.tensor_tensor(onehot, onehot, tmp.broadcast_to([P, TT, n]), ALU.is_equal), t)

        R = lambda x, n: rt[:, :, x:x + n]
        gmax, goh, tmp1, eg, gsum = R(0, 1), R(1, 4), R(5, 1), R(6, 4), R(10, 1)
        el, m1, oh1, m2, oh2 = R(11, 8), R(19, 1), R(20, 8), R(28, 1), R(29, 8)
        e2, w1, w2_ = R(37, 1), R(38, 1), R(39, 1)
        d1, d2, sel = R(64, 32), R(96, 32), R(128, 32)
        pos, tmp32, slf = R(160, 32), R(192, 32), R(224, 2)
        gl = lg[:, :, 0:4]
        t_g = first_max(gl, 4, goh, gmax, tmp1, t)
        t = VE.do(lambda e: e.tensor_tensor(eg, gl, gmax.broadcast_to([P, TT, 4]), ALU.subtract), t_g)
        t = AC.do(lambda e: e.activation(eg, eg, ACT.Exp), t)
        t = VE.do(lambda e: e.tensor_reduce(gsum, eg, AXX, ALU.add), t)
        t = VE.do(lambda e: e.reciprocal(gsum, gsum), t)
        for g in range(NGRP):
            eo = lg[:, :, 4 + 8 * g:12 + 8 * g]
            if g == 0:
                t = VE.do(lambda e, eo=eo: e.tensor_tensor(el, eo, goh[:, :, 0:1].broadcast_to([P, TT, 8]), ALU.mult), t)
            else:
                t = VE.do(lambda e, eo=eo, g=g: e.tensor_tensor(
                    d1[:, :, 0:8], eo, goh[:, :, g:g + 1].broadcast_to([P, TT, 8]), ALU.mult), t)
                t = VE.do(lambda e: e.tensor_tensor(el, el, d1[:, :, 0:8], ALU.add), t)
        t = first_max(el, 8, oh1, m1, tmp1, t)
        t = VE.do(lambda e: e.scalar_tensor_tensor(out=el, in0=oh1, scalar=-3.0e38, in1=el,
                                                   op0=ALU.mult, op1=ALU.add), t)
        t = first_max(el, 8, oh2, m2, tmp1, t)
        t = VE.do(lambda e: e.tensor_tensor(e2, m2, m1, ALU.subtract), t)
        t = AC.do(lambda e: e.activation(e2, e2, ACT.Exp), t)
        t = VE.do(lambda e: e.tensor_scalar(w1, e2, 1.0, None, ALU.add), t)
        t = VE.do(lambda e: e.reciprocal(w1, w1), t)
        t = VE.do(lambda e: e.tensor_tensor(w1, w1, gsum, ALU.mult), t)
        t_w12 = VE.do(lambda e: e.tensor_tensor(w2_, w1, e2, ALU.mult), t)
        for dd, oh in ((d1, oh1), (d2, oh2)):
            for g in range(NGRP):
                t = VE.do(lambda e, dd=dd, oh=oh, g=g: e.tensor_tensor(
                    dd[:, :, 8 * g:8 * g + 8], oh, goh[:, :, g:g + 1].broadcast_to([P, TT, 8]), ALU.mult), t_w12)
        t = VE.do(lambda e: e.tensor_tensor(sel, d1, d2, ALU.add), t)
        for j in range(TT):
            i, fr = take("side")
            t1 = PE.do(lambda e, i=i, j=j: e.matmul(banks[i][:, 0:32], tri[:, :], sel[:, j, :], start=True,
                                                    stop=j == 0), t, t_tri, fr)
            if j:
                t1 = PE.do(lambda e, i=i: e.matmul(banks[i][:, 0:32], ones[:, :], sel[:, 0, :], start=False, stop=True))
            t1 = VE.do(lambda e, i=i, j=j: e.tensor_copy(pos[:, j, :], banks[i][:, 0:32]), t1)
            bank_free[i] = t1
        wov = sb("wov", [P, TT, NE], stack=b5)
        over = sb("over", [P, 4], stack=b5)
        flag = sb("flag", [P, 1], I32)
        t = VE.do(lambda e: e.tensor_scalar(tmp32, pos, float(CAP), None, ALU.is_ge), t1)
        t = VE.do(lambda e: e.tensor_tensor(sel, sel, tmp32, ALU.mult), t)
        VE.do(lambda e: e.tensor_reduce(over[:, 0:2].unsqueeze(2), sel, AXX, ALU.add), t)
        for j in range(TT):
            t1 = VE.do(lambda e, j=j: e.tensor_scalar(wov[:, j, :], d1[:, j, :], w1[:, j, :], None, ALU.mult), t)
            t1 = VE.do(lambda e, j=j: e.scalar_tensor_tensor(
                out=wov[:, j, :], in0=d2[:, j, :], scalar=w2_[:, j, :], in1=wov[:, j, :],
                op0=ALU.mult, op1=ALU.add), t1)
        t1 = VE.do(lambda e: e.tensor_tensor(wov[:, :, :], wov[:, :, :], tmp32, ALU.mult), t1)
        i, fr = take("side")
        t1 = PE.do(lambda e, i=i: e.matmul(banks[i][:, 0:2], ones[:, :], over[:, 0:2], start=True, stop=True), t1, fr)
        t1 = VE.do(lambda e, i=i: e.tensor_copy(over[:, 2:4], banks[i][:, 0:2]), t1)
        bank_free[i] = t1
        t1 = VE.do(lambda e: e.tensor_tensor(over[:, 0:1], over[:, 2:3], over[:, 3:4], ALU.add), t1)
        t1 = VE.do(lambda e: e.tensor_copy(flag[:, :], over[:, 0:1]), t1)
        t = VE.do(lambda e: e.tensor_scalar(tmp32, tmp32, 1.0e6, None, ALU.mult), t1)
        t = VE.do(lambda e: e.tensor_tensor(tmp32, tmp32, pos, ALU.add), t)
        t = VE.do(lambda e: e.tensor_tensor(tmp32, tmp32, ecol[:, 32:64].unsqueeze(1).broadcast_to([P, TT, 32]),
                                            ALU.add), t)
        for r, dd in enumerate((d1, d2)):
            t1 = VE.do(lambda e, dd=dd: e.tensor_tensor(sel, tmp32, dd, ALU.mult), t, VE.last(), PE.last())
            t1 = VE.do(lambda e, r=r: e.tensor_reduce(slf[:, :, r:r + 1], sel, AXX, ALU.add), t1)
        t_sl = VE.do(lambda e: e.tensor_copy(slots[:, :, :], slf), t1)
        t_sc = []
        for j in range(TT):
            for r in range(2):
                s = sem(f"d_slot{j}{r}")
                PO.items.append(([t_sl, t_ti, t_tk], lambda e, j=j, r=r: e.indirect_dma_start(
                    a["slot_table"], bass.IndirectOffsetOnAxis(ap=slots[:, j, r:r + 1].bitcast(U32), axis=0),
                    toki[:, j, r, :], None, bounds_check=NSLOT - 1, oob_is_err=False), (s, 16)))
                t_sc.append((s, 16))
        t_tab = load(PO, "table", tab[:, :, :], a["slot_table"].rearrange("(q p) c -> p q c", p=P), t_sc)

        xg = [sb(f"xg{i}", [P, D], stack=b5) for i in range(3)]
        xgT = [sb(f"xgT{i}", [P, KC, P], stack=b5) for i in range(2)]
        hp = [sb(f"hp{i}", [P, HID], stack=b5) for i in range(2)]
        hpT = [sb(f"hpT{i}", [P, 4, P], stack=b5) for i in range(2)]
        yo = [sb(f"yo{i}", [P, D], stack=b5) for i in range(2)]
        xg_free, xgT_free, hp_free, hpT_free, yo_free = ([None] * 3 for _ in range(5))
        xg_free = [f4] * 3
        gat = {}

        def gather(p):
            s = sem(f"d_gather{p}")
            PO.items.append(([t_tab, t_rows2, xg_free[p % 3]], lambda e, p=p: e.indirect_dma_start(
                xg[p % 3][:, :], None, a["urows"],
                bass.IndirectOffsetOnAxis(ap=tab[:, p, 0:1].bitcast(U32), axis=0)), (s, 16)))
            gat[p] = (s, 16)

        for p in range(3):
            gather(p)
        t_scat = []
        eng_free = {}

        def expert_block(w, e):
            if w == "down":
                return stream(a["expert_w_down_2"][0, e], 4, D)
            return stream(a[f"expert_w_{w}_2"][0, e])

        for p in range(NPAIR):
            E2 = (2 * p, 2 * p + 1)
            X = xgT[p % 2]
            for k0 in range(0, KC, 4):
                i, fr = take("side")
                for k in range(4):
                    f = lambda e, i=i, k=k, k0=k0, p=p: e.transpose(
                        banks[i][:, k * P:(k + 1) * P], xg[p % 3][:, (k0 + k) * P:(k0 + k + 1) * P], ident[:, :])
                    t = (PE.do if k == 3 else PE.quiet)(f, gat[p], fr)
                t2 = AC.do(lambda e, i=i, k0=k0, X=X: e.activation(
                    X[:, k0:k0 + 4, :], banks[i][:, :].rearrange("p (k s) -> p k s", k=4), ACT.Copy), t,
                    xgT_free[p % 2], f4)
                bank_free[i] = t2
            xg_free[p % 3] = t
            t_X = t2
            if p + 3 < NPAIR:
                gather(p + 3)
            tg = {}
            for w in ("gate", "up"):
                bl = [expert_block(w, e) for e in E2]
                bk, fr = take("gemm")
                for k in range(KC):
                    for s_ in range(2):
                        f = lambda e, bk=bk, s_=s_, k=k, bl=bl, X=X: e.matmul(
                            banks[bk][64 * s_:64 * s_ + 64, :], X[:, k, 64 * s_:64 * s_ + 64], bl[s_][1][:, k, :],
                            start=k == 0, stop=k == KC - 1)
                        t = (PE.do if k == KC - 1 else PE.quiet)(f, bl[s_][2], fr, t_X)
                        ring_free[bl[s_][0]] = t
                H = hp[p % 2]
                if w == "gate":
                    t = AC.do(lambda e, bk=bk, H=H: e.activation(H[:, :], banks[bk][:, :], ACT.Silu), t,
                              hp_free[p % 2], f4)
                    bank_free[bk] = t
                    tgate = t
                else:
                    t = VE.do(lambda e, bk=bk, H=H: e.tensor_tensor(H[:, :], banks[bk][:, :], H[:, :], ALU.mult), t,
                              tgate)
                    bank_free[bk] = t
            xgT_free[p % 2] = PE.last()
            i, fr = take("side")
            for c in range(4):
                f = lambda e, i=i, c=c, H=H: e.transpose(banks[i][:, c * P:(c + 1) * P], H[:, c * P:(c + 1) * P],
                                                         ident[:, :])
                t2 = (PE.do if c == 3 else PE.quiet)(f, t, fr)
            hp_free[p % 2] = t2
            HT = hpT[p % 2]
            t = AC.do(lambda e, i=i, HT=HT: e.activation(HT[:, :, :], banks[i][:, :].rearrange(
                "p (k s) -> p k s", k=4), ACT.Copy), t2, hpT_free[p % 2], f4)
            bank_free[i] = t
            bl = [expert_block("down", e) for e in E2]
            bks = [take("gemm") for _ in range(2)]
            for n in range(2):
                bk, fr = bks[n]
                for k in range(4):
                    for s_ in range(2):
                        f = lambda e, bk=bk, s_=s_, k=k, n=n, bl=bl, HT=HT: e.matmul(
                            banks[bk][64 * s_:64 * s_ + 64, :], HT[:, k, 64 * s_:64 * s_ + 64],
                            bl[s_][1][:, k, n * 512:(n + 1) * 512], start=k == 0, stop=k == 3)
                        t3 = (PE.do if k == 3 else PE.quiet)(f, bl[s_][2], fr, t)
                        ring_free[bl[s_][0]] = t3
                Y = yo[p % 2]
                q = (VE, AC)[n]
                t4 = q.do((lambda e, bk=bk, Y=Y: e.tensor_copy(Y[:, 0:512], banks[bk][:, :])) if n == 0 else
                          (lambda e, bk=bk, Y=Y: e.activation(Y[:, 512:1024], banks[bk][:, :], ACT.Copy)), t3,
                          yo_free[p % 2], f4)
                bank_free[bk] = t4
            hpT_free[p % 2] = PE.last()
            s = sem(f"d_scatter{p}")
            PO.items.append(([VE.last(), AC.last(), t_zr], lambda e, p=p, Y=Y: e.indirect_dma_start(
                a["rows"], bass.IndirectOffsetOnAxis(ap=tab[:, p, 1:2].bitcast(U32), axis=0), Y[:, :], None,
                bounds_check=511, oob_is_err=False), (s, 16)))
            yo_free[p % 2] = (s, 16)
            t_scat.append((s, 16))

        back = [[ring[0][:, 0:D], ring[0][:, D:2 * D]], [ring[1][:, 0:D], ring[1][:, D:2 * D]]]
        for j in range(TT):
            tb = [load(SP, f"back{j}{r}", back[j][r], a["rows"][r * T + j * P:r * T + (j + 1) * P, :], t_scat,
                       ring_free[0], ring_free[1]) for r in range(2)]
            o = xtok2[:, j, :]
            t = VE.do(lambda e, j=j, o=o: e.scalar_tensor_tensor(
                out=o, in0=back[j][0], scalar=w1[:, j, :], in1=o, op0=ALU.mult, op1=ALU.add), tb)
            t = VE.do(lambda e, j=j, o=o: e.scalar_tensor_tensor(
                out=o, in0=back[j][1], scalar=w2_[:, j, :], in1=o, op0=ALU.mult, op1=ALU.add), t)
        VE.quiet(lambda e: e.wait_ge(VE.sem, VE.count))
        AC.quiet(lambda e: e.wait_ge(t_fr[0], t_fr[1]))

        with nc.Block() as block:
            block.sync(SP.emit)
            block.scalar(AC.emit)
            block.vector(VE.emit)
            block.gpsimd(PO.emit)
            block.tensor(PE.emit)

        hidT = sb("hidT", [P, 4, T], stack=b5)
        wcol = sb("wcol", [P, TT, 1], stack=b5)
        loop_sems = [nc.alloc_semaphore(f"loop{i}") for i in range(6)]
        first = loop_sems[0].num
        assert [x.num for x in loop_sems] == list(range(first, first + 6))
        n_over = nc.values_load(flag[0:1, 0:1], min_val=0, max_val=2 * T)
        with nc.If(n_over > 0):
            with nc.Fori(0, NE) as ex:
                lPE, lAC, lVE = (Queue(n, s) for n, s in zip(("pe", "act", "dve"), loop_sems[3:6]))
                W = []
                for i, (name, kc, cols) in enumerate((("gate", KC, HID), ("up", KC, HID), ("down", 4, D))):
                    w = ring[i][:, 0:kc * cols].rearrange("p (k n) -> p k n", k=kc)
                    src = a[f"expert_w_{name}_2"][0, bass.ds(ex, 1)].rearrange("o (k p) n -> p (o k) n", p=P)
                    nc.sync.dma_start(w, src).then_inc(loop_sems[i], 16)
                    W.append((w, (loop_sems[i], 16)))
                t_wc = lVE.do(lambda e: e.tensor_copy(wcol[:, :, :], wov[:, :, bass.ds(ex, 1)]))
                for m in range(2):
                    for c in range(4):
                        for k in range(KC):
                            whole = c == 3 and k == KC - 1
                            (lPE.do if whole else lPE.quiet)(lambda e, m=m, c=c, k=k: e.matmul(
                                banks[2 * m + c // 2][:, (c % 2) * T:(c % 2 + 1) * T],
                                W[m][0][:, k, c * P:(c + 1) * P], uTe[:, k, :], start=k == 0, stop=k == KC - 1),
                                W[m][1])
                t_h = None
                for b in range(2):
                    h2 = hidT[:, 2 * b:2 * b + 2, :].rearrange("p c t -> p (c t)")
                    t_s = lAC.do(lambda e, b=b, h2=h2: e.activation(h2, banks[b][:, :], ACT.Silu), (lPE.sem, 1))
                    t_h = lVE.do(lambda e, b=b, h2=h2: e.tensor_tensor(h2, banks[2 + b][:, :], h2, ALU.mult),
                                 t_s, (lPE.sem, 2))
                for j in range(TT):
                    for n in range(2):
                        for k in range(4):
                            f = lambda e, j=j, n=n, k=k: e.matmul(
                                banks[4 + 2 * j + n][:, :], hidT[:, k, j * P:(j + 1) * P],
                                W[2][0][:, k, n * 512:(n + 1) * 512], start=k == 0, stop=k == 3)
                            t = (lPE.do if k == 3 else lPE.quiet)(f, W[2][1], t_h)
                        o = xtok2[:, j, n * 512:(n + 1) * 512]
                        lVE.do(lambda e, j=j, n=n, o=o: e.scalar_tensor_tensor(
                            out=o, in0=banks[4 + 2 * j + n][:, :], scalar=wcol[:, j, :], in1=o,
                            op0=ALU.mult, op1=ALU.add), t, t_wc)
                lPE.emit(nc.tensor)
                lAC.emit(nc.scalar)
                lVE.emit(nc.vector)
                nc.vector.wait_ge(lVE.sem, lVE.count)
                nc.all_engine_barrier(sems_to_clear=range(first, first + 6))

        ss2 = small[:, 34:36]
        outs = []
        tAC, tVE, tSP = (Queue(n, sem("s_tail_" + n)) for n in ("act", "dve", "sp"))
        for j in range(TT):
            o = xtok2[:, j, :]
            t = tAC.do(lambda e, j=j, o=o: e.activation(back[j][0], o, ACT.Square, accum_out=ss2[:, j:j + 1]))
            t = tAC.do(lambda e, j=j: e.activation(ss2[:, j:j + 1], ss2[:, j:j + 1], ACT.Sqrt, bias=epsc[:, 0:1],
                                                   scale=1.0 / D), t)
            t = tVE.do(lambda e, j=j: e.reciprocal(ss2[:, j:j + 1], ss2[:, j:j + 1]), t)
            t = tVE.do(lambda e, j=j, o=o: e.scalar_tensor_tensor(
                out=back[j][1], in0=o, scalar=ss2[:, j:j + 1], in1=frow[:, :], op0=ALU.mult, op1=ALU.mult), t)
            outs.append(load(tSP, f"out{j}", out[0, j * P:(j + 1) * P, :], back[j][1], t))

        def store(e):
            tSP.emit(e)
            for s, v in outs:
                e.wait_ge(s, v)

        with nc.Block() as block:
            block.scalar(tAC.emit)
            block.vector(tVE.emit)
            block.sync(store)


def two_pi_parts():
    rest, parts = 2 * np.pi, []
    for bits in (9, 11):
        scale = 2.0 ** (bits - 3)
        part = np.floor(rest * scale * 2.0 ** (0 if not parts else 9)) / (scale * 2.0 ** (0 if not parts else 9))
        parts.append(float(part))
        rest -= part
    return parts + [float(np.float32(rest))]


TWO_PI_PARTS = two_pi_parts()


def constants():
    s, t = np.arange(P)[:, None], np.arange(P)[None, :]
    masks = np.zeros((P, len(LEVELS), P), np.int32)
    for i, m in enumerate(LEVELS):
        masks[:, i, :] = (s == t) if m == 1 else ((s // m == t // m) & (s % m < m // 2) & (t % m >= m // 2))
    far = 1.0e32
    q, k = np.arange(P)[:, None], np.arange(T)[None, :]
    d0 = (q - k[:, :P]).astype(np.float64)
    d1 = (q + P - k).astype(np.float64)
    dist = np.concatenate([np.where(d0 >= 0, d0, far), np.where(d1 >= 0, d1, far)], 1).astype(np.float32)
    lg = np.log(1.0 - 2.0 ** (-5.0 - np.arange(HEADS)))
    dec = np.zeros((P, HEADS, 384), np.float32)
    for h in range(HEADS):
        r0 = np.arange(T)[None, :] - s
        r1 = t - s
        r = np.concatenate([r0, r1], 1)
        dec[:, h] = np.where(r >= 0, np.exp(lg[h] * np.maximum(r, 0)), 0.0)
    theta = (np.float32(1.0) / np.power(np.float32(10000.0), np.linspace(0.0, 1.0, P, dtype=np.float32)))
    ecol = np.tile(np.concatenate([np.arange(32), CAP * np.arange(32)]).astype(np.float32), (P, 1))
    toki = np.zeros((P, TT, 2, 2), np.int32)
    for j in range(TT):
        for r in range(2):
            toki[:, j, r, 0] = j * P + np.arange(P)
            toki[:, j, r, 1] = r * T + j * P + np.arange(P)
    tab0 = np.tile(np.array([0, 1 << 20], np.int32), (P, NSLOT // P)).reshape(P, -1)
    return {"ident": np.eye(P, dtype=np.float32), "masks": masks, "dist": dist, "decay": dec,
            "theta": theta.astype(np.float32).reshape(P, 1), "tri": (s < t).astype(np.float32), "ecol": ecol,
            "toki": toki, "tab0": tab0}


def kernel(**inputs):
    import concourse.bacc as bacc
    from concourse.bass_utils import run_bass_kernel_spmd

    nc = bacc.Bacc("TRN2", target_bir_lowering=False, num_devices=1)
    arrays, a = {}, {}
    for name, x in {**inputs, **constants()}.items():
        x = np.ascontiguousarray(x)
        arrays["in_" + name] = x
        a[name] = nc.dram_tensor("in_" + name, x.shape, mybir.dt.from_np(x.dtype), kind="ExternalInput").ap()
    a["slot_table"] = nc.dram_tensor("slot_table", (NSLOT, 2), I32, kind="Internal").ap()
    a["urows"] = nc.dram_tensor("urows", (T, D), F32, kind="Internal").ap()
    a["rows"] = nc.dram_tensor("rows", (2 * T, D), F32, kind="Internal").ap()
    out = nc.dram_tensor("out_0", (1, T, D), F32, kind="ExternalOutput").ap()
    build(nc, a, out)
    r = run_bass_kernel_spmd(nc, [arrays], core_ids=[0])
    return r.results[0]["out_0"]
```

```python
import numpy as np
from contextlib import ExitStack

import concourse.bass as bass
from concourse import mybir
from concourse.alu_op_type import AluOpType as ALU

F32 = mybir.dt.float32
F32R = mybir.dt.float32r
I32 = mybir.dt.int32
U32 = mybir.dt.uint32
ACT = mybir.ActivationFunctionType
AXX = mybir.AxisListType.X

P = 128
T = 256
TT = T // P
D = 1024
KC = D // P
EPS = 1e-6
HEADS = 4
CH = 64
LEVELS = [1, 2, 4, 8, 16, 32, 64, 128]
FF = 2816
FFC = FF // P
NE, NGRP, EPG, HID = 32, 4, 8, 512
CAP = 64
NPAIR = NE // 2
RING = 3
UNITS = 3
UNIT = 1024
ARENA = 23824
LAMBDA_INIT = 0.2
ROWS = dict(b_ada=0, norm1=48, norm2=56, mixn=64, ffnn=72, fin1=80, lb0=88, lb1=92, gn=96,
            subln=97, gkb=98, glan=102, retn=104, c=120)


class Queue:

    def __init__(self, name, sem):
        self.name, self.sem, self.count, self.items = name, sem, 0, []

    def do(self, fn, *after):
        self.count += 1
        self.items.append((after, fn, (self.sem, 1)))
        return (self.sem, self.count)

    def quiet(self, fn, *after):
        self.items.append((after, fn, None))

    def last(self):
        return (self.sem, self.count)

    def emit(self, eng):
        met = {}

        def wait(after):
            for a in after:
                if a is None:
                    continue
                if len(a) == 2 and isinstance(a[1], int):
                    if a[1] > met.get(a[0].num, 0):
                        eng.wait_ge(a[0], a[1])
                        met[a[0].num] = a[1]
                else:
                    wait(a)

        for after, fn, inc in self.items:
            wait(after)
            if fn is None:
                continue
            ins = fn(eng)
            if inc:
                ins.then_inc(inc[0], inc[1])


def build(nc, a, out):
    ctx = ExitStack()
    with ctx:
        arena = [None]

        class Region:

            def __init__(self, start=0):
                self.at = start

        def sb(name, shape, dt=F32, stack=None, ctx=ctx):
            if stack is None:
                return ctx.enter_context(nc.sbuf_tensor(name, shape, dt))
            n = int(np.prod(shape[1:]))
            v = arena[0][0:shape[0], stack.at:stack.at + n]
            stack.at += n
            assert stack.at <= ARENA, (name, stack.at)
            if dt != F32:
                v = v.bitcast(dt)
            if len(shape) == 3:
                v = v.rearrange("p (a b) -> p a b", a=shape[1])
            elif len(shape) == 4:
                v = v.rearrange("p (a b c) -> p a b c", a=shape[1], b=shape[2])
            return v

        def sem(name):
            return ctx.enter_context(nc.semaphore(name))

        PE, AC, VE, PO, SP = (Queue(n, sem("s_" + n)) for n in ("pe", "act", "dve", "pool", "sp"))

        def load(q, name, dst, src, *after):
            s = sem("d_" + name)
            q.items.append((after, lambda e: e.dma_start(dst, src), (s, 16)))
            return (s, 16)

        def fence():
            return [PE.last(), AC.last(), VE.last(), PO.last()]

        arena[0] = ctx.enter_context(nc.sbuf_tensor("arena", [P, ARENA], F32))
        class Slot:

            def __init__(self, name, buf, free=None):
                self.buf, self.sem, self.free, self.uses = buf, sem("s_" + name), free, 0

        ring = [Slot(f"weights{i}", sb(f"weights{i}", [P, KC * 512])) for i in range(RING)]
        ident = sb("ident", [P, P])
        ones = sb("ones", [P, P])
        pcol = sb("pcol", [P, P])
        hT = sb("hT", [P, KC, T])
        modc = sb("modc", [P, 48])
        scl = sb("scl", [P, 16])
        lamrow = sb("lamrow", [1, 4, 64])
        lams = sb("lams", [1, 8])
        chainm = sb("chainm", [P, HEADS * T])
        maskf = sb("masks", [P, len(LEVELS) * P])
        wmix = sb("wmix", [P, KC])
        flag = sb("flag", [P, 1], I32)
        small = sb("small", [P, 64])
        rstd = sb("rstd", [P, T])
        epsc = sb("epsc", [P, 1])
        eps2 = sb("eps2", [P, 1])
        halves = ctx.enter_context(ExitStack())
        XH = sb("XH", [P, KC, T], F32R, ctx=halves)
        XL = sb("XL", [P, KC, T], F32R, ctx=halves)
        WHL = sb("WHL", [P, UNITS, 2, UNIT], F32R, ctx=halves)
        s_hi, s_lo = sem("s_weights_hi"), sem("s_weights_lo")
        x_ready, x_free = [None] * KC, [None] * KC
        unit_free, unit_n = [None] * UNITS, [0]
        mark = {}
        banks = [ctx.enter_context(nc.psum_tensor(f"bank{i}", [P, 512], F32)) for i in range(8)]
        bank_free = [None] * 8
        gemm_n, side_n = [0], [0]

        def take(kind):
            n = gemm_n if kind == "gemm" else side_n
            i = n[0] % 4 + (0 if kind == "gemm" else 4)
            n[0] += 1
            return i, bank_free[i]

        def stream(src, kc=KC, cols=512, rows="(k p) n -> p k n"):
            slot = ring.pop(0)
            ring.append(slot)
            slot.uses += 1
            dst = slot.buf[:, 0:kc * cols].rearrange("p (k n) -> p k n", k=kc)
            s = src.rearrange(rows, p=P)
            SP.items.append(([slot.free], lambda e: e.dma_start(dst, s), (slot.sem, 16)))
            return slot, dst, (slot.sem, 16 * slot.uses)

        early = Region()
        prow = sb("prow", [P, P], stack=early)
        xtok = sb("xtok", [P, TT, D], stack=early)
        t_id = load(AC, "ident", ident[:, :], a["ident"])
        t_x = load(SP, "x", xtok[:, :, :], a["x"][0].rearrange("(i p) d -> p i d", p=P))
        t_rows = []
        for name, src, n in [("b_ada", a["b_ada"], 48), ("norm1", a["norm1_w"], 8), ("norm2", a["norm2_w"], 8),
                             ("mixn", a["norm_mix_w_2"], 8), ("ffnn", a["norm_ffn_w_2"], 8),
                             ("fin1", a["final_norm_w"].rearrange("(o n) -> o n", o=1), 8),
                             ("lb0", a["hgrn_lb_logits"][0:1], 4), ("lb1", a["hgrn_lb_logits"][1:2], 4),
                             ("gn", a["hgrn_gnorm_w"], 1), ("subln", a["diff_subln_w"], 1),
                             ("gkb", a["gla_gk_bias_2"], 4), ("glan", a["gla_norm_w_2"], 2),
                             ("retn", a["ret_norm_w_2"], 16), ("c", a["c"], 8)]:
            r = ROWS[name]
            t_rows.append(load(SP if r % 16 else AC, "row_" + name, prow[r:r + n, :],
                               src.rearrange("o (r p) -> (o r) p", p=P)))
        SP.items.append(([t_rows, t_x, t_id], None, None))
        t_ones = VE.do(lambda e: e.memset(ones[:, :], 1.0))
        t_eps = VE.do(lambda e: e.memset(epsc[:, :], EPS))
        t_eps = VE.do(lambda e: e.memset(eps2[:, :], EPS * EPS))
        bi, bf = take("side")
        t = PE.do(lambda e: e.transpose(banks[bi][:, 0:P], prow[:, :], ident[:, :]), t_rows, t_id)
        t_pcol = VE.do(lambda e: e.tensor_copy(pcol[:, :], banks[bi][:, 0:P]), t)
        bank_free[bi] = t_pcol

        def col(name, k=0):
            r = ROWS[name] + k
            return pcol[:, r:r + 1]

        cT = small[:, 0:8]
        t_cT = AC.do(lambda e: e.activation(cT, pcol[:, ROWS["c"]:ROWS["c"] + 8], ACT.Silu), t_pcol)

        def to_features(src, dst, *after):
            t = None
            for k in range(KC):
                i, fr = take("side")
                for j in range(TT):
                    f = lambda e, i=i, j=j, k=k: e.transpose(banks[i][:, j * P:(j + 1) * P],
                                                             src[:, j, k * P:(k + 1) * P], ident[:, :])
                    t = (PE.do if j == TT - 1 else PE.quiet)(f, after, fr)
                q = VE if k % 2 else AC
                g = ((lambda e, i=i, k=k: e.tensor_copy(dst[:, k, :], banks[i][:, 0:T])) if k % 2 else
                     (lambda e, i=i, k=k: e.activation(dst[:, k, :], banks[i][:, 0:T], ACT.Copy)))
                t = q.do(g, t)
                bank_free[i] = t
            return [AC.last(), VE.last()]

        def to_tokens(src, dst, *after):
            for j in range(TT):
                for k0 in range(0, KC, 4):
                    i, fr = take("side")
                    for k in range(4):
                        f = lambda e, i=i, j=j, k=k, k0=k0: e.transpose(
                            banks[i][:, k * P:(k + 1) * P], src[:, k0 + k, j * P:(j + 1) * P], ident[:, :])
                        t = (PE.do if k == 3 else PE.quiet)(f, after, fr)
                    t = AC.do(lambda e, i=i, j=j, k0=k0: e.activation(
                        dst[:, j, k0 * P:(k0 + 4) * P], banks[i][:, :], ACT.Copy), t)
                    bank_free[i] = t
            return t

        t_h = to_features(xtok, hT, t_x, t_id)

        scratch = sb("squares", [P, KC, T], stack=Region(ARENA - 1024 - KC * T))

        def split_x(k, src, *after, shift=None):
            t = AC.do((lambda e: e.activation(XH[:, k, :], src, ACT.Copy)) if shift is None else
                      (lambda e: e.activation(XH[:, k, :], src, ACT.Identity, bias=shift)), after, x_free[k])
            x_ready[k] = VE.do((lambda e: e.tensor_tensor(XL[:, k, :], src, XH[:, k, :], ALU.subtract))
                               if shift is None else
                               (lambda e: e.scalar_tensor_tensor(out=XL[:, k, :], in0=src, scalar=shift,
                                                                 in1=XH[:, k, :], op0=ALU.add, op1=ALU.subtract)), t)

        def sums(src, sq, toks, scales=(None,)):
            got = [take("side") for _ in scales]
            AC.do(lambda e: e.activation(small[:, 40:41], epsc[:, 0:1], ACT.Sqrt), t_eps)
            for k in range(KC):
                for (i, fr), scale, dst in zip(got, scales, sq):
                    t = AC.do((lambda e, k=k, dst=dst: e.activation(dst[:, k, :], src[:, k, :], ACT.Square))
                              if scale is None else
                              (lambda e, k=k, dst=dst, scale=scale: e.activation(
                                  dst[:, k, :], src[:, k, :], ACT.Square, scale=scale(k))), toks[k])
                    f = lambda e, k=k, i=i, dst=dst: e.matmul(banks[i][:, 0:T], ones[:, :], dst[:, k, :],
                                                              start=k == 0, stop=k == KC - 1)
                    t = (PE.do if k == KC - 1 else PE.quiet)(f, t, fr, t_ones)
            return [i for i, _ in got], t

        def norm_scale(src, toks):
            (i,), t = sums(src, [scratch], toks)
            t = AC.do(lambda e: e.activation(rstd[:, :], banks[i][:, 0:T], ACT.Sqrt, bias=epsc[:, 0:1],
                                             scale=1.0 / D), t, t_eps, VE.last())
            bank_free[i] = t
            return VE.do(lambda e: e.reciprocal(rstd[:, :], rstd[:, :]), t)

        def norm_apply(src, weight, shift, t, *after):
            t2 = {}
            for k in range(KC + 2):
                if k < KC:
                    t2[k] = VE.do(lambda e, k=k: e.scalar_tensor_tensor(
                        out=scratch[:, k, :], in0=src[:, k, :], scalar=weight(k), in1=rstd[:, :],
                        op0=ALU.mult, op1=ALU.mult), t, after)
                if k >= 2:
                    split_x(k - 2, scratch[:, k - 2, :], t2[k - 2], shift=shift(k - 2))

        def steps(src, evac, tok=False, kc=KC, cols=512, parts=1, part=0, hold=None, step=1, xo=0):
            slot, w, t_w = stream(src, kc, cols)
            per = UNIT // cols
            nu = kc // per
            groups = list(range(TT)) if tok else list(range(cols // P))
            nb = TT if tok else (cols + 255) // 256
            if part == 0:
                got = [take("gemm") for _ in range(nb)]
                if hold is not None:
                    hold.extend(got)
            else:
                got = hold
            pieces = {}

            def split(u, ahead):
                n = unit_n[0]
                unit_n[0] += 1
                b = n % UNITS
                hi, lo = (WHL[:, b, x, :].rearrange("p (k n) -> p k n", k=per) for x in range(2))
                ws = w[:, u * per:(u + 1) * per, :]
                for q, item in ((AC, ([t_w, unit_free[b]], lambda e: e.activation(hi, ws, ACT.Copy), (s_hi, 1))),
                                (VE, ([(s_hi, n + 1)], lambda e: e.tensor_tensor(lo, ws, hi, ALU.subtract),
                                      (s_lo, 1)))):
                    if ahead and q in mark:
                        q.items.insert(mark[q], item)
                        mark[q] += 1
                    else:
                        q.items.append(item)
                pieces[u] = (b, hi, lo, (s_lo, n + 1))
                slot.free = (s_lo, n + 1)

            for u in range(min(2, nu)):
                split(u, True)
            for u in range(nu):
                if u + 2 < nu:
                    split(u + 2, False)
                if u == nu - 1:
                    mark[AC], mark[VE] = len(AC.items), len(VE.items)
                b, hi, lo, t_lo = pieces[u]
                for kk in range(per):
                    k = u * per + kk
                    x = xo + k
                    for g in groups:
                        bk, fr = got[g if tok else g // 2]
                        for n, (wp, xp) in enumerate(((hi, XH), (hi, XL), (lo, XH))):
                            if tok:
                                o = banks[bk][:, 0:cols]
                                l, r = xp[:, x, g * P:(g + 1) * P], wp[:, kk, :]
                            else:
                                o = banks[bk][:, (g % 2) * T:(g % 2 + 1) * T]
                                l = (wp[:, kk, 256 * (g // 2) + g % 2:256 * (g // 2) + 256:2] if step == 2 else
                                     wp[:, kk, g * P:(g + 1) * P])
                                r = xp[:, x, :]
                            st = part == 0 and k == 0 and n == 0 and (tok or g % 2 == 0)
                            f = lambda e, o=o, l=l, r=r, st=st, k=k, n=n: e.matmul(
                                o, l, r, start=st, stop=part == parts - 1 and k == kc - 1 and n == 2,
                                skip_group_check=True)
                            last = g == groups[-1] and n == 2
                            t = (PE.do if last else PE.quiet)(f, t_lo, fr if part == 0 else None, x_ready[x])
                    x_free[x] = t
                unit_free[b] = t
                if u == nu // 2 - 1:
                    yield
            if part == parts - 1:
                for b in range(nb):
                    bk = got[b][0]
                    bank_free[bk] = evac(bk, b, t) if tok else evac(bk, 2 * b, min(2, cols // P - 2 * b), t)
            yield

        def project(*args, **kw):
            for _ in steps(*args, **kw):
                pass

        def weave(mains, *lanes):
            n, live = 0, list(lanes)

            def turn(n):
                for lane in list(live):
                    if n is None or lane[0] <= n:
                        try:
                            next(lane[1])
                        except StopIteration:
                            live.remove(lane)
            turn(-1)
            for m in mains:
                for _ in m:
                    turn(n)
                    n += 1
            while live:
                turn(None)

        def copy_T(dst, base=0, scale=1.0, func=ACT.Copy, wait=None):
            def evac(bk, ch, n, t):
                o = dst[:, base + ch:base + ch + n, :]
                return AC.do(lambda e: e.activation(o, banks[bk][:, 0:n * T].rearrange("p (c t) -> p c t", c=n),
                                                    func, scale=scale), t, wait)
            return evac

        def copy_tok(dst, c0, wait=None):
            def evac(bk, j, t):
                return VE.do(lambda e: e.tensor_copy(dst[:, j, c0:c0 + 512], banks[bk][:, :]), t, wait)
            return evac

        mreg = Region(ARENA - 1024)
        macc = [sb(f"macc{i}", [P, 512], stack=mreg) for i in range(2)]
        macc_free = [None, None]
        SPLIT = 5

        def modulations(ns):
            for n in ns:
                slot, w, t_w = stream(a["w_ada"][0][:, n * 512:(n + 1) * 512])
                m, g = macc[n % 2], w[:, SPLIT, :]
                tv = VE.do(lambda e, m=m, w=w: e.tensor_scalar(m[:, :], w[:, 0, :], cT[:, 0:1], None, ALU.mult),
                           t_w, t_cT, macc_free[n % 2])
                for k in range(1, SPLIT):
                    tv = VE.do(lambda e, k=k, m=m, w=w: e.scalar_tensor_tensor(
                        out=m[:, :], in0=w[:, k, :], scalar=cT[:, k:k + 1], in1=m[:, :],
                        op0=ALU.mult, op1=ALU.add), tv)
                for k in range(SPLIT, KC):
                    ta = AC.do(lambda e, k=k, w=w: e.activation(w[:, k, :], w[:, k, :], ACT.Copy,
                                                                scale=cT[:, k:k + 1]), t_w, t_cT)
                tp = None
                for k in range(SPLIT + 1, KC):
                    tp = PO.do(lambda e, k=k, w=w, g=g: e.tensor_tensor(g, g, w[:, k, :], ALU.add), ta, tp)
                yield
                bk, fr = take("side")
                for c in range(4):
                    for last, x in enumerate((m, g)):
                        f = lambda e, c=c, x=x, bk=bk, last=last: e.matmul(
                            banks[bk][:, c * P:(c + 1) * P], x[:, c * P:(c + 1) * P], ones[:, :],
                            start=not last, stop=bool(last))
                        t = (PE.do if c == 3 else PE.quiet)(f, tv, tp, fr, t_ones)
                slot.free = t
                macc_free[n % 2] = t
                t = VE.do(lambda e, bk=bk, n=n: e.tensor_tensor(modc[:, 4 * n:4 * n + 4], banks[bk][:, 0:512:P],
                                                                pcol[:, 4 * n:4 * n + 4], ALU.add), t)
                bank_free[bk] = t

        t_rstd = norm_scale(hT, [t_h] * KC)
        for _ in modulations(range(4)):
            pass
        t_mod0 = VE.last()
        t_scl1 = VE.do(lambda e: e.scalar_tensor_tensor(
            out=scl[:, 0:8], in0=modc[:, 8:16], scalar=1.0, in1=pcol[:, ROWS["norm1"]:ROWS["norm1"] + 8],
            op0=ALU.add, op1=ALU.mult), t_mod0)

        lbc = small[:, 8:12]
        oml = small[:, 12:16]
        l0 = pcol[:, ROWS["lb0"]:ROWS["lb0"] + 4]
        l1 = pcol[:, ROWS["lb1"]:ROWS["lb1"] + 4]
        mx, e0, e1 = small[:, 16:20], small[:, 20:24], small[:, 24:28]
        t = VE.do(lambda e: e.tensor_tensor(mx, l0, l1, ALU.max), t_pcol)
        VE.do(lambda e: e.tensor_tensor(e0, l0, mx, ALU.subtract), t)
        t = VE.do(lambda e: e.tensor_tensor(e1, l1, mx, ALU.subtract), t)
        t = AC.do(lambda e: e.activation(small[:, 20:28], small[:, 20:28], ACT.Exp), t)
        t = VE.do(lambda e: e.tensor_tensor(mx, e0, e1, ALU.add), t)
        t = VE.do(lambda e: e.reciprocal(mx, mx), t)
        VE.do(lambda e: e.tensor_tensor(lbc, e0, mx, ALU.mult), t)
        t_lb = VE.do(lambda e: e.tensor_tensor(oml, e1, mx, ALU.mult), t)

        t_l = [load(PO, "lam" + n, lamrow[:, i, :], a["diff_lambda_" + n]) for i, n in enumerate(["q1", "k1", "q2", "k2"])]
        t = VE.do(lambda e: e.tensor_tensor(lamrow[:, 0::2, :], lamrow[:, 0::2, :], lamrow[:, 1::2, :], ALU.mult), t_l)
        t = VE.do(lambda e: e.tensor_reduce(lams[:, 0:2], lamrow[:, 0::2, :], AXX, ALU.add), t)
        t = AC.do(lambda e: e.activation(lams[:, 2:4], lams[:, 0:2], ACT.Exp), t)
        t = VE.do(lambda e: e.tensor_tensor(lams[:, 4:5], lams[:, 3:4], lams[:, 2:3], ALU.subtract), t)
        t = VE.do(lambda e: e.tensor_scalar(lams[:, 5:6], lams[:, 4:5], -LAMBDA_INIT, None, ALU.add), t)
        i_l, fr = take("side")
        t = PE.do(lambda e: e.matmul(banks[i_l][:, 0:1], ones[0:1, :], lams[0:1, 5:6], start=True, stop=True),
                  t, t_ones, fr)
        neglam = small[:, 28:29]
        t_lam = VE.do(lambda e: e.tensor_copy(neglam, banks[i_l][:, 0:1]), t)
        bank_free[i_l] = t_lam

        t = PO.do(lambda e: e.memset(chainm[:, :], 1.0))
        t_chain = PO.do(lambda e: e.memset(chainm[:, 0:HEADS * T:CH], 0.0), t)
        masks = maskf[:, :].bitcast(U32).rearrange("p (l t) -> p l t", l=len(LEVELS))
        t_masks = load(PO, "masks", masks[:, :, :], a["masks"].bitcast(U32))

        mark[AC], mark[VE] = len(AC.items), len(VE.items)
        norm_apply(hT, lambda k: scl[:, k:k + 1], lambda k: modc[:, k:k + 1], t_rstd, t_scl1, t_mod0)
        f0 = fence()

        def gated(name, stack, q, k, v, b, dv, escale, oT, ready, ztok, result):
            lev = [[sb(f"{name}_{x}{i}", [P, HEADS, T], stack=stack) for x in ("e", "q", "k")] for i in range(2)]
            A0 = sb(name + "_A0", [P, HEADS, T], stack=stack)
            A1 = sb(name + "_A1", [P, HEADS, P], stack=stack)
            bl = sb(name + "_bl", [P, HEADS, 1], stack=stack)
            NV = dv // P
            tA = [None, None]
            tz = PO.do(lambda e: e.memset(A0[:, :, 0:P], 0.0), ztok)
            tz = PO.do(lambda e: e.memset(A1[:, :, :], 0.0), tz)
            for i in range(2):
                PO.do(lambda e, i=i: e.memset(lev[i][1][:, :, :], 0.0), ztok)
                tz = PO.do(lambda e, i=i: e.memset(lev[i][2][:, :, :], 0.0), ztok)
            free = [tz, tz]

            def factors(li, m):
                E, Q, K = lev[li % 2]
                if m == 1:
                    return q, k, ready
                g = HEADS * T // m
                vw = lambda x: x[:, :, :].rearrange("p h (g m) -> p (h g) m", m=m)
                B, Ev, Qv, Kv = vw(b), vw(E), vw(Q), vw(K)
                qq, kk = vw(q), vw(k)
                half = m // 2
                fr = free[li % 2]
                if m <= P:
                    ref = B[:, :, half - 1:half].broadcast_to([P, g, half])
                    if m <= CH:
                        VE.do(lambda e: e.tensor_tensor(Ev[:, :, half:], B[:, :, half:], ref, ALU.subtract), ready, fr)
                    else:
                        VE.do(lambda e: e.tensor_copy(Ev[:, :, 64:], B[:, :, 64:]), ready, fr)
                    t = VE.do(lambda e: e.tensor_tensor(Ev[:, :, 0:half], ref, B[:, :, 0:half], ALU.subtract), ready, fr)
                else:
                    t0 = VE.do(lambda e: e.tensor_tensor(bl[:, :, :], b[:, :, 63:64], b[:, :, 127:128], ALU.add),
                               ready, fr)
                    VE.do(lambda e: e.tensor_copy(E[:, :, 128:192], b[:, :, 128:192]), ready, fr)
                    VE.do(lambda e: e.tensor_tensor(
                        E[:, :, 192:256], b[:, :, 192:256], b[:, :, 191:192].broadcast_to([P, HEADS, 64]),
                        ALU.add), ready, fr)
                    VE.do(lambda e: e.tensor_tensor(
                        E[:, :, 64:128], b[:, :, 127:128].broadcast_to([P, HEADS, 64]), b[:, :, 64:128],
                        ALU.subtract), ready, fr)
                    t = VE.do(lambda e: e.tensor_tensor(
                        E[:, :, 0:64], bl[:, :, :].broadcast_to([P, HEADS, 64]), b[:, :, 0:64],
                        ALU.subtract), t0, fr)
                t = AC.do(lambda e: e.activation(E[:, :, :], E[:, :, :], ACT.Exp, scale=escale), t)
                tk = PO.do(lambda e: e.tensor_tensor(
                    Kv[:, :, 0:half], kk[:, :, 0:half], Ev[:, :, 0:half], ALU.mult), t, fr, ready)
                tq = VE.do(lambda e: e.tensor_tensor(
                    Qv[:, :, half:], qq[:, :, half:], Ev[:, :, half:], ALU.mult), t, fr, ready)
                return Q, K, [tk, tq]

            every = LEVELS + [256]
            ahead = [factors(li, every[li]) for li in range(2)]
            yield
            for li, m in enumerate(every):
                Qs, Ks, tq = ahead.pop(0)
                tiles = [(0, 0), (1, 1)] if m <= P else [(0, 1)]
                done = []
                for si, ti in tiles:
                    i, fr = take("side")
                    for h in range(HEADS):
                        f = lambda e, i=i, h=h, si=si, ti=ti, Qs=Qs, Ks=Ks: e.matmul(
                            banks[i][:, h * P:(h + 1) * P], Ks[:, h, si * P:(si + 1) * P],
                            Qs[:, h, ti * P:(ti + 1) * P], start=True, stop=True)
                        t = (PE.do if h == HEADS - 1 else PE.quiet)(f, tq, fr)
                    ps = banks[i][:, :].rearrange("p (h t) -> p h t", h=HEADS)
                    if m > P:
                        t2 = VE.do(lambda e, ps=ps: e.tensor_copy(A0[:, :, P:T], ps), t, ztok)
                    else:
                        dst = A0[:, :, 0:P] if si == 0 else A1[:, :, :]
                        mk = masks[:, li:li + 1, :].broadcast_to([P, HEADS, P])
                        t2 = VE.do(lambda e, dst=dst, mk=mk, ps=ps: e.copy_predicated(dst, mk, ps), t, tz, t_masks,
                                   tA[si])
                        tA[si] = t2
                    bank_free[i] = t2
                    done.append(t)
                if m > 1:
                    free[li % 2] = done[-1]
                if li + 2 < len(every):
                    ahead.append(factors(li + 2, every[li + 2]))
                if m > 1:
                    yield
            tA = VE.last()
            for h in range(HEADS):
                for c0 in range(0, NV, 2):
                    n = min(2, NV - c0)
                    i, fr = take("side")
                    for c in range(n):
                        vs = lambda j, h=h, c=c, c0=c0: v[:, j, h * dv + (c0 + c) * P:h * dv + (c0 + c + 1) * P]
                        PE.quiet(lambda e, i=i, c=c, h=h, vs=vs: e.matmul(
                            banks[i][:, c * T:(c + 1) * T], vs(0), A0[:, h, :], start=True, stop=False,
                            skip_group_check=True), tA, fr)
                        t = PE.do(lambda e, i=i, c=c, h=h, vs=vs: e.matmul(
                            banks[i][:, c * T + P:(c + 1) * T], vs(1), A1[:, h, :], start=False, stop=True,
                            skip_group_check=True), tA, fr)
                    o = oT[:, h * NV + c0:h * NV + c0 + n, :]
                    t = AC.do(lambda e, i=i, o=o, n=n: e.activation(
                        o, banks[i][:, 0:n * T].rearrange("p (c t) -> p c t", c=n), ACT.Copy), t, ztok)
                    bank_free[i] = t
            yield
            sq = lev[0][0] if NV == 1 else None
            rs = lev[1][0]
            tr = []
            for h in range(HEADS):
                i, fr = take("side")
                sqh = lev[0][0][:, 0:NV, :]
                t1 = AC.do(lambda e, h=h, sqh=sqh: e.activation(sqh, oT[:, h * NV:(h + 1) * NV, :], ACT.Square),
                           AC.last(), PE.last())
                for c in range(NV):
                    f = lambda e, i=i, c=c: e.matmul(banks[i][:, 0:T], ones[:, :], lev[0][0][:, c, :],
                                                     start=c == 0, stop=c == NV - 1)
                    t = (PE.do if c == NV - 1 else PE.quiet)(f, t1, fr)
                t = AC.do(lambda e, i=i, h=h: e.activation(rs[:, h, :], banks[i][:, 0:T], ACT.Sqrt,
                                                           bias=epsc[:, 0:1], scale=1.0 / dv), t)
                bank_free[i] = t
                tr.append(VE.do(lambda e, h=h: e.reciprocal(rs[:, h, :], rs[:, h, :]), t))
            result.append((rs, tr))
            yield

        b1 = Region()
        hq = sb("hq", [P, HEADS, T], stack=b1)
        hk = sb("hk", [P, HEADS, T], stack=b1)
        hb = sb("hb", [P, HEADS, T], stack=b1)
        hv = sb("hv", [P, TT, 512], stack=b1)
        hf = sb("hf", [P, HEADS, T], stack=b1)
        hg = hf
        aq = sb("aq", [P, HEADS, T], stack=b1)
        ak = sb("ak", [P, HEADS, T], stack=b1)
        av = sb("av", [P, TT, 512], stack=b1)
        mixT = sb("mixT", [P, KC, T], stack=b1)
        distc = sb("distc", [P, 384], stack=b1)
        t_dist = load(PO, "dist", distc[:, :], a["dist"], f0)
        win = lambda i: a["w_in"][0][:, i * 512:(i + 1) * 512]
        project(win(1), copy_T(hf, func=ACT.Sigmoid, wait=f0))
        t = AC.last()
        for h in range(HEADS):
            t2 = VE.do(lambda e, h=h: e.tensor_scalar(hf[:, h, :], hf[:, h, :], oml[:, h:h + 1], lbc[:, h:h + 1],
                                                      ALU.mult, ALU.add), t, t_lb)
        t2 = VE.do(lambda e: e.tensor_scalar(hf[:, :, :], hf[:, :, :], 1e-18, None, ALU.max), t2)
        VE.do(lambda e: e.tensor_scalar(hk[:, :, :], hf[:, :, :], -1.0, 1.0, ALU.mult, ALU.add), t2, f0)
        t = AC.do(lambda e: e.activation(hf[:, :, :], hf[:, :, :], ACT.Ln), VE.last())
        t_hb = VE.do(lambda e: e.tensor_tensor_scan(
            hb[:, :, :].rearrange("p h t -> p (h t)"), chainm[:, :], hf[:, :, :].rearrange("p h t -> p (h t)"),
            0.0, ALU.mult, ALU.add), t, t_chain, f0)
        project(win(0), copy_T(hq, wait=f0))
        t_hready = [t_hb, AC.last()]
        hst = Region(b1.at)
        h_rs = []
        gen_h = gated("hg", hst, hq, hk, hv, hb, P, 1.0, mixT, t_hready, f0, h_rs)

        done_da = {}
        t_a = {}

        def keep(name, evac):
            def kept(*args):
                t_a[name] = evac(*args)
                return t_a[name]
            return kept

        def diff_attention():
            S = [[sb(f"S{i}{m}", [P, 384], stack=hst) for m in range(2)] for i in range(2)]
            W = [sb(f"W{i}", [P, 384], stack=hst) for i in range(2)]
            WT = [sb(f"WT{i}", [P, 384], stack=hst) for i in range(2)]
            st = sb("dstat", [P, HEADS, 12], stack=hst)
            t_in = [t_a["q"], t_a["k"]]
            span = [(0, P), (P, 384)]
            sfree, wfree, wtfree = [None, None], [None, None], [None, None]
            t_w, t_wt = {}, {}

            def scores(h):
                slope = 2.0 ** (-8.0 * (h + 1) / HEADS)
                Sh, Wh = S[h % 2], W[h % 2]
                for m in range(2):
                    i, fr = take("side")
                    for j in range(TT):
                        a0, a1 = span[j]
                        f = lambda e, i=i, m=m, j=j, a0=a0, a1=a1: e.matmul(
                            banks[i][:, a0:a1], aq[64 * m:64 * m + 64, h, j * P:(j + 1) * P],
                            ak[64 * m:64 * m + 64, h, 0:a1 - a0], start=True, stop=True)
                        t = (PE.do if j == 1 else PE.quiet)(f, t_in, fr)
                    t = VE.do(lambda e, i=i, m=m: e.scalar_tensor_tensor(
                        out=Sh[m][:, :], in0=distc[:, :], scalar=-slope, in1=banks[i][:, 0:384],
                        op0=ALU.mult, op1=ALU.add), t, t_dist, sfree[h % 2])
                    bank_free[i] = t
                    for j in range(TT):
                        a0, a1 = span[j]
                        tr = VE.do(lambda e, m=m, j=j, a0=a0, a1=a1: e.tensor_reduce(
                            st[:, h, 2 * m + j:2 * m + j + 1], Sh[m][:, a0:a1], AXX, ALU.max), t)
                t = VE.do(lambda e: e.tensor_scalar(st[:, h, 0:4], st[:, h, 0:4], -1.0, None, ALU.mult), tr)
                for m in range(2):
                    for j in range(TT):
                        a0, a1 = span[j]
                        c = 2 * m + j
                        te = AC.do(lambda e, m=m, c=c, a0=a0, a1=a1: e.activation(
                            Sh[m][:, a0:a1], Sh[m][:, a0:a1], ACT.Exp, bias=st[:, h, c:c + 1],
                            accum_out=st[:, h, 4 + c:5 + c]), t)
                t = VE.do(lambda e: e.reciprocal(st[:, h, 8:12], st[:, h, 4:8]), te)
                t = VE.do(lambda e: e.tensor_scalar(st[:, h, 10:12], st[:, h, 10:12], neglam, None, ALU.mult),
                          t, t_lam)
                for j in range(TT):
                    a0, a1 = span[j]
                    t1 = VE.do(lambda e, j=j, a0=a0, a1=a1: e.tensor_scalar(
                        Wh[:, a0:a1], Sh[0][:, a0:a1], st[:, h, 8 + j:9 + j], None, ALU.mult), t, wfree[h % 2])
                    t1 = VE.do(lambda e, j=j, a0=a0, a1=a1: e.scalar_tensor_tensor(
                        out=Wh[:, a0:a1], in0=Sh[1][:, a0:a1], scalar=st[:, h, 10 + j:11 + j], in1=Wh[:, a0:a1],
                        op0=ALU.mult, op1=ALU.add), t1)
                sfree[h % 2] = t_w[h] = t1

            def turned(h):
                i, fr = take("side")
                for c in range(3):
                    f = lambda e, c=c: e.transpose(banks[i][:, c * P:(c + 1) * P], W[h % 2][:, c * P:(c + 1) * P],
                                                   ident[:, :])
                    t = (PE.do if c == 2 else PE.quiet)(f, t_w[h], fr)
                wfree[h % 2] = t
                t_wt[h] = AC.do(lambda e: e.activation(WT[h % 2][:, :], banks[i][:, 0:384], ACT.Copy), t,
                                wtfree[h % 2])
                bank_free[i] = t_wt[h]

            def values(h):
                i, fr = take("side")
                PE.quiet(lambda e: e.matmul(
                    banks[i][:, 0:T], av[:, 0, h * P:(h + 1) * P], WT[h % 2][:, 0:T], start=True, stop=False,
                    skip_group_check=True), t_wt[h], fr, t_a["v"])
                t = PE.do(lambda e: e.matmul(
                    banks[i][:, P:T], av[:, 1, h * P:(h + 1) * P], WT[h % 2][:, T:384], start=False, stop=True,
                    skip_group_check=True))
                wtfree[h % 2] = t
                bank_free[i] = AC.do(lambda e: e.activation(mixT[:, 4 + h, :], banks[i][:, 0:T], ACT.Copy), t, f0)

            for step in range(HEADS + 2):
                if step >= 2:
                    values(step - 2)
                if 1 <= step <= HEADS:
                    turned(step - 1)
                if step < HEADS:
                    scores(step)
                yield
            t = AC.last()
            t = AC.do(lambda e: e.activation(aq[:, :, :], mixT[:, 4:8, :], ACT.Square), t, PE.last())
            yield
            subs = small[:, 29:30]
            t2 = VE.do(lambda e: e.tensor_scalar(subs, col("subln"), 1.0 - LAMBDA_INIT, None, ALU.mult))
            for h in range(HEADS):
                i, fr = take("side")
                t1 = PE.do(lambda e, i=i, h=h: e.matmul(banks[i][:, 0:T], ones[:, :], aq[:, h, :],
                                                        start=True, stop=True), t, fr)
                t1 = AC.do(lambda e, i=i, h=h: e.activation(ak[:, h, :], banks[i][:, 0:T], ACT.Sqrt,
                                                            bias=epsc[:, 0:1], scale=1.0 / P), t1)
                bank_free[i] = t1
                t1 = VE.do(lambda e, h=h: e.reciprocal(ak[:, h, :], ak[:, h, :]), t1)
                done_da[h] = VE.do(lambda e, h=h: e.scalar_tensor_tensor(
                    out=mixT[:, 4 + h, :], in0=mixT[:, 4 + h, :], scalar=subs, in1=ak[:, h, :],
                    op0=ALU.mult, op1=ALU.mult), t1, t2)
            yield

        res_tok = {}
        hold = []

        def out_of_hgrn():
            rs, tr = h_rs[0]
            for h in range(HEADS):
                t = VE.do(lambda e, h=h: e.scalar_tensor_tensor(
                    out=mixT[:, h, :], in0=mixT[:, h, :], scalar=col("gn"), in1=rs[:, h, :],
                    op0=ALU.mult, op1=ALU.mult), tr[h])
                t = VE.do(lambda e, h=h: e.tensor_tensor(mixT[:, h, :], mixT[:, h, :], hg[:, h, :], ALU.mult), t,
                          t_a["g"])
                split_x(h, mixT[:, h, :], t)
            yield from steps(a["w_out"][0][0:512, :], None, kc=4, cols=D, parts=2, part=0, hold=hold)

        weave([steps(win(4), keep("q", copy_T(aq, scale=0.125, wait=f0))),
               steps(win(5), keep("k", copy_T(ak, wait=f0))),
               steps(win(6), keep("v", copy_tok(av, 0, f0)), tok=True),
               steps(win(2), copy_tok(hv, 0, f0), tok=True),
               steps(win(3), keep("g", copy_T(hg, func=ACT.Silu, wait=t_hb))),
               out_of_hgrn()],
              (-1, gen_h), (0, modulations(range(4, 10))), (5, diff_attention()))
        t_mod = VE.last()
        t_scl2 = VE.do(lambda e: e.scalar_tensor_tensor(
            out=scl[:, 8:16], in0=modc[:, 32:40], scalar=1.0, in1=pcol[:, ROWS["norm2"]:ROWS["norm2"] + 8],
            op0=ALU.add, op1=ALU.mult), t_mod)

        def residual(gate, base):
            def evac(bk, ch, n, t):
                for c in range(n):
                    k = base + ch + c
                    t2 = VE.do(lambda e, bk=bk, c=c, k=k: e.scalar_tensor_tensor(
                        out=hT[:, k, :], in0=banks[bk][:, c * T:(c + 1) * T], scalar=modc[:, gate + k:gate + k + 1],
                        in1=hT[:, k, :], op0=ALU.mult, op1=ALU.add), t, t_mod)
                    res_tok[k] = t2
                return t2
            return evac

        for k in range(4, KC):
            split_x(k, mixT[:, k, :], done_da[k - 4])
        project(a["w_out"][0][512:D, :], residual(16, 0), kc=4, cols=D, parts=2, part=1, hold=hold, xo=4)
        t_rstd = norm_scale(hT, [res_tok[k] for k in range(KC)])
        norm_apply(hT, lambda k: scl[:, 8 + k:9 + k], lambda k: modc[:, 24 + k:25 + k], t_rstd, t_scl2)
        f1 = fence()

        b2 = Region()
        hid = sb("hid", [P, FFC, T], stack=b2)
        t_hid = {}
        t_g = {}

        def evac_up(c0):
            def evac(bk, ch, m, t):
                o = hid[:, c0 // P + ch:c0 // P + ch + m, :]
                t = VE.do(lambda e: e.tensor_tensor(
                    o, banks[bk][:, 0:m * T].rearrange("p (c t) -> p c t", c=m), o, ALU.mult), t, t_g[c0])
                for x in range(m):
                    t_hid[c0 // P + ch + x] = t
                return t
            return evac

        def gate_up():
            for c0 in range(0, FF, 512):
                n = min(512, FF - c0)
                yield from steps(a["w_ffn_gate"][0][:, c0:c0 + n], copy_T(hid, c0 // P, func=ACT.Silu, wait=f1), cols=n)
                t_g[c0] = AC.last()
                yield from steps(a["w_ffn_up"][0][:, c0:c0 + n], evac_up(c0), cols=n)

        weave([gate_up()], (4, modulations(range(10, 12))))
        t_mod = VE.last()
        hold = [[], []]
        for part, (k0, kn) in enumerate([(0, 8), (8, 8), (16, 6)]):
            for k in range(kn):
                split_x(k, hid[:, k0 + k, :], t_hid[k0 + k])
            for c in range(2):
                project(a["w_ffn_down"][0][k0 * P:(k0 + kn) * P, c * 512:(c + 1) * 512], residual(40, 4 * c), kc=kn,
                        parts=3, part=part, hold=hold[c])
        sq2 = sb("sq2", [P, KC, T], stack=b2)
        r1 = sb("r1", [P, T], stack=b2)
        t_wm = VE.do(lambda e: e.tensor_tensor(wmix[:, :], pcol[:, ROWS["fin1"]:ROWS["fin1"] + 8],
                                               pcol[:, ROWS["mixn"]:ROWS["mixn"] + 8], ALU.mult))
        (i1, i2), t = sums(hT, [scratch, sq2], [res_tok[k] for k in range(KC)], (None, lambda k: col("fin1", k)))
        t0 = AC.do(lambda e, i1=i1: e.activation(r1[:, :], banks[i1][:, 0:T], ACT.Copy, scale=EPS), t)
        t2 = VE.do(lambda e, i2=i2: e.tensor_tensor(rstd[:, :], banks[i2][:, 0:T], r1[:, :], ALU.add), t0)
        t = AC.do(lambda e: e.activation(rstd[:, :], rstd[:, :], ACT.Sqrt, bias=eps2[:, 0:1], scale=1.0 / D), t2)
        bank_free[i2] = t2
        t = VE.do(lambda e: e.reciprocal(rstd[:, :], rstd[:, :]), t)
        t_u = {}
        for k in range(KC + 2):
            if k < KC:
                t_u[k] = VE.do(lambda e, k=k: e.scalar_tensor_tensor(
                    out=scratch[:, k, :], in0=hT[:, k, :], scalar=wmix[:, k:k + 1], in1=rstd[:, :],
                    op0=ALU.mult, op1=ALU.mult), t, t_wm)
            if k >= 2:
                split_x(k - 2, scratch[:, k - 2, :], t_u[k - 2])
        t = AC.do(lambda e, i1=i1: e.activation(r1[:, :], banks[i1][:, 0:T], ACT.Sqrt, bias=epsc[:, 0:1],
                                                scale=1.0 / D), t0, t2)
        bank_free[i1] = t
        t = VE.do(lambda e: e.reciprocal(r1[:, :], r1[:, :]), t)
        for k in range(KC):
            t_h = VE.do(lambda e, k=k: e.scalar_tensor_tensor(
                out=hT[:, k, :], in0=hT[:, k, :], scalar=col("fin1", k), in1=r1[:, :],
                op0=ALU.mult, op1=ALU.mult), t, t_u[k])
        f2 = fence()

        outer = Region()
        w2 = a["w_in_2"][0]
        rq = sb("rq", [P, 8, T], stack=outer)
        rk = sb("rk", [P, 8, T], stack=outer)
        rv = sb("rv", [P, TT, 2048], stack=outer)
        oG = sb("oG", [P, 8, T], stack=outer)
        b3 = Region(outer.at)
        gq = sb("gq", [P, HEADS, T], stack=b3)
        gk = sb("gk", [P, HEADS, T], stack=b3)
        gb = sb("gb", [P, HEADS, T], stack=b3)
        gv = sb("gv", [P, TT, 1024], stack=b3)
        gd = sb("gd", [16, T], stack=b3)
        gup = sb("gup", [16, 512], stack=b3)
        z = oG[:, 0:4, :]
        t_gup = load(PO, "gup", gup[:, :], a["gla_gk_up_2"][0], f2)

        def evac_gd(bk, ch, n, t):
            return AC.do(lambda e: e.activation(gd[:, :], banks[bk][0:16, 0:T], ACT.Copy), t, f2)
        project(w2[:, 3072:3200], evac_gd, cols=P)
        t = AC.last()
        t_gd = t
        project(w2[:, 0:512], copy_T(gq, scale=float(P) ** -0.5, wait=f2))
        gbf = [None] * 2
        for hh in range(2):
            i, fr = take("side")
            for c in range(2):
                h = 2 * hh + c
                t = PE.do(lambda e, i=i, c=c, h=h: e.matmul(banks[i][:, c * T:(c + 1) * T],
                                                            gup[:, h * P:(h + 1) * P], gd[:, :], start=True,
                                                            stop=True), t_gd, t_gup, fr)
            for c in range(2):
                h = 2 * hh + c
                t2 = AC.do(lambda e, i=i, c=c, h=h: e.activation(z[:, h, :], banks[i][:, c * T:(c + 1) * T],
                                                                 ACT.Identity, bias=col("gkb", h)), t, f2)
            bank_free[i] = t2
        t = AC.do(lambda e: e.activation(gb[:, :, :], z[:, :, :], ACT.Abs), t2, f2)
        t = AC.do(lambda e: e.activation(gb[:, :, :], gb[:, :, :], ACT.Exp, scale=-1.0), t)
        t = AC.do(lambda e: e.activation(gb[:, :, :], gb[:, :, :], ACT.Ln, bias=ones[:, 0:1]), t)
        t = VE.do(lambda e: e.scalar_tensor_tensor(out=z[:, :, :], in0=z[:, :, :], scalar=0.0, in1=gb[:, :, :],
                                                   op0=ALU.min, op1=ALU.subtract), t)
        t_gb = VE.do(lambda e: e.tensor_tensor_scan(
            gb[:, :, :].rearrange("p h t -> p (h t)"), chainm[:, :], z[:, :, :].rearrange("p h t -> p (h t)"),
            0.0, ALU.mult, ALU.add), t)
        project(w2[:, 512:1024], copy_T(gk, wait=f2))
        t_gready = [t_gb, AC.last()]
        gst = Region(b3.at)
        g_rs = []
        gen_g = gated("gl", gst, gq, gk, gv, gb, 256, 1.0 / 16.0, oG, t_gready, f2, g_rs)
        GG, RQ, RK, RV, RG, MA, MB = 2048, 3088, 4112, 5136, 7184, 9232, 10256
        weave([steps(w2[:, 1024 + c * 512:1536 + c * 512], copy_tok(gv, c * 512, f2), tok=True) for c in range(2)]
              + [steps(w2[:, RQ + c * 512:RQ + (c + 1) * 512], copy_T(rq, 4 * c, wait=f2), step=2)
                 for c in range(2)]
              + [steps(w2[:, RK + c * 512:RK + (c + 1) * 512],
                         copy_T(rk, 4 * c, scale=1.0 / 16.0, wait=f2), step=2) for c in range(2)],
              (-1, gen_g))
        rs, t = g_rs[0]
        for c in range(2):
            t = VE.do(lambda e, c=c: e.scalar_tensor_tensor(
                out=oG[:, c::2, :], in0=oG[:, c::2, :], scalar=col("glan", c), in1=rs[:, :, :],
                op0=ALU.mult, op1=ALU.mult), t)
        t_oGn = t
        fg = fence()

        merged = sb("merged", [P, KC, T], stack=Region(ARENA - KC * T))
        mgb = sb("mgb", [P, KC, T], stack=Region(KC * T))
        xtok2 = sb("xtok2", [P, TT, D], stack=Region())
        b4 = Region(outer.at)
        oR = sb("oR", [P, 16, T], stack=b4)
        gtmp = [sb(f"gtmp{i}", [P, 512], stack=b4)[:, :] for i in range(2)]
        tmpfree = [fg, fg]
        rot = [sb(f"rot{i}", [P, HEADS, T], stack=b4) for i in range(2)]
        cosT = sb("cosT", [P, T], stack=b4)
        sinT = sb("sinT", [P, T], stack=b4)
        posi = sb("posi", [P, T], I32, stack=b4)
        mean = [sb(f"mean{i}", [P, T], stack=Region(b4.at - T + i * T)) for i in range(2)]
        ang = sb("ang", [P, T], stack=b4)
        dec = sb("dec", [P, HEADS, 384], stack=b4)
        AT = [sb(f"ret_A{i}", [P, 384], stack=b4) for i in range(2)]
        theta = sb("theta", [P, 1], stack=b4)
        assert b4.at <= ARENA - KC * T
        t_pos = load(PO, "pos", posi[:, :], a["positions_2"].partition_broadcast(P).rearrange("p o t -> p (o t)"), fg)
        t_th = load(PO, "theta", theta[:, :], a["theta"], fg)
        t_dec = load(PO, "dec", dec[:, :, :], a["decay"], fg)
        t_rot = []

        def rotate():
            t = VE.do(lambda e: e.tensor_copy(ang[:, :], posi[:, :]), t_pos, fg)
            t_ang = VE.do(lambda e: e.tensor_scalar(ang[:, :], ang[:, :], theta[:, 0:1], None, ALU.mult), t, t_th)
            MAGIC = 12582912.0
            for dst, shift in ((sinT, 0.0), (cosT, 0.25)):
                kt = rot[0][:, 0, :]
                t = VE.do(lambda e, kt=kt, shift=shift: e.tensor_scalar(
                    kt, ang[:, :], float(1.0 / (2 * np.pi)), shift, ALU.mult, ALU.add), t_ang, t, fg)
                t = VE.do(lambda e, kt=kt: e.tensor_scalar(kt, kt, MAGIC, None, ALU.add), t)
                t = VE.do(lambda e, kt=kt: e.tensor_scalar(kt, kt, -MAGIC, None, ALU.add), t)
                src = ang
                yield
                for part in TWO_PI_PARTS:
                    t = VE.do(lambda e, kt=kt, part=part, src=src, dst=dst: e.scalar_tensor_tensor(
                        out=dst[:, :], in0=kt, scalar=-part, in1=src[:, :], op0=ALU.mult, op1=ALU.add), t)
                    src = dst
                t = VE.do(lambda e, dst=dst, shift=shift: e.tensor_scalar(
                    dst[:, :], dst[:, :], float(2 * np.pi * shift), None, ALU.add), t)
                t = VE.do(lambda e, dst=dst: e.tensor_scalar(
                    dst[:, :], dst[:, :], 3.1415925, -3.1415925, ALU.min, ALU.max), t)
                t = AC.do(lambda e, dst=dst: e.activation(dst[:, :], dst[:, :], ACT.Sin), t)
                yield
            t_cs = t
            cb = cosT[:, :].unsqueeze(1).broadcast_to([P, HEADS, T])
            sbb = sinT[:, :].unsqueeze(1).broadcast_to([P, HEADS, T])
            tr = None
            for x in (rq, rk):
                ev, od = x[:, 0::2, :], x[:, 1::2, :]
                t1 = VE.do(lambda e, ev=ev: e.tensor_tensor(rot[0][:, :, :], ev, sbb, ALU.mult), t_cs, VE.last())
                t2 = PO.do(lambda e, od=od: e.tensor_tensor(rot[1][:, :, :], od, sbb, ALU.mult), t_cs, tr, fg)
                t3 = VE.do(lambda e, ev=ev: e.tensor_tensor(ev, ev, cb, ALU.mult), t1, fg)
                yield
                t4 = VE.do(lambda e, od=od: e.tensor_tensor(od, od, cb, ALU.mult), t2)
                VE.do(lambda e, ev=ev: e.tensor_tensor(ev, ev, rot[1][:, :, :], ALU.subtract), t3, t2)
                tr = VE.do(lambda e, od=od: e.tensor_tensor(od, od, rot[0][:, :, :], ALU.add), t4, t1)
                yield
            t_rot.append(tr)

        rdone = {}

        def retention(lane):
            A, mn, sq = AT[lane], mean[lane], rot[lane]
            afree = None
            for h in range(lane, HEADS, 2):
                i, fr = take("side")
                for c in range(2):
                    PE.quiet(lambda e, i=i, c=c, h=h: e.matmul(
                        banks[i][:, 0:T], rk[:, 2 * h + c, 0:P], rq[:, 2 * h + c, :], start=c == 0, stop=c == 1),
                        t_rot, fr)
                for c in range(2):
                    t = (PE.do if c else PE.quiet)(lambda e, i=i, c=c, h=h: e.matmul(
                        banks[i][:, T:384], rk[:, 2 * h + c, P:T], rq[:, 2 * h + c, P:T], start=c == 0, stop=c == 1))
                t = VE.do(lambda e, i=i, h=h: e.tensor_tensor(A[:, :], banks[i][:, 0:384], dec[:, h, :], ALU.mult),
                          t, t_dec, afree)
                bank_free[i] = t
                yield
                for c0 in range(0, 4, 2):
                    i, fr = take("side")
                    for c in range(2):
                        vc = slice(h * 512 + (c0 + c) * P, h * 512 + (c0 + c + 1) * P)
                        PE.quiet(lambda e, i=i, c=c, vc=vc: e.matmul(
                            banks[i][:, c * T:(c + 1) * T], rv[:, 0, vc], A[:, 0:T], start=True, stop=False,
                            skip_group_check=True), t, fr, t_rv[h])
                        t2 = PE.do(lambda e, i=i, c=c, vc=vc: e.matmul(
                            banks[i][:, c * T + P:(c + 1) * T], rv[:, 1, vc], A[:, T:384], start=False, stop=True,
                            skip_group_check=True))
                    afree = t2
                    t2 = AC.do(lambda e, i=i, c0=c0, h=h: e.activation(
                        oR[:, 4 * h + c0:4 * h + c0 + 2, :], banks[i][:, :].rearrange("p (c t) -> p c t", c=2),
                        ACT.Copy), t2, fg)
                    bank_free[i] = t2
                yield
                o = oR[:, 4 * h:4 * h + 4, :]
                i, fr = take("side")
                for c in range(4):
                    t = (PE.do if c == 3 else PE.quiet)(lambda e, i=i, c=c, h=h: e.matmul(
                        banks[i][:, 0:T], ones[:, :], oR[:, 4 * h + c, :], start=c == 0, stop=c == 3), t2, fr)
                t = AC.do(lambda e, i=i: e.activation(mn[:, :], banks[i][:, 0:T], ACT.Copy, scale=1.0 / 512), t,
                          t_rot, rdone.get(h - 2))
                bank_free[i] = t
                t = VE.do(lambda e, o=o: e.tensor_tensor(
                    o, o, mn[:, :].unsqueeze(1).broadcast_to([P, 4, T]), ALU.subtract), t)
                t2 = AC.do(lambda e, o=o: e.activation(sq[:, :, :], o, ACT.Square), t, t_rot, PE.last())
                yield
                i, fr = take("side")
                for c in range(4):
                    t = (PE.do if c == 3 else PE.quiet)(lambda e, i=i, c=c: e.matmul(
                        banks[i][:, 0:T], ones[:, :], sq[:, c, :], start=c == 0, stop=c == 3), t2, fr)
                t = AC.do(lambda e, i=i: e.activation(mn[:, :], banks[i][:, 0:T], ACT.Sqrt, bias=epsc[:, 0:1],
                                                      scale=1.0 / 512), t)
                bank_free[i] = t
                t = VE.do(lambda e: e.reciprocal(mn[:, :], mn[:, :]), t)
                for c in range(4):
                    t2 = VE.do(lambda e, c=c, h=h: e.scalar_tensor_tensor(
                        out=oR[:, 4 * h + c, :], in0=oR[:, 4 * h + c, :], scalar=col("retn", 4 * h + c),
                        in1=mn[:, :], op0=ALU.mult, op1=ALU.mult), t)
                rdone[h] = t2
                yield

        def evac_gate(dst, base, t_in, func, done):
            def evac(bk, ch, n, t):
                j = (ch // 2) % 2
                t = AC.do(lambda e: e.activation(gtmp[j], banks[bk][:, 0:n * T], func), t, tmpfree[j])
                o = dst[:, base + ch:base + ch + n, :]
                tmpfree[j] = VE.do(lambda e: e.tensor_tensor(o, o, gtmp[j].rearrange("p (c t) -> p c t", c=n),
                                                             ALU.mult), t, t_in)
                for x in range(n):
                    done[base + ch + x] = tmpfree[j]
                return t
            return evac

        t_rv, t_oG, t_mga, t_ya = {}, {}, {}, {}

        def evac_rv(c):
            def evac(bk, j, t):
                t_rv[c] = VE.do(lambda e: e.tensor_copy(rv[:, j, c * 512:(c + 1) * 512], banks[bk][:, :]), t, f2)
                return t_rv[c]
            return evac

        def evac_ya(base):
            def evac(bk, ch, n, t):
                o = merged[:, base + ch:base + ch + n, :]
                return VE.do(lambda e: e.tensor_tensor(o, banks[bk][:, 0:n * T].rearrange("p (c t) -> p c t", c=n),
                                                       o, ALU.mult), t, t_mga[0])
            return evac

        def gate_a():
            for c in range(2):
                yield from steps(w2[:, MA + c * 512:MA + (c + 1) * 512],
                                   copy_T(merged, 4 * c, func=ACT.Sigmoid, wait=fg))
            t_mga[0] = AC.last()

        weave([steps(w2[:, RV + c * 512:RV + (c + 1) * 512], evac_rv(c), tok=True) for c in range(4)]
              + [steps(w2[:, GG + c * 512:GG + (c + 1) * 512], evac_gate(oG, 4 * c, t_oGn, ACT.Silu, t_oG))
                 for c in range(2)]
              + [gate_a()],
              (-1, rotate()), (7, retention(0)), (8, retention(1)))
        f3 = fence()
        t_oR = {}
        for c in range(2):
            project(w2[:, MB + c * 512:MB + (c + 1) * 512], copy_T(mgb, 4 * c, func=ACT.Sigmoid, wait=f3))
        t_mgb = AC.last()
        for c in range(4):
            project(w2[:, RG + c * 512:RG + (c + 1) * 512], evac_gate(oR, 4 * c, rdone[c], ACT.Silu, t_oR))
        for k in range(KC):
            split_x(k, oG[:, k, :], t_oG[k])
        for c in range(2):
            project(a["w_branch_gla_2"][0][:, c * 512:(c + 1) * 512], evac_ya(4 * c))
        t_merged = {}
        def evac_yb(base):
            def evac(bk, ch, n, t):
                o = merged[:, base + ch:base + ch + n, :]
                g = mgb[:, base + ch:base + ch + n, :]
                t = VE.do(lambda e: e.tensor_tensor(g, banks[bk][:, 0:n * T].rearrange("p (c t) -> p c t", c=n),
                                                    g, ALU.mult), t, t_mgb)
                t2 = VE.do(lambda e: e.tensor_tensor(o, o, g, ALU.add), t)
                for x in range(n):
                    t_merged[base + ch + x] = t2
                return t
            return evac
        t_x2 = to_tokens(hT, xtok2, t_h, f3)
        hold = [[], []]
        for part in range(2):
            for k in range(KC):
                split_x(k, oR[:, 8 * part + k, :], t_oR[8 * part + k])
            for c in range(2):
                project(a["w_branch_ret_2"][0][part * D:(part + 1) * D, c * 512:(c + 1) * 512], evac_yb(4 * c),
                        parts=2, part=part, hold=hold[c])
        for k in range(KC):
            split_x(k, merged[:, k, :], t_merged[k])

        b5 = Region(4096)
        rw = sb("rw", [P, KC, 36], stack=b5)
        rb = sb("rb", [P, 36], stack=b5)
        wrow = sb("wrow", [P, D], stack=b5)
        frow = sb("frow", [P, D], stack=b5)
        tri = sb("tri", [P, P], stack=b5)
        iota = sb("iota", [P, CAP], stack=b5)
        assert b5.at <= 8192
        t_rw = [load(PO, f"rw{g}", rw[:, :, 4 + 8 * g:12 + 8 * g], a["router_expert_w_2"][0, g].rearrange(
            "(k p) e -> p k e", p=P), f3) for g in range(NGRP)]
        t_rw.append(load(PO, "rwg", rw[:, :, 0:4], a["router_group_w_2"][0].rearrange("(k p) e -> p k e", p=P), f3))
        t_rb = [load(PO, "rbg", rb[:, 0:4], a["router_group_b_2"].partition_broadcast(P).rearrange("p o e -> p (o e)"), f3),
                load(PO, "rbe", rb[:, 4:36], a["router_expert_b_2"].rearrange("o g e -> o (g e)").partition_broadcast(
                    P).rearrange("p o e -> p (o e)"), f3)]
        t_wr = load(PO, "wrow", wrow[:, :], a["norm_ffn_w_2"].partition_broadcast(P).rearrange("p o e -> p (o e)"), f3)
        t_fr = load(PO, "frow", frow[:, :], a["norm_final_w_2"].rearrange("(o e) -> o e", o=1).partition_broadcast(
            P).rearrange("p o e -> p (o e)"), f3)
        t_tri = load(PO, "tri", tri[:, :], a["tri"], f3)
        t_io = load(PO, "iota", iota[:, :], a["iota"], f3)

        f4 = fence()
        utok = sb("utok", [P, TT, D], stack=b5)
        lg = sb("lg", [P, TT, 36], stack=b5)
        ss = sb("ss", [P, 8], stack=b5)
        for n in range(2):
            ring.insert(2 + n, Slot(f"weights{RING + n}", sb(f"weights{RING + n}", [P, KC * 512],
                                                         stack=Region(ARENA - (3 - n) * KC * 512)), f4))

        def evac_res(c):
            def evac(bk, j, t):
                o = xtok2[:, j, c * 512:(c + 1) * 512]
                t = VE.do(lambda e: e.tensor_tensor(o, banks[bk][:, :], o, ALU.add), t, t_x2)
                t_ss[2 * j + c] = AC.do(lambda e: e.activation(
                    utok[:, j, c * 512:(c + 1) * 512], o, ACT.Square, accum_out=ss[:, 2 * j + c:2 * j + c + 1]), t, f4)
                return t
            return evac
        t_ss = {}
        for c in range(2):
            project(a["w_out_2"][0][:, c * 512:(c + 1) * 512], evac_res(c), tok=True)
        f5 = fence()
        ring.append(Slot(f"weights{RING + 2}", sb(f"weights{RING + 2}", [P, KC * 512],
                                                  stack=Region(ARENA - KC * 512)), f5))
        halves.close()
        yo = [sb(f"yo{i}", [P, D]) for i in range(2)]
        for n in range(3, 5):
            ring.append(Slot(f"weights{RING + n}", sb(f"weights{RING + n}", [P, KC * 512]), f5))
        uTe = hT
        for j in range(TT):
            sj = ss[:, 4 + j:5 + j]
            t = VE.do(lambda e, j=j, sj=sj: e.tensor_tensor(sj, ss[:, 2 * j:2 * j + 1], ss[:, 2 * j + 1:2 * j + 2],
                                                            ALU.add), t_ss[2 * j], t_ss[2 * j + 1])
            t = AC.do(lambda e, sj=sj: e.activation(sj, sj, ACT.Sqrt, bias=epsc[:, 0:1], scale=1.0 / D), t)
            t = VE.do(lambda e, sj=sj: e.reciprocal(sj, sj), t)
            for half in range(2):
                c = slice(half * 512, (half + 1) * 512)
                t2 = VE.do(lambda e, j=j, sj=sj, c=c: e.scalar_tensor_tensor(
                    out=utok[:, j, c], in0=xtok2[:, j, c], scalar=sj, in1=wrow[:, c],
                    op0=ALU.mult, op1=ALU.mult), t, t_wr)
                i, fr = take("side")
                for k in range(4):
                    f = lambda e, i=i, j=j, k=k, half=half: e.transpose(
                        banks[i][:, k * P:(k + 1) * P], utok[:, j, (4 * half + k) * P:(4 * half + k + 1) * P],
                        ident[:, :])
                    t3 = (PE.do if k == 3 else PE.quiet)(f, t2, fr)
                t3 = AC.do(lambda e, i=i, j=j, half=half: e.activation(
                    uTe[:, 4 * half:4 * half + 4, j * P:(j + 1) * P],
                    banks[i][:, :].rearrange("p (k t) -> p k t", k=4), ACT.Copy), t3)
                bank_free[i] = t3
            i, fr = take("side")
            for k in range(KC):
                f = lambda e, i=i, j=j, k=k: e.matmul(banks[i][:, 0:36], uTe[:, k, j * P:(j + 1) * P], rw[:, k, :],
                                                      start=k == 0, stop=k == KC - 1)
                t3 = (PE.do if k == KC - 1 else PE.quiet)(f, t3, t_rw, fr)
            t = VE.do(lambda e, i=i, j=j: e.tensor_tensor(lg[:, j, :], banks[i][:, 0:36], rb[:, :], ALU.add), t3, t_rb)
            bank_free[i] = t
        t_utok = t2

        rt = sb("rt", [P, TT, 96], stack=b5)
        R = lambda x, n: rt[:, :, x:x + n]

        def first_max(src, n, onehot, mxo, tmp, after):
            t = VE.do(lambda e: e.tensor_reduce(mxo, src, AXX, ALU.max), after)
            t = VE.do(lambda e: e.tensor_tensor(onehot, src, mxo.broadcast_to([P, TT, n]), ALU.is_lt), t)
            t = VE.do(lambda e: e.scalar_tensor_tensor(
                out=onehot, in0=onehot, scalar=1000.0, in1=iota[:, 0:n].unsqueeze(1).broadcast_to([P, TT, n]),
                op0=ALU.mult, op1=ALU.add), t, t_io)
            t = VE.do(lambda e: e.tensor_reduce(tmp, onehot, AXX, ALU.min), t)
            return VE.do(lambda e: e.tensor_tensor(onehot, onehot, tmp.broadcast_to([P, TT, n]), ALU.is_equal), t)

        gmax, goh, tmp1, eg, gsum = R(0, 1), R(1, 4), R(5, 1), R(6, 4), R(10, 1)
        el, m1, oh1, m2, oh2 = R(11, 8), R(19, 1), R(20, 8), R(28, 1), R(29, 8)
        e2, w12, el2, sel = R(37, 1), R(38, 2), R(40, 8), R(48, 32)
        two = 2 * TT
        d12 = sb("d12", [P, TT, 2, NE], stack=b5)
        wpT = [sb(f"wpT{i}", [P, T], stack=b5) for i in range(2)]
        early = Region(b5.at - 2 * T)
        dpos = sb("dpos", [P, TT, 2, NE], stack=early)
        pair = sb("pair", [P, two, NPAIR], stack=b5)
        wpair = sb("wpair", [P, two, NPAIR], stack=b5)
        par = sb("par", [P, two, 2], stack=b5)
        place = sb("place", [P, two, 1], stack=b5)
        ph = sb("ph", [P, two, CAP], stack=early)
        inpair = sb("inpair", [P, two, 2, CAP], stack=b5)
        pos = sb("pos", [P, TT, NE], stack=b5)
        isover = sb("isover", [P, TT, NE], stack=b5)
        wov = sb("wov", [P, TT, NE], stack=b5)
        over = sb("over", [P, 4], stack=b5)
        wcol = sb("wcol", [P, TT, 1], stack=b5)
        gl = lg[:, :, 0:4]
        t_g = first_max(gl, 4, goh, gmax, tmp1, t)
        eo = lg[:, :, 4:36].rearrange("p j (g x) -> p j g x", g=NGRP)
        t = VE.do(lambda e: e.tensor_tensor(dpos[:, :, 0, :].rearrange("p j (g x) -> p j g x", g=NGRP), eo,
                                            goh.unsqueeze(3).broadcast_to([P, TT, NGRP, EPG]), ALU.mult), t_g)
        t = VE.do(lambda e: e.tensor_reduce(el.unsqueeze(3), dpos[:, :, 0, :].rearrange("p j (g x) -> p j x g", g=NGRP),
                                            AXX, ALU.add), t)
        t = first_max(el, 8, oh1, m1, tmp1, t)
        t = VE.do(lambda e: e.scalar_tensor_tensor(out=el2, in0=oh1, scalar=-3.0e38, in1=el,
                                                   op0=ALU.mult, op1=ALU.add), t)
        t = first_max(el2, 8, oh2, m2, tmp1, t)
        for r, oh in enumerate((oh1, oh2)):
            t = VE.do(lambda e, r=r, oh=oh: e.tensor_tensor(
                d12[:, :, r, :].rearrange("p j (g x) -> p j g x", g=NGRP),
                oh.unsqueeze(2).broadcast_to([P, TT, NGRP, EPG]),
                goh.unsqueeze(3).broadcast_to([P, TT, NGRP, EPG]), ALU.mult), t)
        t = VE.do(lambda e: e.tensor_tensor(sel, d12[:, :, 0, :], d12[:, :, 1, :], ALU.add), t)
        i, fr = take("side")
        PE.quiet(lambda e, i=i: e.matmul(banks[i][:, 0:2 * NE], tri[:, :], sel, start=True, stop=False,
                                         skip_group_check=True), t, t_tri, fr)
        t1 = PE.do(lambda e, i=i: e.matmul(banks[i][:, NE:2 * NE], ones[:, :], sel[:, 0, :], start=False, stop=True,
                                           skip_group_check=True))
        dv = d12[:, :, :, :].rearrange("p j r e -> p (j r) e")
        VE.do(lambda e: e.tensor_reduce(pair[:, :, :].unsqueeze(3), dv.rearrange("p a (q b) -> p a q b", b=2), AXX,
                                        ALU.add), t)
        t = VE.do(lambda e: e.tensor_reduce(par[:, :, :].unsqueeze(3), dv.rearrange("p a (q b) -> p a b q", b=2), AXX,
                                            ALU.add), t)
        t1 = VE.do(lambda e, i=i: e.tensor_copy(pos[:, :, :], banks[i][:, 0:2 * NE].rearrange("p (j e) -> p j e", j=TT)),
                   t1)
        bank_free[i] = t1
        t1 = VE.do(lambda e: e.tensor_tensor(dpos[:, :, :, :], d12[:, :, :, :],
                                             pos[:, :, :].unsqueeze(2).broadcast_to([P, TT, 2, NE]), ALU.mult), t1)
        t1 = VE.do(lambda e: e.tensor_reduce(place[:, :, :], dpos[:, :, :, :].rearrange("p j r e -> p (j r) e"), AXX,
                                             ALU.add), t1)
        t1 = VE.do(lambda e: e.tensor_tensor(ph[:, :, :], iota[:, :].unsqueeze(1).broadcast_to([P, two, CAP]),
                                             place[:, :, :].broadcast_to([P, two, CAP]), ALU.is_equal), t1, t_io)
        t_in = VE.do(lambda e: e.tensor_tensor(
            inpair[:, :, :, :], ph[:, :, :].unsqueeze(2).broadcast_to([P, two, 2, CAP]),
            par[:, :, :].unsqueeze(3).broadcast_to([P, two, 2, CAP]), ALU.mult), t1, t)

        b6 = Region(2048)
        xgT = [sb(f"xgT{i}", [P, KC, P], stack=b6) for i in range(2)]
        hp = [chainm[:, i * HID:(i + 1) * HID] for i in range(2)]
        hpT = [maskf[:, i * HID:(i + 1) * HID].rearrange("p (k s) -> p k s", k=4) for i in range(2)]
        pick = [sb(f"pick{i}", [P, TT, P], stack=b5) for i in range(2)]
        wpick = [sb(f"wpick{i}", [P, TT, P], stack=b5) for i in range(2)]
        assert b5.at <= ARENA - 3 * KC * 512, b5.at
        pick_free, wpick_free, wpT_free = [None] * 2, [None] * 2, [None] * 2
        xgT_free, hp_free, hpT_free, yo_free = [f4] * 2, [f4] * 2, [f4] * 2, [f4] * 2
        acc = [take("gemm") for _ in range(4)]
        t_X, t_wpT, t_Y = {}, {}, {}

        def slots_of(p, dst, weight, after):
            for j in range(TT):
                VE.do(lambda e, j=j: e.tensor_scalar(
                    dst[:, j, :], inpair[:, 2 * j, :, :].rearrange("p b s -> p (b s)"), weight[:, 2 * j, p:p + 1], None,
                    ALU.mult), after)
                t = VE.do(lambda e, j=j: e.scalar_tensor_tensor(
                    out=dst[:, j, :], in0=inpair[:, 2 * j + 1, :, :].rearrange("p b s -> p (b s)"),
                    scalar=weight[:, 2 * j + 1, p:p + 1], in1=dst[:, j, :], op0=ALU.mult, op1=ALU.add), VE.last())
            return t

        def choose(p):
            S, X = pick[p % 2], xgT[p % 2]
            for half in range(2):
                i, fr = take("side")
                for k in range(4):
                    for j in range(TT):
                        f = lambda e, i=i, k=k, j=j, half=half: e.matmul(
                            banks[i][:, k * P:(k + 1) * P], utok[:, j, 4 * half + k::KC],
                            S[:, j, :], start=j == 0, stop=j == TT - 1)
                        t = (PE.do if k == 3 and j == TT - 1 else PE.quiet)(f, t_pick[p], t_utok, fr)
                f = ((lambda e, i=i, half=half: e.tensor_copy(
                    X[:, 4 * half:4 * half + 4, :], banks[i][:, :].rearrange("p (k s) -> p k s", k=4))) if half else
                    (lambda e, i=i, half=half: e.activation(
                        X[:, 4 * half:4 * half + 4, :], banks[i][:, :].rearrange("p (k s) -> p k s", k=4), ACT.Copy)))
                t2 = (VE if half else AC).do(f, t, xgT_free[p % 2])
                bank_free[i] = t2
                t_X[p, half] = t2
            pick_free[p % 2] = t

        def combine(p):
            for n in range(2):
                for j in range(TT):
                    bk, fr = acc[2 * j + n]
                    t = PE.do(lambda e, bk=bk, j=j, n=n: e.matmul(
                        banks[bk][:, :], wpT[p % 2][:, j * P:(j + 1) * P], yo[p % 2][:, n * 512:(n + 1) * 512],
                        start=p == 0, stop=p == NPAIR - 1, skip_group_check=True), t_wpT[p], t_Y[p, n], fr)
                    t_acc[j, n] = t
            wpT_free[p % 2] = yo_free[p % 2] = t

        def expert_block(w, e):
            if w == "down":
                return stream(a["expert_w_down_2"][0, e], 4, D, rows="(p k) n -> p k n")
            return stream(a[f"expert_w_{w}_2"][0, e], rows="(p k) n -> p k n")

        t_pick, t_acc = {}, {}
        t_pick[0] = slots_of(0, pick[0], pair, t_in)
        choose(0)

        t = VE.do(lambda e: e.tensor_tensor(eg, gl, gmax.broadcast_to([P, TT, 4]), ALU.subtract), t_g)
        t1 = AC.do(lambda e: e.activation(eg, eg, ACT.Exp), t)
        t = VE.do(lambda e: e.tensor_tensor(e2, m2, m1, ALU.subtract), t_in)
        t2 = AC.do(lambda e: e.activation(e2, e2, ACT.Exp), t)
        t = VE.do(lambda e: e.tensor_reduce(gsum, eg, AXX, ALU.add), t1)
        t = VE.do(lambda e: e.reciprocal(gsum, gsum), t)
        w1, w2_ = w12[:, :, 0:1], w12[:, :, 1:2]
        t2 = VE.do(lambda e: e.tensor_scalar(w1, e2, 1.0, None, ALU.add), t2)
        t2 = VE.do(lambda e: e.reciprocal(w1, w1), t2)
        t = VE.do(lambda e: e.tensor_tensor(w1, w1, gsum, ALU.mult), t, t2)
        t = VE.do(lambda e: e.tensor_tensor(w2_, w1, e2, ALU.mult), t)
        for j in range(TT):
            t_wp = VE.do(lambda e, j=j: e.tensor_tensor(
                wpair[:, 2 * j:2 * j + 2, :], pair[:, 2 * j:2 * j + 2, :],
                w12[:, j, :].unsqueeze(2).broadcast_to([P, 2, NPAIR]), ALU.mult), t)
        t1 = VE.do(lambda e: e.tensor_scalar(isover[:, :, :], pos[:, :, :], float(CAP), None, ALU.is_ge), t_in)
        t1 = VE.do(lambda e: e.tensor_tensor(sel, sel, isover[:, :, :], ALU.mult), t1, PE.last())
        t1 = VE.do(lambda e: e.tensor_reduce(over[:, 0:2].unsqueeze(2), sel, AXX, ALU.add), t1)
        i, fr = take("side")
        t1 = PE.do(lambda e, i=i: e.matmul(banks[i][:, 0:2], ones[:, :], over[:, 0:2], start=True, stop=True), t1, fr)
        t1 = VE.do(lambda e, i=i: e.tensor_copy(over[:, 2:4], banks[i][:, 0:2]), t1)
        bank_free[i] = t1
        t1 = VE.do(lambda e: e.tensor_tensor(over[:, 0:1], over[:, 2:3], over[:, 3:4], ALU.add), t1)
        VE.do(lambda e: e.tensor_copy(flag[:, :], over[:, 0:1]), t1)
        for j in range(TT):
            t1 = VE.do(lambda e, j=j: e.tensor_scalar(wov[:, j, :], d12[:, j, 0, :], w1[:, j, :], None, ALU.mult), t)
            t1 = VE.do(lambda e, j=j: e.scalar_tensor_tensor(
                out=wov[:, j, :], in0=d12[:, j, 1, :], scalar=w2_[:, j, :], in1=wov[:, j, :],
                op0=ALU.mult, op1=ALU.add), t1)
        VE.do(lambda e: e.tensor_tensor(wov[:, :, :], wov[:, :, :], isover[:, :, :], ALU.mult), t1)

        for p in range(NPAIR):
            E2 = (2 * p, 2 * p + 1)
            X, H, HT, Y = xgT[p % 2], hp[p % 2], hpT[p % 2], yo[p % 2]
            if p + 1 < NPAIR:
                t_pick[p + 1] = slots_of(p + 1, pick[(p + 1) % 2], pair, [t_in, pick_free[(p + 1) % 2]])
            t_wpick = slots_of(p, wpick[p % 2], wpair, [t_wp, wpick_free[p % 2]])
            for w in ("gate", "up"):
                bl = [expert_block(w, e) for e in E2]
                bk, fr = take("side")
                for k in range(KC):
                    for s_ in range(2):
                        f = lambda e, bk=bk, s_=s_, k=k, bl=bl, X=X: e.matmul(
                            banks[bk][64 * s_:64 * s_ + 64, :], X[:, k, 64 * s_:64 * s_ + 64], bl[s_][1][:, k, :],
                            start=k == 0, stop=k == KC - 1)
                        t = (PE.do if k == KC - 1 else PE.quiet)(f, bl[s_][2], fr, t_X[p, k // 4])
                        bl[s_][0].free = t
                if w == "gate":
                    t = AC.do(lambda e, bk=bk, H=H: e.activation(H, banks[bk][:, :], ACT.Silu), t, hp_free[p % 2])
                    bank_free[bk] = t
                    tgate = t
                else:
                    t_H = VE.do(lambda e, bk=bk, H=H: e.tensor_tensor(H, banks[bk][:, :], H, ALU.mult), t, tgate)
                    bank_free[bk] = t_H
            xgT_free[p % 2] = PE.last()
            i, fr = take("side")
            for j in range(TT):
                f = lambda e, i=i, j=j, p=p: e.transpose(banks[i][:, j * P:(j + 1) * P], wpick[p % 2][:, j, :],
                                                         ident[:, :])
                t = (PE.do if j == TT - 1 else PE.quiet)(f, t_wpick, fr)
            wpick_free[p % 2] = t
            t_wpT[p] = AC.do(lambda e, i=i, p=p: e.activation(wpT[p % 2][:, :], banks[i][:, 0:T], ACT.Copy), t,
                             wpT_free[p % 2])
            bank_free[i] = t_wpT[p]
            if p:
                combine(p - 1)
            i, fr = take("side")
            for c in range(4):
                f = lambda e, i=i, c=c, H=H: e.transpose(banks[i][:, c * P:(c + 1) * P], H[:, c::4],
                                                         ident[:, :])
                t2 = (PE.do if c == 3 else PE.quiet)(f, t_H, fr)
            hp_free[p % 2] = t2
            t_HT = AC.do(lambda e, i=i, HT=HT: e.activation(HT, banks[i][:, :].rearrange(
                "p (k s) -> p k s", k=4), ACT.Copy), t2, hpT_free[p % 2])
            bank_free[i] = t_HT
            if p + 1 < NPAIR:
                choose(p + 1)
            bl = [expert_block("down", e) for e in E2]
            for n in range(2):
                bk, fr = take("side")
                for k in range(4):
                    for s_ in range(2):
                        f = lambda e, bk=bk, s_=s_, k=k, n=n, bl=bl, HT=HT: e.matmul(
                            banks[bk][64 * s_:64 * s_ + 64, :], HT[:, k, 64 * s_:64 * s_ + 64],
                            bl[s_][1][:, k, n * 512:(n + 1) * 512], start=k == 0, stop=k == 3)
                        t3 = (PE.do if k == 3 else PE.quiet)(f, bl[s_][2], fr, t_HT)
                        bl[s_][0].free = t3
                t_Y[p, n] = (AC if n else VE).do(
                    (lambda e, bk=bk, Y=Y: e.activation(Y[:, 512:1024], banks[bk][:, :], ACT.Copy)) if n else
                    (lambda e, bk=bk, Y=Y: e.tensor_copy(Y[:, 0:512], banks[bk][:, :])), t3, yo_free[p % 2])
                bank_free[bk] = t_Y[p, n]
            hpT_free[p % 2] = PE.last()
        combine(NPAIR - 1)
        for n in range(2):
            for j in range(TT):
                o = xtok2[:, j, n * 512:(n + 1) * 512]
                VE.do(lambda e, j=j, n=n, o=o: e.tensor_tensor(o, banks[acc[2 * j + n][0]][:, :], o, ALU.add),
                      t_acc[j, n])
        VE.quiet(lambda e: e.wait_ge(VE.sem, VE.count))
        AC.quiet(lambda e: e.wait_ge(t_fr[0], t_fr[1]))

        with nc.Block() as block:
            block.sync(SP.emit)
            block.scalar(AC.emit)
            block.vector(VE.emit)
            block.gpsimd(PO.emit)
            block.tensor(PE.emit)

        hidT = chainm[:, :].rearrange("p (k t) -> p k t", k=4)
        loop_sems = [nc.alloc_semaphore(f"loop{i}") for i in range(6)]
        first = loop_sems[0].num
        assert [x.num for x in loop_sems] == list(range(first, first + 6))
        n_over = nc.values_load(flag[0:1, 0:1], min_val=0, max_val=2 * T)
        with nc.If(n_over > 0):
            with nc.Fori(0, NE) as ex:
                lPE, lAC, lVE = (Queue(n, s) for n, s in zip(("pe", "act", "dve"), loop_sems[3:6]))
                W = []
                for i, (name, kc, cols) in enumerate((("gate", KC, HID), ("up", KC, HID), ("down", 4, D))):
                    w = ring[i].buf[:, 0:kc * cols].rearrange("p (k n) -> p k n", k=kc)
                    src = a[f"expert_w_{name}_2"][0, bass.ds(ex, 1)].rearrange("o (k p) n -> p (o k) n", p=P)
                    nc.sync.dma_start(w, src).then_inc(loop_sems[i], 16)
                    W.append((w, (loop_sems[i], 16)))
                t_wc = lVE.do(lambda e: e.tensor_copy(wcol[:, :, :], wov[:, :, bass.ds(ex, 1)]))
                for m in range(2):
                    for c in range(4):
                        for k in range(KC):
                            whole = c == 3 and k == KC - 1
                            (lPE.do if whole else lPE.quiet)(lambda e, m=m, c=c, k=k: e.matmul(
                                banks[2 * m + c // 2][:, (c % 2) * T:(c % 2 + 1) * T],
                                W[m][0][:, k, c * P:(c + 1) * P], uTe[:, k, :], start=k == 0, stop=k == KC - 1),
                                W[m][1])
                t_h = None
                for b in range(2):
                    h2 = hidT[:, 2 * b:2 * b + 2, :].rearrange("p c t -> p (c t)")
                    t_s = lAC.do(lambda e, b=b, h2=h2: e.activation(h2, banks[b][:, :], ACT.Silu), (lPE.sem, 1))
                    t_h = lVE.do(lambda e, b=b, h2=h2: e.tensor_tensor(h2, banks[2 + b][:, :], h2, ALU.mult),
                                 t_s, (lPE.sem, 2))
                for j in range(TT):
                    for n in range(2):
                        for k in range(4):
                            f = lambda e, j=j, n=n, k=k: e.matmul(
                                banks[4 + 2 * j + n][:, :], hidT[:, k, j * P:(j + 1) * P],
                                W[2][0][:, k, n * 512:(n + 1) * 512], start=k == 0, stop=k == 3)
                            t = (lPE.do if k == 3 else lPE.quiet)(f, W[2][1], t_h)
                        o = xtok2[:, j, n * 512:(n + 1) * 512]
                        lVE.do(lambda e, j=j, n=n, o=o: e.scalar_tensor_tensor(
                            out=o, in0=banks[4 + 2 * j + n][:, :], scalar=wcol[:, j, :], in1=o,
                            op0=ALU.mult, op1=ALU.add), t, t_wc)
                lPE.emit(nc.tensor)
                lAC.emit(nc.scalar)
                lVE.emit(nc.vector)
                nc.vector.wait_ge(lVE.sem, lVE.count)
                nc.all_engine_barrier(sems_to_clear=range(first, first + 6))

        ss2 = small[:, 34:36]
        sq = [yo[j][:, :] for j in range(TT)]
        res = [utok[:, j, :] for j in range(TT)]
        outs = []
        tAC, tVE, tSP = (Queue(n, sem("s_tail_" + n)) for n in ("act", "dve", "sp"))
        for j in range(TT):
            o = xtok2[:, j, :]
            t = tAC.do(lambda e, j=j, o=o: e.activation(sq[j], o, ACT.Square, accum_out=ss2[:, j:j + 1]))
            t = tAC.do(lambda e, j=j: e.activation(ss2[:, j:j + 1], ss2[:, j:j + 1], ACT.Sqrt, bias=epsc[:, 0:1],
                                                   scale=1.0 / D), t)
            t = tVE.do(lambda e, j=j: e.reciprocal(ss2[:, j:j + 1], ss2[:, j:j + 1]), t)
            t = tVE.do(lambda e, j=j, o=o: e.scalar_tensor_tensor(
                out=res[j], in0=o, scalar=ss2[:, j:j + 1], in1=frow[:, :], op0=ALU.mult, op1=ALU.mult), t)
            outs.append(load(tSP, f"out{j}", out[0, j * P:(j + 1) * P, :], res[j], t))

        def store(e):
            tSP.emit(e)
            for s, v in outs:
                e.wait_ge(s, v)

        with nc.Block() as block:
            block.scalar(tAC.emit)
            block.vector(tVE.emit)
            block.sync(store)


def two_pi_parts():
    rest, parts = 2 * np.pi, []
    for bits in (9, 11):
        scale = 2.0 ** (bits - 3)
        part = np.floor(rest * scale * 2.0 ** (0 if not parts else 9)) / (scale * 2.0 ** (0 if not parts else 9))
        parts.append(float(part))
        rest -= part
    return parts + [float(np.float32(rest))]


TWO_PI_PARTS = two_pi_parts()


def constants():
    s, t = np.arange(P)[:, None], np.arange(P)[None, :]
    masks = np.zeros((P, len(LEVELS), P), np.int32)
    for i, m in enumerate(LEVELS):
        masks[:, i, :] = (s == t) if m == 1 else ((s // m == t // m) & (s % m < m // 2) & (t % m >= m // 2))
    far = 1.0e32
    q, k = np.arange(P)[:, None], np.arange(T)[None, :]
    d0 = (q - k[:, :P]).astype(np.float64)
    d1 = (q + P - k).astype(np.float64)
    dist = np.concatenate([np.where(d0 >= 0, d0, far), np.where(d1 >= 0, d1, far)], 1).astype(np.float32)
    lg = np.log(1.0 - 2.0 ** (-5.0 - np.arange(HEADS)))
    dec = np.zeros((P, HEADS, 384), np.float32)
    for h in range(HEADS):
        r0 = np.arange(T)[None, :] - s
        r1 = t - s
        r = np.concatenate([r0, r1], 1)
        dec[:, h] = np.where(r >= 0, np.exp(lg[h] * np.maximum(r, 0)), 0.0)
    theta = (np.float32(1.0) / np.power(np.float32(10000.0), np.linspace(0.0, 1.0, P, dtype=np.float32)))
    iota = np.tile(np.arange(CAP, dtype=np.float32), (P, 1))
    return {"ident": np.eye(P, dtype=np.float32), "masks": masks, "dist": dist, "decay": dec,
            "theta": theta.astype(np.float32).reshape(P, 1), "tri": (s < t).astype(np.float32), "iota": iota}


def kernel(**inputs):
    import concourse.bacc as bacc
    from concourse.bass_utils import run_bass_kernel_spmd

    nc = bacc.Bacc("TRN2", target_bir_lowering=False, num_devices=1)
    arrays, a = {}, {}
    for name, x in {**inputs, **constants()}.items():
        x = np.ascontiguousarray(x)
        arrays["in_" + name] = x
        a[name] = nc.dram_tensor("in_" + name, x.shape, mybir.dt.from_np(x.dtype), kind="ExternalInput").ap()
    out = nc.dram_tensor("out_0", (1, T, D), F32, kind="ExternalOutput").ap()
    build(nc, a, out)
    r = run_bass_kernel_spmd(nc, [arrays], core_ids=[0])
    return r.results[0]["out_0"]
```

```python
import numpy as np
from contextlib import ExitStack

import concourse.bass as bass
from concourse import mybir
from concourse.alu_op_type import AluOpType as ALU

F32 = mybir.dt.float32
F32R = mybir.dt.float32r
I32 = mybir.dt.int32
U32 = mybir.dt.uint32
ACT = mybir.ActivationFunctionType
AXX = mybir.AxisListType.X

P = 128
T = 256
TT = T // P
D = 1024
KC = D // P
EPS = 1e-6
HEADS = 4
CH = 64
LEVELS = [1, 2, 4, 8, 16, 32, 64, 128]
FF = 2816
FFC = FF // P
NE, NGRP, EPG, HID = 32, 4, 8, 512
CAP = 64
NPAIR = NE // 2
RING = 3
UNITS = 3
UNIT = 1024
ARENA = 23824
LAMBDA_INIT = 0.2
ROWS = dict(b_ada=0, norm1=48, norm2=56, mixn=64, ffnn=72, fin1=80, lb0=88, lb1=92, gn=96,
            subln=97, gkb=98, glan=102, retn=104, c=120)


class Queue:

    def __init__(self, name, sem):
        self.name, self.sem, self.count, self.items = name, sem, 0, []

    def do(self, fn, *after):
        self.count += 1
        self.items.append((after, fn, (self.sem, 1)))
        return (self.sem, self.count)

    def quiet(self, fn, *after):
        self.items.append((after, fn, None))

    def last(self):
        return (self.sem, self.count)

    def emit(self, eng):
        met = {}

        def wait(after):
            for a in after:
                if a is None:
                    continue
                if len(a) == 2 and isinstance(a[1], int):
                    if a[1] > met.get(a[0].num, 0):
                        eng.wait_ge(a[0], a[1])
                        met[a[0].num] = a[1]
                else:
                    wait(a)

        for after, fn, inc in self.items:
            wait(after)
            if fn is None:
                continue
            ins = fn(eng)
            if inc:
                ins.then_inc(inc[0], inc[1])


def build(nc, a, out):
    ctx = ExitStack()
    with ctx:
        arena = [None]

        class Region:

            def __init__(self, start=0):
                self.at = start

        def sb(name, shape, dt=F32, stack=None, ctx=ctx):
            if stack is None:
                return ctx.enter_context(nc.sbuf_tensor(name, shape, dt))
            n = int(np.prod(shape[1:]))
            v = arena[0][0:shape[0], stack.at:stack.at + n]
            stack.at += n
            assert stack.at <= ARENA, (name, stack.at)
            if dt != F32:
                v = v.bitcast(dt)
            if len(shape) == 3:
                v = v.rearrange("p (a b) -> p a b", a=shape[1])
            elif len(shape) == 4:
                v = v.rearrange("p (a b c) -> p a b c", a=shape[1], b=shape[2])
            return v

        def sem(name):
            return ctx.enter_context(nc.semaphore(name))

        PE, AC, VE, PO, SP = (Queue(n, sem("s_" + n)) for n in ("pe", "act", "dve", "pool", "sp"))

        def load(q, name, dst, src, *after):
            s = sem("d_" + name)
            q.items.append((after, lambda e: e.dma_start(dst, src), (s, 16)))
            return (s, 16)

        def fence():
            return [PE.last(), AC.last(), VE.last(), PO.last()]

        arena[0] = ctx.enter_context(nc.sbuf_tensor("arena", [P, ARENA], F32))
        class Slot:

            def __init__(self, name, buf, free=None):
                self.buf, self.sem, self.free, self.uses = buf, sem("s_" + name), free, 0

        whole = []

        def new_slots(where, free=None):
            i = len(whole)
            whole.append(sb(f"weights{i}", [P, KC * 512], stack=where))
            return [Slot(f"weights{i}{x}", whole[i][:, x * KC * 256:(x + 1) * KC * 256], free) for x in range(2)]

        ring = []
        for _ in range(RING):
            ring += new_slots(None)
        ident = sb("ident", [P, P])
        ones = sb("ones", [P, P])
        pcol = sb("pcol", [P, P])
        hT = sb("hT", [P, KC, T])
        modc = sb("modc", [P, 48])
        scl = sb("scl", [P, 16])
        lamrow = sb("lamrow", [1, 4, 64])
        lams = sb("lams", [1, 8])
        chainm = sb("chainm", [P, HEADS * T])
        maskf = sb("masks", [P, len(LEVELS) * P])
        wmix = sb("wmix", [P, 2, KC])
        flag = sb("flag", [P, 1], I32)
        small = sb("small", [P, 64])
        rstd = sb("rstd", [P, T])
        r1 = sb("r1", [P, T])
        epsc = sb("epsc", [P, 1])
        eps2 = sb("eps2", [P, 1])
        split_memory = ctx.enter_context(ExitStack())
        XH = sb("XH", [P, KC, T], F32R, ctx=split_memory)
        XL = sb("XL", [P, KC, T], F32R, ctx=split_memory)
        WHL = sb("WHL", [P, UNITS, 2, UNIT], F32R, ctx=split_memory)
        s_hi, s_lo = sem("s_weights_hi"), sem("s_weights_lo")
        x_ready, x_free = [None] * KC, [None] * KC
        unit_free, unit_n = [None] * UNITS, [0]
        mark = {}
        banks = [ctx.enter_context(nc.psum_tensor(f"bank{i}", [P, 512], F32)) for i in range(8)]
        bank_free = [None] * 8
        gemm_n, side_n = [0], [0]

        def take(kind):
            n = gemm_n if kind == "gemm" else side_n
            i = n[0] % 4 + (0 if kind == "gemm" else 4)
            n[0] += 1
            return i, bank_free[i]

        def stream(src):
            slot = ring.pop(0)
            ring.append(slot)
            slot.uses += 1
            kc, cols = src.shape[1:]
            dst = slot.buf[:, 0:kc * cols].rearrange("p (k n) -> p k n", k=kc)
            SP.items.append(([slot.free], lambda e: e.dma_start(dst, src), (slot.sem, 16)))
            return slot, dst, (slot.sem, 16 * slot.uses)

        def stream_block(src):
            rows, cols = src.shape
            step = KC * 256 // cols * P
            return [stream(src[r:min(r + step, rows), :].rearrange("(k p) n -> p k n", p=P))
                    for r in range(0, rows, step)]

        early = Region()
        prow = sb("prow", [P, P], stack=early)
        xtok = sb("xtok", [P, TT, D], stack=early)
        t_id = load(AC, "ident", ident[:, :], a["ident"])
        t_x = load(SP, "x", xtok[:, :, :], a["x"][0].rearrange("(i p) d -> p i d", p=P))
        t_rows = []
        for name, src, n in [("b_ada", a["b_ada"], 48), ("norm1", a["norm1_w"], 8), ("norm2", a["norm2_w"], 8),
                             ("mixn", a["norm_mix_w_2"], 8), ("ffnn", a["norm_ffn_w_2"], 8),
                             ("fin1", a["final_norm_w"].rearrange("(o n) -> o n", o=1), 8),
                             ("lb0", a["hgrn_lb_logits"][0:1], 4), ("lb1", a["hgrn_lb_logits"][1:2], 4),
                             ("gn", a["hgrn_gnorm_w"], 1), ("subln", a["diff_subln_w"], 1),
                             ("gkb", a["gla_gk_bias_2"], 4), ("glan", a["gla_norm_w_2"], 2),
                             ("retn", a["ret_norm_w_2"], 16), ("c", a["c"], 8)]:
            r = ROWS[name]
            t_rows.append(load(SP if r % 16 else AC, "row_" + name, prow[r:r + n, :],
                               src.rearrange("o (r p) -> (o r) p", p=P)))
        SP.items.append(([t_rows, t_x, t_id], None, None))
        t_ones = VE.do(lambda e: e.memset(ones[:, :], 1.0))
        t_eps = VE.do(lambda e: e.memset(epsc[:, :], EPS))
        t_eps = VE.do(lambda e: e.memset(eps2[:, :], EPS * EPS))
        bi, bf = take("side")
        t = PE.do(lambda e: e.transpose(banks[bi][:, 0:P], prow[:, :], ident[:, :]), t_rows, t_id)
        t_pcol = VE.do(lambda e: e.tensor_copy(pcol[:, :], banks[bi][:, 0:P]), t)
        bank_free[bi] = t_pcol

        def col(name, k=0):
            r = ROWS[name] + k
            return pcol[:, r:r + 1]

        cT = small[:, 0:8]
        t_cT = AC.do(lambda e: e.activation(cT, pcol[:, ROWS["c"]:ROWS["c"] + 8], ACT.Silu), t_pcol)

        def to_features(src, dst, *after):
            t = None
            for k in range(KC):
                i, fr = take("side")
                for j in range(TT):
                    f = lambda e, i=i, j=j, k=k: e.transpose(banks[i][:, j * P:(j + 1) * P],
                                                             src[:, j, k * P:(k + 1) * P], ident[:, :])
                    t = (PE.do if j == TT - 1 else PE.quiet)(f, after, fr)
                q = VE if k % 2 else AC
                g = ((lambda e, i=i, k=k: e.tensor_copy(dst[:, k, :], banks[i][:, 0:T])) if k % 2 else
                     (lambda e, i=i, k=k: e.activation(dst[:, k, :], banks[i][:, 0:T], ACT.Copy)))
                t = q.do(g, t)
                bank_free[i] = t
            return [AC.last(), VE.last()]

        def to_tokens(src, dst, *after):
            for j in range(TT):
                for k0 in range(0, KC, 4):
                    i, fr = take("side")
                    for k in range(4):
                        f = lambda e, i=i, j=j, k=k, k0=k0: e.transpose(
                            banks[i][:, k * P:(k + 1) * P], src[:, k0 + k, j * P:(j + 1) * P], ident[:, :])
                        t = (PE.do if k == 3 else PE.quiet)(f, after, fr)
                    t = AC.do(lambda e, i=i, j=j, k0=k0: e.activation(
                        dst[:, j, k0 * P:(k0 + 4) * P], banks[i][:, :], ACT.Copy), t)
                    bank_free[i] = t
            return t

        t_h = to_features(xtok, hT, t_x, t_id)

        scratch = sb("squares", [P, KC, T], stack=Region(ARENA - 1024 - KC * T))

        def split_x(k, src, *after, shift=None):
            t = AC.do((lambda e: e.activation(XH[:, k, :], src, ACT.Copy)) if shift is None else
                      (lambda e: e.activation(XH[:, k, :], src, ACT.Identity, bias=shift)), after, x_free[k])
            x_ready[k] = VE.do((lambda e: e.tensor_tensor(XL[:, k, :], src, XH[:, k, :], ALU.subtract))
                               if shift is None else
                               (lambda e: e.scalar_tensor_tensor(out=XL[:, k, :], in0=src, scalar=shift,
                                                                 in1=XH[:, k, :], op0=ALU.add, op1=ALU.subtract)), t)

        def sums(src, sq, toks, weights=None, ks=range(KC), got=None):
            if got is None:
                got = [take("side") for _ in sq]
                AC.do(lambda e: e.activation(small[:, 40:41], epsc[:, 0:1], ACT.Sqrt), t_eps)
            for k in ks:
                t = [AC.do(lambda e, k=k: e.activation(sq[0][:, k, :], src[:, k, :], ACT.Square), toks(k))]
                if weights is not None:
                    t.append(VE.do(lambda e, k=k: e.scalar_tensor_tensor(
                        out=sq[1][:, k, :], in0=src[:, k, :], scalar=weights[:, k:k + 1], in1=src[:, k, :],
                        op0=ALU.mult, op1=ALU.mult), toks(k)))
                for (i, fr), dst, t1 in zip(got, sq, t):
                    f = lambda e, k=k, i=i, dst=dst: e.matmul(banks[i][:, 0:T], ones[:, :], dst[:, k, :],
                                                              start=k == 0, stop=k == KC - 1, skip_group_check=True)
                    t_mm = (PE.do if k == KC - 1 else PE.quiet)(f, t1, fr, t_ones)
            return got, t_mm

        def norm_scale(src, toks):
            ((i, _),), t = sums(src, [scratch], toks)
            t = AC.do(lambda e: e.activation(rstd[:, :], banks[i][:, 0:T], ACT.Sqrt, bias=epsc[:, 0:1],
                                             scale=1.0 / D), t, t_eps, VE.last())
            bank_free[i] = t
            return VE.do(lambda e: e.reciprocal(rstd[:, :], rstd[:, :]), t)

        def norm_apply(src, weight, shift, t, *after):
            t2 = {}
            for k in range(KC + 2):
                if k < KC:
                    t2[k] = VE.do(lambda e, k=k: e.scalar_tensor_tensor(
                        out=scratch[:, k, :], in0=src[:, k, :], scalar=weight(k), in1=rstd[:, :],
                        op0=ALU.mult, op1=ALU.mult), t, after)
                if k >= 2:
                    split_x(k - 2, scratch[:, k - 2, :], t2[k - 2], shift=shift(k - 2))

        def steps(src, evac, tok=False, kc=KC, cols=512, parts=1, part=0, hold=None, step=1, xo=0,
                  before=None):
            halves = stream_block(src)
            per = UNIT // cols
            nu = kc // per
            groups = list(range(TT)) if tok else list(range(cols // P))
            nb = TT if tok else (cols + 255) // 256
            if part == 0:
                got = [take("gemm") for _ in range(nb)]
                if hold is not None:
                    hold.extend(got)
            else:
                got = hold
            pieces = {}

            def split(u, ahead):
                n = unit_n[0]
                unit_n[0] += 1
                b = n % UNITS
                hi, lo = (WHL[:, b, x, :].rearrange("p (k n) -> p k n", k=per) for x in range(2))
                slot, w, t_w = halves[u // 2]
                ws = w[:, u % 2 * per:(u % 2 + 1) * per, :]
                for q, item in ((AC, ([t_w, unit_free[b]], lambda e: e.activation(hi, ws, ACT.Copy), (s_hi, 1))),
                                (VE, ([(s_hi, n + 1)], lambda e: e.tensor_tensor(lo, ws, hi, ALU.subtract),
                                      (s_lo, 1)))):
                    if ahead and q in mark:
                        q.items.insert(mark[q], item)
                        mark[q] += 1
                    else:
                        q.items.append(item)
                pieces[u] = (b, hi, lo, (s_lo, n + 1))
                slot.free = (s_lo, n + 1)

            for u in range(min(2, nu)):
                split(u, True)
            for u in range(nu):
                if u + 2 < nu:
                    split(u + 2, False)
                if u == nu - 1:
                    mark[AC], mark[VE] = len(AC.items), len(VE.items)
                b, hi, lo, t_lo = pieces[u]
                for kk in range(per):
                    k = u * per + kk
                    x = xo + k
                    for g in groups:
                        bk, fr = got[g if tok else g // 2]
                        for n, (wp, xp) in enumerate(((hi, XH), (hi, XL), (lo, XH))):
                            if tok:
                                o = banks[bk][:, 0:cols]
                                l, r = xp[:, x, g * P:(g + 1) * P], wp[:, kk, :]
                            else:
                                o = banks[bk][:, (g % 2) * T:(g % 2 + 1) * T]
                                l = (wp[:, kk, 256 * (g // 2) + g % 2:256 * (g // 2) + 256:2] if step == 2 else
                                     wp[:, kk, g * P:(g + 1) * P])
                                r = xp[:, x, :]
                            st = part == 0 and k == 0 and n == 0 and (tok or g % 2 == 0)
                            f = lambda e, o=o, l=l, r=r, st=st, k=k, n=n: e.matmul(
                                o, l, r, start=st, stop=part == parts - 1 and k == kc - 1 and n == 2,
                                skip_group_check=True)
                            last = g == groups[-1] and n == 2
                            t = (PE.do if last else PE.quiet)(f, t_lo, fr if part == 0 else None, x_ready[x])
                    x_free[x] = t
                unit_free[b] = t
                if u == nu // 2 - 1:
                    yield
            if before is not None:
                before()
            if part == parts - 1:
                for b in range(nb):
                    bk = got[b][0]
                    bank_free[bk] = evac(bk, b, t) if tok else evac(bk, 2 * b, min(2, cols // P - 2 * b), t)
            yield

        def project(*args, **kw):
            for _ in steps(*args, **kw):
                pass

        def weave(mains, *lanes):
            n, live = 0, list(lanes)

            def turn(n):
                for lane in list(live):
                    if n is None or lane[0] <= n:
                        try:
                            next(lane[1])
                        except StopIteration:
                            live.remove(lane)
            turn(-1)
            for m in mains:
                for _ in m:
                    turn(n)
                    n += 1
            while live:
                turn(None)

        def copy_T(dst, base=0, scale=1.0, func=ACT.Copy, wait=None):
            def evac(bk, ch, n, t):
                o = dst[:, base + ch:base + ch + n, :]
                return AC.do(lambda e: e.activation(o, banks[bk][:, 0:n * T].rearrange("p (c t) -> p c t", c=n),
                                                    func, scale=scale), t, wait)
            return evac

        def copy_tok(dst, c0, wait=None, done=None):
            def evac(bk, j, t):
                t = AC.do(lambda e: e.activation(dst[:, j, c0:c0 + 512], banks[bk][:, :], ACT.Copy), t, wait)
                if done is not None:
                    done.append(t)
                return t
            return evac

        mreg = Region(ARENA - 1024)
        macc = [sb(f"macc{i}", [P, 512], stack=mreg) for i in range(2)]
        macc_free = [None, None]
        SPLIT = 5

        def weigh(n):
            halves = stream_block(a["w_ada"][0][:, n * 512:(n + 1) * 512])
            w = [halves[k // 4][1][:, k % 4, :] for k in range(KC)]
            t_w = [halves[k // 4][2] for k in range(KC)]
            m = macc[n % 2]
            tv = VE.do(lambda e: e.tensor_scalar(m[:, :], w[0], cT[:, 0:1], None, ALU.mult),
                       t_w[0], t_cT, macc_free[n % 2])
            for k in range(1, SPLIT):
                tv = VE.do(lambda e, k=k: e.scalar_tensor_tensor(
                    out=m[:, :], in0=w[k], scalar=cT[:, k:k + 1], in1=m[:, :], op0=ALU.mult, op1=ALU.add), tv, t_w[k])
            for k in range(SPLIT, KC):
                ta = AC.do(lambda e, k=k: e.activation(w[k], w[k], ACT.Copy, scale=cT[:, k:k + 1]), t_w[k], t_cT)
            for slot, _, _ in halves:
                slot.free = [tv, ta]
            return n, [slot for slot, _, _ in halves], [m[:, :]] + w[SPLIT:], [tv, ta]

        def sum_up(n, slots, rows, ready):
            bk, fr = take("side")
            for c in range(4):
                for i, x in enumerate(rows):
                    f = lambda e, c=c, x=x, i=i: e.matmul(banks[bk][:, c * P:(c + 1) * P], x[:, c * P:(c + 1) * P],
                                                          ones[:, :], start=i == 0, stop=i == len(rows) - 1)
                    last = c == 3 and i == len(rows) - 1
                    t = (PE.do if last else PE.quiet)(f, ready, fr, t_ones)
            for slot in slots:
                slot.free = [t, ready]
            macc_free[n % 2] = t
            bank_free[bk] = VE.do(lambda e: e.tensor_tensor(modc[:, 4 * n:4 * n + 4], banks[bk][:, 0:512:P],
                                                            pcol[:, 4 * n:4 * n + 4], ALU.add), t)

        def modulations(ns):
            for n in ns:
                n, slots, rows, ready = weigh(n)
                tp = None
                for k in range(2, len(rows)):
                    tp = PO.do(lambda e, k=k, rows=rows: e.tensor_tensor(rows[1], rows[1], rows[k], ALU.add),
                               ready[1], tp)
                yield
                sum_up(n, slots, rows[:2], [ready, tp])

        block = weigh(0)
        t_rstd = norm_scale(hT, lambda k: t_h)
        for n in range(1, 4):
            following = weigh(n)
            sum_up(*block)
            block = following
        sum_up(*block)
        t_mod0 = VE.last()
        t_scl1 = VE.do(lambda e: e.scalar_tensor_tensor(
            out=scl[:, 0:8], in0=modc[:, 8:16], scalar=1.0, in1=pcol[:, ROWS["norm1"]:ROWS["norm1"] + 8],
            op0=ALU.add, op1=ALU.mult), t_mod0)

        lbc = small[:, 8:12]
        oml = small[:, 12:16]
        l0 = pcol[:, ROWS["lb0"]:ROWS["lb0"] + 4]
        l1 = pcol[:, ROWS["lb1"]:ROWS["lb1"] + 4]
        mx, e0, e1 = small[:, 16:20], small[:, 20:24], small[:, 24:28]
        t = VE.do(lambda e: e.tensor_tensor(mx, l0, l1, ALU.max), t_pcol)
        VE.do(lambda e: e.tensor_tensor(e0, l0, mx, ALU.subtract), t)
        t = VE.do(lambda e: e.tensor_tensor(e1, l1, mx, ALU.subtract), t)
        t = AC.do(lambda e: e.activation(small[:, 20:28], small[:, 20:28], ACT.Exp), t)
        t = VE.do(lambda e: e.tensor_tensor(mx, e0, e1, ALU.add), t)
        t = VE.do(lambda e: e.reciprocal(mx, mx), t)
        VE.do(lambda e: e.tensor_tensor(lbc, e0, mx, ALU.mult), t)
        t_lb = VE.do(lambda e: e.tensor_tensor(oml, e1, mx, ALU.mult), t)

        t_l = [load(PO, "lam" + n, lamrow[:, i, :], a["diff_lambda_" + n]) for i, n in enumerate(["q1", "k1", "q2", "k2"])]
        t = VE.do(lambda e: e.tensor_tensor(lamrow[:, 0::2, :], lamrow[:, 0::2, :], lamrow[:, 1::2, :], ALU.mult), t_l)
        t = VE.do(lambda e: e.tensor_reduce(lams[:, 0:2], lamrow[:, 0::2, :], AXX, ALU.add), t)
        t = AC.do(lambda e: e.activation(lams[:, 2:4], lams[:, 0:2], ACT.Exp), t)
        t = VE.do(lambda e: e.tensor_tensor(lams[:, 4:5], lams[:, 3:4], lams[:, 2:3], ALU.subtract), t)
        t = VE.do(lambda e: e.tensor_scalar(lams[:, 5:6], lams[:, 4:5], -LAMBDA_INIT, None, ALU.add), t)
        i_l, fr = take("side")
        t = PE.do(lambda e: e.matmul(banks[i_l][:, 0:1], ones[0:1, :], lams[0:1, 5:6], start=True, stop=True),
                  t, t_ones, fr)
        neglam = small[:, 28:29]
        t_lam = VE.do(lambda e: e.tensor_copy(neglam, banks[i_l][:, 0:1]), t)
        bank_free[i_l] = t_lam

        t = PO.do(lambda e: e.memset(chainm[:, :], 1.0))
        t_chain = PO.do(lambda e: e.memset(chainm[:, 0:HEADS * T:CH], 0.0), t)
        masks = maskf[:, :].bitcast(U32).rearrange("p (l t) -> p l t", l=len(LEVELS))
        t_masks = load(PO, "masks", masks[:, :, :], a["masks"].bitcast(U32))

        mark[AC], mark[VE] = len(AC.items), len(VE.items)
        norm_apply(hT, lambda k: scl[:, k:k + 1], lambda k: modc[:, k:k + 1], t_rstd, t_scl1, t_mod0)
        f0 = fence()

        def gated(name, stack, q, k, v, b, dv, escale, oT, ready, ztok, t_v, result):
            lev = [[sb(f"{name}_{x}{i}", [P, HEADS, T], stack=stack) for x in ("e", "q", "k")] for i in range(2)]
            A0 = sb(name + "_A0", [P, HEADS, T], stack=stack)
            A1 = sb(name + "_A1", [P, HEADS, P], stack=stack)
            bl = sb(name + "_bl", [P, HEADS, 1], stack=stack)
            NV = dv // P
            tA = [None, None]
            tz = PO.do(lambda e: e.memset(A0[:, :, 0:P], 0.0), ztok)
            tz = PO.do(lambda e: e.memset(A1[:, :, :], 0.0), tz)
            for i in range(2):
                PO.do(lambda e, i=i: e.memset(lev[i][1][:, :, :], 0.0), ztok)
                tz = PO.do(lambda e, i=i: e.memset(lev[i][2][:, :, :], 0.0), ztok)
            free = [tz, tz]

            def factors(li, m):
                E, Q, K = lev[li % 2]
                if m == 1:
                    return q, k, ready
                g = HEADS * T // m
                vw = lambda x: x[:, :, :].rearrange("p h (g m) -> p (h g) m", m=m)
                B, Ev, Qv, Kv = vw(b), vw(E), vw(Q), vw(K)
                qq, kk = vw(q), vw(k)
                half = m // 2
                fr = free[li % 2]
                if m <= P:
                    ref = B[:, :, half - 1:half].broadcast_to([P, g, half])
                    if m <= CH:
                        VE.do(lambda e: e.tensor_tensor(Ev[:, :, half:], B[:, :, half:], ref, ALU.subtract), ready, fr)
                    else:
                        VE.do(lambda e: e.tensor_copy(Ev[:, :, 64:], B[:, :, 64:]), ready, fr)
                    t = VE.do(lambda e: e.tensor_tensor(Ev[:, :, 0:half], ref, B[:, :, 0:half], ALU.subtract), ready, fr)
                else:
                    t0 = VE.do(lambda e: e.tensor_tensor(bl[:, :, :], b[:, :, 63:64], b[:, :, 127:128], ALU.add),
                               ready, fr)
                    VE.do(lambda e: e.tensor_copy(E[:, :, 128:192], b[:, :, 128:192]), ready, fr)
                    VE.do(lambda e: e.tensor_tensor(
                        E[:, :, 192:256], b[:, :, 192:256], b[:, :, 191:192].broadcast_to([P, HEADS, 64]),
                        ALU.add), ready, fr)
                    VE.do(lambda e: e.tensor_tensor(
                        E[:, :, 64:128], b[:, :, 127:128].broadcast_to([P, HEADS, 64]), b[:, :, 64:128],
                        ALU.subtract), ready, fr)
                    t = VE.do(lambda e: e.tensor_tensor(
                        E[:, :, 0:64], bl[:, :, :].broadcast_to([P, HEADS, 64]), b[:, :, 0:64],
                        ALU.subtract), t0, fr)
                t = AC.do(lambda e: e.activation(E[:, :, :], E[:, :, :], ACT.Exp, scale=escale), t)
                tk = PO.do(lambda e: e.tensor_tensor(
                    Kv[:, :, 0:half], kk[:, :, 0:half], Ev[:, :, 0:half], ALU.mult), t, fr, ready)
                tq = VE.do(lambda e: e.tensor_tensor(
                    Qv[:, :, half:], qq[:, :, half:], Ev[:, :, half:], ALU.mult), t, fr, ready)
                return Q, K, [tk, tq]

            every = LEVELS + [256]
            ahead = [factors(li, every[li]) for li in range(2)]
            yield
            for li, m in enumerate(every):
                Qs, Ks, tq = ahead.pop(0)
                tiles = [(0, 0), (1, 1)] if m <= P else [(0, 1)]
                done = []
                for si, ti in tiles:
                    i, fr = take("side")
                    for h in range(HEADS):
                        f = lambda e, i=i, h=h, si=si, ti=ti, Qs=Qs, Ks=Ks: e.matmul(
                            banks[i][:, h * P:(h + 1) * P], Ks[:, h, si * P:(si + 1) * P],
                            Qs[:, h, ti * P:(ti + 1) * P], start=True, stop=True)
                        t = (PE.do if h == HEADS - 1 else PE.quiet)(f, tq, fr)
                    ps = banks[i][:, :].rearrange("p (h t) -> p h t", h=HEADS)
                    if m > P:
                        t2 = VE.do(lambda e, ps=ps: e.tensor_copy(A0[:, :, P:T], ps), t, ztok)
                    else:
                        dst = A0[:, :, 0:P] if si == 0 else A1[:, :, :]
                        mk = masks[:, li:li + 1, :].broadcast_to([P, HEADS, P])
                        t2 = VE.do(lambda e, dst=dst, mk=mk, ps=ps: e.copy_predicated(dst, mk, ps), t, tz, t_masks,
                                   tA[si])
                        tA[si] = t2
                    bank_free[i] = t2
                    done.append(t)
                if m > 1:
                    free[li % 2] = done[-1]
                if li + 2 < len(every):
                    ahead.append(factors(li + 2, every[li + 2]))
                if m > 1:
                    yield
            tA = [VE.last(), t_v[-1]]
            for h in range(HEADS):
                for c0 in range(0, NV, 2):
                    n = min(2, NV - c0)
                    i, fr = take("side")
                    for c in range(n):
                        vs = lambda j, h=h, c=c, c0=c0: v[:, j, h * dv + (c0 + c) * P:h * dv + (c0 + c + 1) * P]
                        PE.quiet(lambda e, i=i, c=c, h=h, vs=vs: e.matmul(
                            banks[i][:, c * T:(c + 1) * T], vs(0), A0[:, h, :], start=True, stop=False,
                            skip_group_check=True), tA, fr)
                        t = PE.do(lambda e, i=i, c=c, h=h, vs=vs: e.matmul(
                            banks[i][:, c * T + P:(c + 1) * T], vs(1), A1[:, h, :], start=False, stop=True,
                            skip_group_check=True), tA, fr)
                    o = oT[:, h * NV + c0:h * NV + c0 + n, :]
                    t = AC.do(lambda e, i=i, o=o, n=n: e.activation(
                        o, banks[i][:, 0:n * T].rearrange("p (c t) -> p c t", c=n), ACT.Copy), t, ztok)
                    bank_free[i] = t
            yield
            rs = lev[1][0]
            tr = []
            t_o = [AC.last(), PE.last()]
            for h in range(HEADS):
                i, fr = take("side")
                sqh = lev[0][h * NV // HEADS][:, h * NV % HEADS:h * NV % HEADS + NV, :]
                t1 = AC.do(lambda e, h=h, sqh=sqh: e.activation(sqh, oT[:, h * NV:(h + 1) * NV, :], ACT.Square), t_o)
                for c in range(NV):
                    f = lambda e, i=i, c=c, sqh=sqh: e.matmul(banks[i][:, 0:T], ones[:, :], sqh[:, c, :],
                                                     start=c == 0, stop=c == NV - 1)
                    t = (PE.do if c == NV - 1 else PE.quiet)(f, t1, fr)
                t = AC.do(lambda e, i=i, h=h: e.activation(rs[:, h, :], banks[i][:, 0:T], ACT.Sqrt,
                                                           bias=epsc[:, 0:1], scale=1.0 / dv), t)
                bank_free[i] = t
                tr.append(VE.do(lambda e, h=h: e.reciprocal(rs[:, h, :], rs[:, h, :]), t))
            result.append((rs, tr))
            yield

        b1 = Region()
        hq = sb("hq", [P, HEADS, T], stack=b1)
        hk = sb("hk", [P, HEADS, T], stack=b1)
        hb = sb("hb", [P, HEADS, T], stack=b1)
        hv = sb("hv", [P, TT, 512], stack=b1)
        hf = sb("hf", [P, HEADS, T], stack=b1)
        hg = hf
        aq = sb("aq", [P, HEADS, T], stack=b1)
        ak = sb("ak", [P, HEADS, T], stack=b1)
        av = sb("av", [P, TT, 512], stack=b1)
        mixT = sb("mixT", [P, KC, T], stack=b1)
        distc = sb("distc", [P, 384], stack=b1)
        t_dist = load(PO, "dist", distc[:, :], a["dist"], f0)
        win = lambda i: a["w_in"][0][:, i * 512:(i + 1) * 512]
        project(win(1), copy_T(hf, func=ACT.Sigmoid, wait=f0))
        t = AC.last()
        for h in range(HEADS):
            t2 = VE.do(lambda e, h=h: e.tensor_scalar(hf[:, h, :], hf[:, h, :], oml[:, h:h + 1], lbc[:, h:h + 1],
                                                      ALU.mult, ALU.add), t, t_lb)
        t2 = VE.do(lambda e: e.tensor_scalar(hf[:, :, :], hf[:, :, :], 1e-18, None, ALU.max), t2)
        VE.do(lambda e: e.tensor_scalar(hk[:, :, :], hf[:, :, :], -1.0, 1.0, ALU.mult, ALU.add), t2, f0)
        t = AC.do(lambda e: e.activation(hf[:, :, :], hf[:, :, :], ACT.Ln), VE.last())
        t_hb = VE.do(lambda e: e.tensor_tensor_scan(
            hb[:, :, :].rearrange("p h t -> p (h t)"), chainm[:, :], hf[:, :, :].rearrange("p h t -> p (h t)"),
            0.0, ALU.mult, ALU.add), t, t_chain, f0)
        project(win(0), copy_T(hq, wait=f0))
        t_hready = [t_hb, AC.last()]
        hst = Region(b1.at)
        h_rs, t_hv = [], []
        gen_h = gated("hg", hst, hq, hk, hv, hb, P, 1.0, mixT, t_hready, f0, t_hv, h_rs)

        done_da = {}
        t_a = {}

        def keep(name, evac):
            def kept(*args):
                t_a[name] = evac(*args)
                return t_a[name]
            return kept

        def diff_attention():
            S = [[sb(f"S{i}{m}", [P, 384], stack=hst) for m in range(2)] for i in range(2)]
            W = [sb(f"W{i}", [P, 384], stack=hst) for i in range(2)]
            WT = [sb(f"WT{i}", [P, 384], stack=hst) for i in range(2)]
            st = sb("dstat", [P, HEADS, 12], stack=hst)
            t_in = [t_a["q"], t_a["k"]]
            span = [(0, P), (P, 384)]
            sfree, wfree, wtfree = [None, None], [None, None], [None, None]
            t_w, t_wt = {}, {}

            def scores(h):
                slope = 2.0 ** (-8.0 * (h + 1) / HEADS)
                Sh, Wh = S[h % 2], W[h % 2]
                for m in range(2):
                    i, fr = take("side")
                    for j in range(TT):
                        a0, a1 = span[j]
                        f = lambda e, i=i, m=m, j=j, a0=a0, a1=a1: e.matmul(
                            banks[i][:, a0:a1], aq[64 * m:64 * m + 64, h, j * P:(j + 1) * P],
                            ak[64 * m:64 * m + 64, h, 0:a1 - a0], start=True, stop=True)
                        t = (PE.do if j == 1 else PE.quiet)(f, t_in, fr)
                    t = VE.do(lambda e, i=i, m=m: e.scalar_tensor_tensor(
                        out=Sh[m][:, :], in0=distc[:, :], scalar=-slope, in1=banks[i][:, 0:384],
                        op0=ALU.mult, op1=ALU.add), t, t_dist, sfree[h % 2])
                    bank_free[i] = t
                    for j in range(TT):
                        a0, a1 = span[j]
                        tr = VE.do(lambda e, m=m, j=j, a0=a0, a1=a1: e.tensor_reduce(
                            st[:, h, 2 * m + j:2 * m + j + 1], Sh[m][:, a0:a1], AXX, ALU.max), t)
                t = VE.do(lambda e: e.tensor_scalar(st[:, h, 0:4], st[:, h, 0:4], -1.0, None, ALU.mult), tr)
                for m in range(2):
                    for j in range(TT):
                        a0, a1 = span[j]
                        c = 2 * m + j
                        te = AC.do(lambda e, m=m, c=c, a0=a0, a1=a1: e.activation(
                            Sh[m][:, a0:a1], Sh[m][:, a0:a1], ACT.Exp, bias=st[:, h, c:c + 1],
                            accum_out=st[:, h, 4 + c:5 + c]), t)
                t = VE.do(lambda e: e.reciprocal(st[:, h, 8:12], st[:, h, 4:8]), te)
                t = VE.do(lambda e: e.tensor_scalar(st[:, h, 10:12], st[:, h, 10:12], neglam, None, ALU.mult),
                          t, t_lam)
                for j in range(TT):
                    a0, a1 = span[j]
                    t1 = VE.do(lambda e, j=j, a0=a0, a1=a1: e.tensor_scalar(
                        Wh[:, a0:a1], Sh[0][:, a0:a1], st[:, h, 8 + j:9 + j], None, ALU.mult), t, wfree[h % 2])
                    t1 = VE.do(lambda e, j=j, a0=a0, a1=a1: e.scalar_tensor_tensor(
                        out=Wh[:, a0:a1], in0=Sh[1][:, a0:a1], scalar=st[:, h, 10 + j:11 + j], in1=Wh[:, a0:a1],
                        op0=ALU.mult, op1=ALU.add), t1)
                sfree[h % 2] = t_w[h] = t1

            def turned(h):
                i, fr = take("side")
                for c in range(3):
                    f = lambda e, c=c: e.transpose(banks[i][:, c * P:(c + 1) * P], W[h % 2][:, c * P:(c + 1) * P],
                                                   ident[:, :])
                    t = (PE.do if c == 2 else PE.quiet)(f, t_w[h], fr)
                wfree[h % 2] = t
                t_wt[h] = AC.do(lambda e: e.activation(WT[h % 2][:, :], banks[i][:, 0:384], ACT.Copy), t,
                                wtfree[h % 2])
                bank_free[i] = t_wt[h]

            def values(h):
                i, fr = take("side")
                PE.quiet(lambda e: e.matmul(
                    banks[i][:, 0:T], av[:, 0, h * P:(h + 1) * P], WT[h % 2][:, 0:T], start=True, stop=False,
                    skip_group_check=True), t_wt[h], fr, t_a["v"])
                t = PE.do(lambda e: e.matmul(
                    banks[i][:, P:T], av[:, 1, h * P:(h + 1) * P], WT[h % 2][:, T:384], start=False, stop=True,
                    skip_group_check=True))
                wtfree[h % 2] = t
                t = AC.do(lambda e: e.activation(mixT[:, 4 + h, :], banks[i][:, 0:T], ACT.Copy), t, f0)
                bank_free[i] = t
                t_sq[h] = AC.do(lambda e: e.activation(aq[:, h, :], mixT[:, 4 + h, :], ACT.Square), t)

            def head_norm(h):
                i, fr = take("side")
                t = PE.do(lambda e: e.matmul(banks[i][:, 0:T], ones[:, :], aq[:, h, :], start=True, stop=True),
                          t_sq[h], fr)
                t = AC.do(lambda e: e.activation(ak[:, h, :], banks[i][:, 0:T], ACT.Sqrt, bias=epsc[:, 0:1],
                                                 scale=1.0 / P), t)
                bank_free[i] = t
                t = VE.do(lambda e: e.reciprocal(ak[:, h, :], ak[:, h, :]), t)
                done_da[h] = VE.do(lambda e: e.scalar_tensor_tensor(
                    out=mixT[:, 4 + h, :], in0=mixT[:, 4 + h, :], scalar=subs, in1=ak[:, h, :],
                    op0=ALU.mult, op1=ALU.mult), t, t_subs)

            t_sq = {}
            subs = small[:, 29:30]
            t_subs = VE.do(lambda e: e.tensor_scalar(subs, col("subln"), 1.0 - LAMBDA_INIT, None, ALU.mult))
            for step in range(HEADS + 3):
                if 2 <= step < HEADS + 2:
                    values(step - 2)
                if 1 <= step <= HEADS:
                    turned(step - 1)
                if step < HEADS:
                    scores(step)
                for h in {HEADS: (0, 1), HEADS + 1: (2,), HEADS + 2: (3,)}.get(step, ()):
                    head_norm(h)
                yield

        res_tok = {}
        hold = []

        def out_of_hgrn():
            rs, tr = h_rs[0]
            for h in range(HEADS):
                t = VE.do(lambda e, h=h: e.scalar_tensor_tensor(
                    out=mixT[:, h, :], in0=mixT[:, h, :], scalar=col("gn"), in1=rs[:, h, :],
                    op0=ALU.mult, op1=ALU.mult), tr[h])
                t = VE.do(lambda e, h=h: e.tensor_tensor(mixT[:, h, :], mixT[:, h, :], hg[:, h, :], ALU.mult), t,
                          t_a["g"])
                split_x(h, mixT[:, h, :], t)
            yield from steps(a["w_out"][0][0:512, :], None, kc=4, cols=D, parts=2, part=0, hold=hold)

        weave([steps(win(4), keep("q", copy_T(aq, scale=0.125, wait=f0))),
               steps(win(5), keep("k", copy_T(ak, wait=f0))),
               steps(win(6), keep("v", copy_tok(av, 0, f0)), tok=True),
               steps(win(2), copy_tok(hv, 0, f0, t_hv), tok=True),
               steps(win(3), keep("g", copy_T(hg, func=ACT.Silu, wait=t_hb))),
               out_of_hgrn()],
              (0, modulations(range(4, 10))), (-1, gen_h), (4, diff_attention()))
        t_mod = VE.last()
        t_scl2 = VE.do(lambda e: e.scalar_tensor_tensor(
            out=scl[:, 8:16], in0=modc[:, 32:40], scalar=1.0, in1=pcol[:, ROWS["norm2"]:ROWS["norm2"] + 8],
            op0=ALU.add, op1=ALU.mult), t_mod)

        def residual(gate, base):
            def evac(bk, ch, n, t):
                for c in range(n):
                    k = base + ch + c
                    t2 = VE.do(lambda e, bk=bk, c=c, k=k: e.scalar_tensor_tensor(
                        out=hT[:, k, :], in0=banks[bk][:, c * T:(c + 1) * T], scalar=modc[:, gate + k:gate + k + 1],
                        in1=hT[:, k, :], op0=ALU.mult, op1=ALU.add), t, t_mod)
                    res_tok[k] = t2
                return t2
            return evac

        for k in range(4, KC):
            split_x(k, mixT[:, k, :], done_da[k - 4])
        project(a["w_out"][0][512:D, :], residual(16, 0), kc=4, cols=D, parts=2, part=1, hold=hold, xo=4)
        t_rstd = norm_scale(hT, lambda k: res_tok[k])
        norm_apply(hT, lambda k: scl[:, 8 + k:9 + k], lambda k: modc[:, 24 + k:25 + k], t_rstd, t_scl2)
        f1 = fence()

        b2 = Region()
        hid = sb("hid", [P, FFC, T], stack=b2)
        t_hid = {}
        t_g = {}

        def evac_up(c0):
            def evac(bk, ch, m, t):
                o = hid[:, c0 // P + ch:c0 // P + ch + m, :]
                t = VE.do(lambda e: e.tensor_tensor(
                    o, banks[bk][:, 0:m * T].rearrange("p (c t) -> p c t", c=m), o, ALU.mult), t, t_g[c0])
                for x in range(m):
                    t_hid[c0 // P + ch + x] = t
                return t
            return evac

        def split_hid(k0, kn):
            for k in range(kn):
                split_x(k, hid[:, k0 + k, :], t_hid[k0 + k])

        def gate_up():
            for c0 in range(0, FF, 512):
                n = min(512, FF - c0)
                yield from steps(a["w_ffn_gate"][0][:, c0:c0 + n], copy_T(hid, c0 // P, func=ACT.Silu, wait=f1), cols=n)
                t_g[c0] = AC.last()
                yield from steps(a["w_ffn_up"][0][:, c0:c0 + n], evac_up(c0), cols=n,
                                 before=(lambda: split_hid(0, 8)) if c0 + n == FF else None)

        weave([gate_up()], (4, modulations(range(10, 12))))
        t_mod = VE.last()
        sq2 = sb("sq2", [P, KC, T], stack=b2)
        t_wm = VE.do(lambda e: e.tensor_tensor(wmix[:, 0, :], pcol[:, ROWS["fin1"]:ROWS["fin1"] + 8],
                                               pcol[:, ROWS["mixn"]:ROWS["mixn"] + 8], ALU.mult))
        t_wm = VE.do(lambda e: e.tensor_tensor(wmix[:, 1, :], pcol[:, ROWS["fin1"]:ROWS["fin1"] + 8],
                                               pcol[:, ROWS["fin1"]:ROWS["fin1"] + 8], ALU.mult))
        got_sums = []

        def first_sums():
            got_sums[:] = sums(hT, [scratch, sq2], lambda k: [res_tok[k], t_wm], wmix[:, 1, :], range(4))[0]

        hold = [[], []]
        for part, (k0, kn) in enumerate([(0, 8), (8, 8), (16, 6)]):
            if part:
                split_hid(k0, kn)
            for c in range(2):
                project(a["w_ffn_down"][0][k0 * P:(k0 + kn) * P, c * 512:(c + 1) * 512], residual(40, 4 * c), kc=kn,
                        parts=3, part=part, hold=hold[c], before=first_sums if part == 2 and c == 1 else None)
        t_sums = sums(hT, [scratch, sq2], lambda k: [res_tok[k], t_wm], wmix[:, 1, :], range(4, KC), got_sums)[1]
        (i1, _), (i2, _) = got_sums
        t = t_sums
        t_r1 = AC.do(lambda e, i1=i1: e.activation(r1[:, :], banks[i1][:, 0:T], ACT.Copy), t)
        bank_free[i1] = t_r1
        t_rs2 = VE.do(lambda e, i2=i2: e.scalar_tensor_tensor(out=rstd[:, :], in0=r1[:, :], scalar=EPS,
                                                           in1=banks[i2][:, 0:T], op0=ALU.mult, op1=ALU.add), t_r1)
        t = AC.do(lambda e: e.activation(rstd[:, :], rstd[:, :], ACT.Sqrt, bias=eps2[:, 0:1], scale=1.0 / D), t_rs2)
        bank_free[i2] = t_rs2
        t = VE.do(lambda e: e.reciprocal(rstd[:, :], rstd[:, :]), t)
        t_u = {}
        for k in range(KC + 2):
            if k < KC:
                t_u[k] = VE.do(lambda e, k=k: e.scalar_tensor_tensor(
                    out=scratch[:, k, :], in0=hT[:, k, :], scalar=wmix[:, 0, k:k + 1], in1=rstd[:, :],
                    op0=ALU.mult, op1=ALU.mult), t, t_wm)
            if k >= 2:
                split_x(k - 2, scratch[:, k - 2, :], t_u[k - 2])
        t_h = []

        def final_norm():
            t = AC.do(lambda e: e.activation(r1[:, :], r1[:, :], ACT.Sqrt, bias=epsc[:, 0:1], scale=1.0 / D), t_rs2)
            t = VE.do(lambda e: e.reciprocal(r1[:, :], r1[:, :]), t)
            for k in range(KC):
                t1 = VE.do(lambda e, k=k: e.scalar_tensor_tensor(
                    out=hT[:, k, :], in0=hT[:, k, :], scalar=col("fin1", k), in1=r1[:, :],
                    op0=ALU.mult, op1=ALU.mult), t, t_u[k])
                if k % 2:
                    yield
            t_h.append(t1)
        f2 = fence()

        outer = Region()
        w2 = a["w_in_2"][0]
        rq = sb("rq", [P, 8, T], stack=outer)
        rk = sb("rk", [P, 8, T], stack=outer)
        rv = sb("rv", [P, TT, 2048], stack=outer)
        oG = sb("oG", [P, 8, T], stack=outer)
        b3 = Region(outer.at)
        gq = sb("gq", [P, HEADS, T], stack=b3)
        gk = sb("gk", [P, HEADS, T], stack=b3)
        gb = sb("gb", [P, HEADS, T], stack=b3)
        gv = sb("gv", [P, TT, 1024], stack=b3)
        gd = sb("gd", [16, T], stack=b3)
        gup = sb("gup", [16, 512], stack=b3)
        z = oG[:, 0:4, :]
        t_gup = load(PO, "gup", gup[:, :], a["gla_gk_up_2"][0], f2)

        def evac_gd(bk, ch, n, t):
            return AC.do(lambda e: e.activation(gd[:, :], banks[bk][0:16, 0:T], ACT.Copy), t, f2)
        project(w2[:, 3072:3200], evac_gd, cols=P)
        t = AC.last()
        t_gd = t
        project(w2[:, 0:512], copy_T(gq, scale=float(P) ** -0.5, wait=f2))
        gbf = [None] * 2
        for hh in range(2):
            i, fr = take("side")
            for c in range(2):
                h = 2 * hh + c
                t = PE.do(lambda e, i=i, c=c, h=h: e.matmul(banks[i][:, c * T:(c + 1) * T],
                                                            gup[:, h * P:(h + 1) * P], gd[:, :], start=True,
                                                            stop=True), t_gd, t_gup, fr)
            for c in range(2):
                h = 2 * hh + c
                t2 = AC.do(lambda e, i=i, c=c, h=h: e.activation(z[:, h, :], banks[i][:, c * T:(c + 1) * T],
                                                                 ACT.Identity, bias=col("gkb", h)), t, f2)
            bank_free[i] = t2
        t_gready = []
        t_z = t2

        def log_decay():
            t = AC.do(lambda e: e.activation(gb[:, :, :], z[:, :, :], ACT.Abs), t_z, f2)
            t = AC.do(lambda e: e.activation(gb[:, :, :], gb[:, :, :], ACT.Exp, scale=-1.0), t)
            yield
            t = AC.do(lambda e: e.activation(gb[:, :, :], gb[:, :, :], ACT.Ln, bias=ones[:, 0:1]), t)
            yield
            t = VE.do(lambda e: e.scalar_tensor_tensor(out=z[:, :, :], in0=z[:, :, :], scalar=0.0, in1=gb[:, :, :],
                                                       op0=ALU.min, op1=ALU.subtract), t)
            t_gready.append(VE.do(lambda e: e.tensor_tensor_scan(
                gb[:, :, :].rearrange("p h t -> p (h t)"), chainm[:, :], z[:, :, :].rearrange("p h t -> p (h t)"),
                0.0, ALU.mult, ALU.add), t))

        def keys():
            yield from steps(w2[:, 512:1024], copy_T(gk, wait=f2))
            t_gready.append(AC.last())
        gst = Region(b3.at)
        g_rs, t_gv = [], []
        gen_g = gated("gl", gst, gq, gk, gv, gb, 256, 1.0 / 16.0, oG, t_gready, f2, t_gv, g_rs)
        GG, RQ, RK, RV, RG, MA, MB = 2048, 3088, 4112, 5136, 7184, 9232, 10256
        weave([keys()] + [steps(w2[:, 1024 + c * 512:1536 + c * 512], copy_tok(gv, c * 512, f2, t_gv), tok=True) for c in range(2)]
              + [steps(w2[:, RQ + c * 512:RQ + (c + 1) * 512], copy_T(rq, 4 * c, wait=f2), step=2)
                 for c in range(2)]
              + [steps(w2[:, RK + c * 512:RK + (c + 1) * 512],
                         copy_T(rk, 4 * c, scale=1.0 / 16.0, wait=f2), step=2) for c in range(2)],
              (-1, log_decay()), (2, gen_g))
        rs, t = g_rs[0]
        for c in range(2):
            t = VE.do(lambda e, c=c: e.scalar_tensor_tensor(
                out=oG[:, c::2, :], in0=oG[:, c::2, :], scalar=col("glan", c), in1=rs[:, :, :],
                op0=ALU.mult, op1=ALU.mult), t)
        t_oGn = t
        fg = fence()

        merged = sb("merged", [P, KC, T], stack=Region(ARENA - KC * T))
        mgb = sb("mgb", [P, KC, T], stack=Region(KC * T))
        xtok2 = sb("xtok2", [P, TT, D], stack=Region())
        b4 = Region(outer.at)
        oR = sb("oR", [P, 16, T], stack=b4)
        gtmp = [sb(f"gtmp{i}", [P, 512], stack=b4)[:, :] for i in range(2)]
        tmpfree = [fg, fg]
        rot = [sb(f"rot{i}", [P, HEADS, T], stack=b4) for i in range(2)]
        cosT = sb("cosT", [P, T], stack=b4)
        sinT = sb("sinT", [P, T], stack=b4)
        posi = sb("posi", [P, T], I32, stack=b4)
        mean = [sb(f"mean{i}", [P, T], stack=Region(b4.at - T + i * T)) for i in range(2)]
        ang = sb("ang", [P, T], stack=b4)
        dec = sb("dec", [P, HEADS, 384], stack=b4)
        AT = [sb(f"ret_A{i}", [P, 384], stack=b4) for i in range(2)]
        theta = sb("theta", [P, 1], stack=b4)
        assert b4.at <= ARENA - KC * T
        t_pos = load(PO, "pos", posi[:, :], a["positions_2"].partition_broadcast(P).rearrange("p o t -> p (o t)"), fg)
        t_th = load(PO, "theta", theta[:, :], a["theta"], fg)
        t_dec = load(PO, "dec", dec[:, :, :], a["decay"], fg)
        t_rot = []

        def rotate():
            t = VE.do(lambda e: e.tensor_copy(ang[:, :], posi[:, :]), t_pos, fg)
            t_ang = VE.do(lambda e: e.tensor_scalar(ang[:, :], ang[:, :], theta[:, 0:1], None, ALU.mult), t, t_th)
            MAGIC = 12582912.0
            for dst, shift in ((sinT, 0.0), (cosT, 0.25)):
                kt = rot[0][:, 0, :]
                t = VE.do(lambda e, kt=kt, shift=shift: e.tensor_scalar(
                    kt, ang[:, :], float(1.0 / (2 * np.pi)), shift, ALU.mult, ALU.add), t_ang, t, fg)
                t = VE.do(lambda e, kt=kt: e.tensor_scalar(kt, kt, MAGIC, None, ALU.add), t)
                t = VE.do(lambda e, kt=kt: e.tensor_scalar(kt, kt, -MAGIC, None, ALU.add), t)
                src = ang
                yield
                for part in TWO_PI_PARTS:
                    t = VE.do(lambda e, kt=kt, part=part, src=src, dst=dst: e.scalar_tensor_tensor(
                        out=dst[:, :], in0=kt, scalar=-part, in1=src[:, :], op0=ALU.mult, op1=ALU.add), t)
                    src = dst
                t = VE.do(lambda e, dst=dst, shift=shift: e.tensor_scalar(
                    dst[:, :], dst[:, :], float(2 * np.pi * shift), None, ALU.add), t)
                t = VE.do(lambda e, dst=dst: e.tensor_scalar(
                    dst[:, :], dst[:, :], 3.1415925, -3.1415925, ALU.min, ALU.max), t)
                t = AC.do(lambda e, dst=dst: e.activation(dst[:, :], dst[:, :], ACT.Sin), t)
                yield
            t_cs = t
            cb = cosT[:, :].unsqueeze(1).broadcast_to([P, HEADS, T])
            sbb = sinT[:, :].unsqueeze(1).broadcast_to([P, HEADS, T])
            tr = None
            for x in (rq, rk):
                ev, od = x[:, 0::2, :], x[:, 1::2, :]
                t1 = VE.do(lambda e, ev=ev: e.tensor_tensor(rot[0][:, :, :], ev, sbb, ALU.mult), t_cs, VE.last())
                t2 = PO.do(lambda e, od=od: e.tensor_tensor(rot[1][:, :, :], od, sbb, ALU.mult), t_cs, tr, fg)
                t3 = VE.do(lambda e, ev=ev: e.tensor_tensor(ev, ev, cb, ALU.mult), t1, fg)
                yield
                t4 = VE.do(lambda e, od=od: e.tensor_tensor(od, od, cb, ALU.mult), t2)
                VE.do(lambda e, ev=ev: e.tensor_tensor(ev, ev, rot[1][:, :, :], ALU.subtract), t3, t2)
                tr = VE.do(lambda e, od=od: e.tensor_tensor(od, od, rot[0][:, :, :], ALU.add), t4, t1)
                yield
            t_rot.append(tr)

        rdone = {}

        def retention(lane):
            A, mn, sq = AT[lane], mean[lane], rot[lane]
            afree = None
            for h in range(lane, HEADS, 2):
                i, fr = take("side")
                for c in range(2):
                    PE.quiet(lambda e, i=i, c=c, h=h: e.matmul(
                        banks[i][:, 0:T], rk[:, 2 * h + c, 0:P], rq[:, 2 * h + c, :], start=c == 0, stop=c == 1),
                        t_rot, fr)
                for c in range(2):
                    t = (PE.do if c else PE.quiet)(lambda e, i=i, c=c, h=h: e.matmul(
                        banks[i][:, T:384], rk[:, 2 * h + c, P:T], rq[:, 2 * h + c, P:T], start=c == 0, stop=c == 1))
                t = VE.do(lambda e, i=i, h=h: e.tensor_tensor(A[:, :], banks[i][:, 0:384], dec[:, h, :], ALU.mult),
                          t, t_dec, afree)
                bank_free[i] = t
                yield
                for c0 in range(0, 4, 2):
                    i, fr = take("side")
                    for c in range(2):
                        vc = slice(h * 512 + (c0 + c) * P, h * 512 + (c0 + c + 1) * P)
                        PE.quiet(lambda e, i=i, c=c, vc=vc: e.matmul(
                            banks[i][:, c * T:(c + 1) * T], rv[:, 0, vc], A[:, 0:T], start=True, stop=False,
                            skip_group_check=True), t, fr, t_rv[h])
                        t2 = PE.do(lambda e, i=i, c=c, vc=vc: e.matmul(
                            banks[i][:, c * T + P:(c + 1) * T], rv[:, 1, vc], A[:, T:384], start=False, stop=True,
                            skip_group_check=True))
                    afree = t2
                    t2 = AC.do(lambda e, i=i, c0=c0, h=h: e.activation(
                        oR[:, 4 * h + c0:4 * h + c0 + 2, :], banks[i][:, :].rearrange("p (c t) -> p c t", c=2),
                        ACT.Copy), t2, fg)
                    bank_free[i] = t2
                yield
                o = oR[:, 4 * h:4 * h + 4, :]
                i, fr = take("side")
                for c in range(4):
                    t = (PE.do if c == 3 else PE.quiet)(lambda e, i=i, c=c, h=h: e.matmul(
                        banks[i][:, 0:T], ones[:, :], oR[:, 4 * h + c, :], start=c == 0, stop=c == 3), t2, fr)
                t = AC.do(lambda e, i=i: e.activation(mn[:, :], banks[i][:, 0:T], ACT.Copy, scale=1.0 / 512), t,
                          t_rot, rdone.get(h - 2))
                bank_free[i] = t
                t = VE.do(lambda e, o=o: e.tensor_tensor(
                    o, o, mn[:, :].unsqueeze(1).broadcast_to([P, 4, T]), ALU.subtract), t)
                t2 = AC.do(lambda e, o=o: e.activation(sq[:, :, :], o, ACT.Square), t, t_rot, PE.last())
                yield
                i, fr = take("side")
                for c in range(4):
                    t = (PE.do if c == 3 else PE.quiet)(lambda e, i=i, c=c: e.matmul(
                        banks[i][:, 0:T], ones[:, :], sq[:, c, :], start=c == 0, stop=c == 3), t2, fr)
                t = AC.do(lambda e, i=i: e.activation(mn[:, :], banks[i][:, 0:T], ACT.Sqrt, bias=epsc[:, 0:1],
                                                      scale=1.0 / 512), t)
                bank_free[i] = t
                t = VE.do(lambda e: e.reciprocal(mn[:, :], mn[:, :]), t)
                for c in range(4):
                    t2 = VE.do(lambda e, c=c, h=h: e.scalar_tensor_tensor(
                        out=oR[:, 4 * h + c, :], in0=oR[:, 4 * h + c, :], scalar=col("retn", 4 * h + c),
                        in1=mn[:, :], op0=ALU.mult, op1=ALU.mult), t)
                rdone[h] = t2
                yield

        def evac_gate(dst, base, t_in, func, done):
            def evac(bk, ch, n, t):
                j = (ch // 2) % 2
                t = AC.do(lambda e: e.activation(gtmp[j], banks[bk][:, 0:n * T], func), t, tmpfree[j])
                o = dst[:, base + ch:base + ch + n, :]
                tmpfree[j] = VE.do(lambda e: e.tensor_tensor(o, o, gtmp[j].rearrange("p (c t) -> p c t", c=n),
                                                             ALU.mult), t, t_in)
                for x in range(n):
                    done[base + ch + x] = tmpfree[j]
                return t
            return evac

        t_rv, t_oG, t_mga, t_ya = {}, {}, {}, {}

        def evac_rv(c):
            def evac(bk, j, t):
                t_rv[c] = AC.do(lambda e: e.activation(rv[:, j, c * 512:(c + 1) * 512], banks[bk][:, :], ACT.Copy), t, f2)
                return t_rv[c]
            return evac

        def evac_ya(base):
            def evac(bk, ch, n, t):
                o = merged[:, base + ch:base + ch + n, :]
                return VE.do(lambda e: e.tensor_tensor(o, banks[bk][:, 0:n * T].rearrange("p (c t) -> p c t", c=n),
                                                       o, ALU.mult), t, t_mga[0])
            return evac

        def gate_a():
            for c in range(2):
                yield from steps(w2[:, MA + c * 512:MA + (c + 1) * 512],
                                   copy_T(merged, 4 * c, func=ACT.Sigmoid, wait=fg))
            t_mga[0] = AC.last()

        weave([steps(w2[:, RV + c * 512:RV + (c + 1) * 512], evac_rv(c), tok=True) for c in range(4)]
              + [steps(w2[:, GG + c * 512:GG + (c + 1) * 512], evac_gate(oG, 4 * c, t_oGn, ACT.Silu, t_oG))
                 for c in range(2)]
              + [gate_a()],
              (-1, rotate()), (7, retention(0)), (8, retention(1)), (9, final_norm()))
        f3 = fence()
        t_oR = {}
        for c in range(2):
            project(w2[:, MB + c * 512:MB + (c + 1) * 512], copy_T(mgb, 4 * c, func=ACT.Sigmoid, wait=f3))
        t_mgb = AC.last()
        def split_all(x, k0, ready, ks=range(KC)):
            for k in ks:
                split_x(k, x[:, k0 + k, :], ready[k0 + k])

        for c in range(4):
            project(w2[:, RG + c * 512:RG + (c + 1) * 512], evac_gate(oR, 4 * c, rdone[c], ACT.Silu, t_oR),
                    before=(lambda: split_all(oG, 0, t_oG)) if c == 3 else None)
        for c in range(2):
            project(a["w_branch_gla_2"][0][:, c * 512:(c + 1) * 512], evac_ya(4 * c),
                    before=(lambda: split_all(oR, 0, t_oR)) if c else None)
        t_merged = {}
        def evac_yb(base):
            def evac(bk, ch, n, t):
                o = merged[:, base + ch:base + ch + n, :]
                g = mgb[:, base + ch:base + ch + n, :]
                t = VE.do(lambda e: e.tensor_tensor(g, banks[bk][:, 0:n * T].rearrange("p (c t) -> p c t", c=n),
                                                    g, ALU.mult), t, t_mgb)
                t2 = VE.do(lambda e: e.tensor_tensor(o, o, g, ALU.add), t)
                for x in range(n):
                    t_merged[base + ch + x] = t2
                return t
            return evac
        t_x2 = to_tokens(hT, xtok2, t_h, f3)
        hold = [[], []]
        for part in range(2):
            if part:
                split_all(oR, KC, t_oR)
            for c in range(2):
                project(a["w_branch_ret_2"][0][part * D:(part + 1) * D, c * 512:(c + 1) * 512], evac_yb(4 * c),
                        parts=2, part=part, hold=hold[c],
                        before=(lambda: split_all(merged, 0, t_merged, range(4))) if part and c else None)
        split_all(merged, 0, t_merged, range(4, KC))

        b5 = Region(4096)
        rw = sb("rw", [P, KC, 36], stack=b5)
        rb = sb("rb", [P, 36], stack=b5)
        wrow = sb("wrow", [P, D], stack=b5)
        frow = sb("frow", [P, D], stack=b5)
        tri = sb("tri", [P, P], stack=b5)
        iota = sb("iota", [P, CAP], stack=b5)
        assert b5.at <= 8192
        t_rw = [load(PO, f"rw{g}", rw[:, :, 4 + 8 * g:12 + 8 * g], a["router_expert_w_2"][0, g].rearrange(
            "(k p) e -> p k e", p=P), f3) for g in range(NGRP)]
        t_rw.append(load(PO, "rwg", rw[:, :, 0:4], a["router_group_w_2"][0].rearrange("(k p) e -> p k e", p=P), f3))
        t_rb = [load(PO, "rbg", rb[:, 0:4], a["router_group_b_2"].partition_broadcast(P).rearrange("p o e -> p (o e)"), f3),
                load(PO, "rbe", rb[:, 4:36], a["router_expert_b_2"].rearrange("o g e -> o (g e)").partition_broadcast(
                    P).rearrange("p o e -> p (o e)"), f3)]
        t_wr = load(PO, "wrow", wrow[:, :], a["norm_ffn_w_2"].partition_broadcast(P).rearrange("p o e -> p (o e)"), f3)
        t_fr = load(PO, "frow", frow[:, :], a["norm_final_w_2"].rearrange("(o e) -> o e", o=1).partition_broadcast(
            P).rearrange("p o e -> p (o e)"), f3)
        t_tri = load(PO, "tri", tri[:, :], a["tri"], f3)
        t_io = load(PO, "iota", iota[:, :], a["iota"], f3)

        f4 = fence()
        utok = sb("utok", [P, TT, D], stack=b5)
        lg = sb("lg", [P, TT, 36], stack=b5)
        ss = sb("ss", [P, 8], stack=b5)
        for n in range(2):
            ring[4 + 2 * n:4 + 2 * n] = new_slots(Region(ARENA - (3 - n) * KC * 512), f4)

        def evac_res(c):
            def evac(bk, j, t):
                o = xtok2[:, j, c * 512:(c + 1) * 512]
                t = VE.do(lambda e: e.tensor_tensor(o, banks[bk][:, :], o, ALU.add), t, t_x2)
                t_ss[2 * j + c] = AC.do(lambda e: e.activation(
                    utok[:, j, c * 512:(c + 1) * 512], o, ACT.Square, accum_out=ss[:, 2 * j + c:2 * j + c + 1]), t, f4)
                return t
            return evac
        t_ss = {}
        for c in range(2):
            if c:
                AC.do(lambda e: e.activation(small[:, 40:41], epsc[:, 0:1], ACT.Sqrt))
            project(a["w_out_2"][0][:, c * 512:(c + 1) * 512], evac_res(c), tok=True)
        f5 = fence()
        ring += new_slots(Region(ARENA - KC * 512), f5)
        split_memory.close()
        yo = [sb(f"yo{i}", [P, D]) for i in range(2)]
        for n in range(2):
            ring += new_slots(None, f5)
        uTe = hT
        for j in range(TT):
            sj = ss[:, 4 + j:5 + j]
            t = VE.do(lambda e, j=j, sj=sj: e.tensor_tensor(sj, ss[:, 2 * j:2 * j + 1], ss[:, 2 * j + 1:2 * j + 2],
                                                            ALU.add), t_ss[2 * j], t_ss[2 * j + 1])
            t = AC.do(lambda e, sj=sj: e.activation(sj, sj, ACT.Sqrt, bias=epsc[:, 0:1], scale=1.0 / D), t)
            t = VE.do(lambda e, sj=sj: e.reciprocal(sj, sj), t)
            for half in range(2):
                c = slice(half * 512, (half + 1) * 512)
                t2 = VE.do(lambda e, j=j, sj=sj, c=c: e.scalar_tensor_tensor(
                    out=utok[:, j, c], in0=xtok2[:, j, c], scalar=sj, in1=wrow[:, c],
                    op0=ALU.mult, op1=ALU.mult), t, t_wr)
                i, fr = take("side")
                for k in range(4):
                    f = lambda e, i=i, j=j, k=k, half=half: e.transpose(
                        banks[i][:, k * P:(k + 1) * P], utok[:, j, (4 * half + k) * P:(4 * half + k + 1) * P],
                        ident[:, :])
                    t3 = (PE.do if k == 3 else PE.quiet)(f, t2, fr)
                t3 = AC.do(lambda e, i=i, j=j, half=half: e.activation(
                    uTe[:, 4 * half:4 * half + 4, j * P:(j + 1) * P],
                    banks[i][:, :].rearrange("p (k t) -> p k t", k=4), ACT.Copy), t3)
                bank_free[i] = t3
        t_utok = t2
        early = Region(b5.at)
        wpT = [sb(f"wpT{i}", [P, T], stack=b5) for i in range(2)]
        lgT = wpT[1]
        i, fr = take("side")
        for k in range(KC):
            f = lambda e, i=i, k=k: e.matmul(banks[i][0:36, 0:T], rw[:, k, :], uTe[:, k, :], start=k == 0,
                                             stop=k == KC - 1)
            t = (PE.do if k == KC - 1 else PE.quiet)(f, t3, t_rw, fr)
        t = AC.do(lambda e, i=i: e.activation(lgT[0:36, :], banks[i][0:36, 0:T], ACT.Copy), t, f4)
        bank_free[i] = t
        i, fr = take("side")
        for j in range(TT):
            t = PE.do(lambda e, i=i, j=j: e.transpose(banks[i][:, j * 36:(j + 1) * 36], lgT[0:36, j * P:(j + 1) * P],
                                                      ident[0:36, 0:36]), t, fr)
        t = VE.do(lambda e, i=i: e.tensor_tensor(
            lg[:, :, :], banks[i][:, 0:72].rearrange("p (j e) -> p j e", j=TT),
            rb[:, :].unsqueeze(1).broadcast_to([P, TT, 36]), ALU.add), t, t_rb)
        bank_free[i] = t

        rt = sb("rt", [P, TT, 96], stack=b5)
        R = lambda x, n: rt[:, :, x:x + n]

        def first_max(src, n, onehot, mxo, tmp, after):
            t = VE.do(lambda e: e.tensor_reduce(mxo, src, AXX, ALU.max), after)
            t = VE.do(lambda e: e.tensor_tensor(onehot, src, mxo.broadcast_to([P, TT, n]), ALU.is_lt), t)
            t = VE.do(lambda e: e.scalar_tensor_tensor(
                out=onehot, in0=onehot, scalar=1000.0, in1=iota[:, 0:n].unsqueeze(1).broadcast_to([P, TT, n]),
                op0=ALU.mult, op1=ALU.add), t, t_io)
            t = VE.do(lambda e: e.tensor_reduce(tmp, onehot, AXX, ALU.min), t)
            return VE.do(lambda e: e.tensor_tensor(onehot, onehot, tmp.broadcast_to([P, TT, n]), ALU.is_equal), t)

        gmax, goh, tmp1, eg, gsum = R(0, 1), R(1, 4), R(5, 1), R(6, 4), R(10, 1)
        el, m1, oh1, m2, oh2 = R(11, 8), R(19, 1), R(20, 8), R(28, 1), R(29, 8)
        e2, w12, el2, sel = R(37, 1), R(38, 2), R(40, 8), R(48, 32)
        two = 2 * TT
        d12 = sb("d12", [P, TT, 2, NE], stack=b5)
        dpos = sb("dpos", [P, TT, 2, NE], stack=early)
        pair = sb("pair", [P, two, NPAIR], stack=b5)
        wpair = sb("wpair", [P, two, NPAIR], stack=b5)
        par = sb("par", [P, two, 2], stack=b5)
        place = sb("place", [P, two, 1], stack=b5)
        ph = sb("ph", [P, two, CAP], stack=early)
        inpair = sb("inpair", [P, two, 2, CAP], stack=b5)
        pos = sb("pos", [P, TT, NE], stack=b5)
        isover = sb("isover", [P, TT, NE], stack=b5)
        wov = sb("wov", [P, TT, NE], stack=b5)
        over = sb("over", [P, 4], stack=b5)
        wcol = sb("wcol", [P, TT, 1], stack=b5)
        gl = lg[:, :, 0:4]
        t_g = first_max(gl, 4, goh, gmax, tmp1, t)
        eo = lg[:, :, 4:36].rearrange("p j (g x) -> p j g x", g=NGRP)
        t = VE.do(lambda e: e.tensor_tensor(dpos[:, :, 0, :].rearrange("p j (g x) -> p j g x", g=NGRP), eo,
                                            goh.unsqueeze(3).broadcast_to([P, TT, NGRP, EPG]), ALU.mult), t_g)
        t = VE.do(lambda e: e.tensor_reduce(el.unsqueeze(3), dpos[:, :, 0, :].rearrange("p j (g x) -> p j x g", g=NGRP),
                                            AXX, ALU.add), t)
        t = first_max(el, 8, oh1, m1, tmp1, t)
        t = VE.do(lambda e: e.scalar_tensor_tensor(out=el2, in0=oh1, scalar=-3.0e38, in1=el,
                                                   op0=ALU.mult, op1=ALU.add), t)
        t = first_max(el2, 8, oh2, m2, tmp1, t)
        for r, oh in enumerate((oh1, oh2)):
            t = VE.do(lambda e, r=r, oh=oh: e.tensor_tensor(
                d12[:, :, r, :].rearrange("p j (g x) -> p j g x", g=NGRP),
                oh.unsqueeze(2).broadcast_to([P, TT, NGRP, EPG]),
                goh.unsqueeze(3).broadcast_to([P, TT, NGRP, EPG]), ALU.mult), t)
        t = VE.do(lambda e: e.tensor_tensor(sel, d12[:, :, 0, :], d12[:, :, 1, :], ALU.add), t)
        i, fr = take("side")
        PE.quiet(lambda e, i=i: e.matmul(banks[i][:, 0:2 * NE], tri[:, :], sel, start=True, stop=False,
                                         skip_group_check=True), t, t_tri, fr)
        t1 = PE.do(lambda e, i=i: e.matmul(banks[i][:, NE:2 * NE], ones[:, :], sel[:, 0, :], start=False, stop=True,
                                           skip_group_check=True))
        dv = d12[:, :, :, :].rearrange("p j r e -> p (j r) e")
        VE.do(lambda e: e.tensor_reduce(pair[:, :, :].unsqueeze(3), dv.rearrange("p a (q b) -> p a q b", b=2), AXX,
                                        ALU.add), t)
        t = VE.do(lambda e: e.tensor_reduce(par[:, :, :].unsqueeze(3), dv.rearrange("p a (q b) -> p a b q", b=2), AXX,
                                            ALU.add), t)
        t2 = VE.do(lambda e, i=i: e.tensor_tensor(
            dpos[:, :, :, :], d12[:, :, :, :], banks[i][:, 0:2 * NE].rearrange("p (j e) -> p j e", j=TT).unsqueeze(
                2).broadcast_to([P, TT, 2, NE]), ALU.mult), t1)
        bank_free[i] = AC.do(lambda e, i=i: e.activation(
            pos[:, :, :], banks[i][:, 0:2 * NE].rearrange("p (j e) -> p j e", j=TT), ACT.Copy), t1, t2)
        t_pos2 = AC.last()
        t1 = t2
        t1 = VE.do(lambda e: e.tensor_reduce(place[:, :, :], dpos[:, :, :, :].rearrange("p j r e -> p (j r) e"), AXX,
                                             ALU.add), t1)
        t1 = VE.do(lambda e: e.tensor_tensor(ph[:, :, :], iota[:, :].unsqueeze(1).broadcast_to([P, two, CAP]),
                                             place[:, :, :].broadcast_to([P, two, CAP]), ALU.is_equal), t1, t_io)
        t_in = VE.do(lambda e: e.tensor_tensor(
            inpair[:, :, :, :], ph[:, :, :].unsqueeze(2).broadcast_to([P, two, 2, CAP]),
            par[:, :, :].unsqueeze(3).broadcast_to([P, two, 2, CAP]), ALU.mult), t1, t)

        b6 = Region(2048)
        xgT = [sb(f"xgT{i}", [P, KC, P], stack=b6) for i in range(2)]
        hp = [chainm[:, i * HID:(i + 1) * HID] for i in range(2)]
        hpT = [maskf[:, i * HID:(i + 1) * HID].rearrange("p (k s) -> p k s", k=4) for i in range(2)]
        pick = [sb(f"pick{i}", [P, TT, P], stack=b5) for i in range(2)]
        wpick = [sb(f"wpick{i}", [P, TT, P], stack=b5) for i in range(2)]
        assert b5.at <= ARENA - 3 * KC * 512, b5.at
        pick_free, wpick_free, wpT_free = [None] * 2, [None] * 2, [None] * 2
        xgT_free, hp_free, hpT_free, yo_free = [f4] * 2, [f4] * 2, [f4] * 2, [f4] * 2
        acc = [take("gemm") for _ in range(4)]
        t_X, t_wpT, t_Y = {}, {}, {}

        def slots_of(p, dst, weight, after):
            for j in range(TT):
                VE.do(lambda e, j=j: e.tensor_scalar(
                    dst[:, j, :], inpair[:, 2 * j, :, :].rearrange("p b s -> p (b s)"), weight[:, 2 * j, p:p + 1], None,
                    ALU.mult), after)
                t = VE.do(lambda e, j=j: e.scalar_tensor_tensor(
                    out=dst[:, j, :], in0=inpair[:, 2 * j + 1, :, :].rearrange("p b s -> p (b s)"),
                    scalar=weight[:, 2 * j + 1, p:p + 1], in1=dst[:, j, :], op0=ALU.mult, op1=ALU.add), VE.last())
            return t

        def choose(p):
            S, X = pick[p % 2], xgT[p % 2]
            for half in range(2):
                i, fr = take("side")
                for k in range(4):
                    for j in range(TT):
                        f = lambda e, i=i, k=k, j=j, half=half: e.matmul(
                            banks[i][:, k * P:(k + 1) * P], utok[:, j, 4 * half + k::KC],
                            S[:, j, :], start=j == 0, stop=j == TT - 1)
                        t = (PE.do if k == 3 and j == TT - 1 else PE.quiet)(f, t_pick[p], t_utok, fr)
                f = ((lambda e, i=i, half=half: e.tensor_copy(
                    X[:, 4 * half:4 * half + 4, :], banks[i][:, :].rearrange("p (k s) -> p k s", k=4))) if half else
                    (lambda e, i=i, half=half: e.activation(
                        X[:, 4 * half:4 * half + 4, :], banks[i][:, :].rearrange("p (k s) -> p k s", k=4), ACT.Copy)))
                t2 = (VE if half else AC).do(f, t, xgT_free[p % 2])
                bank_free[i] = t2
                t_X[p, half] = t2
            pick_free[p % 2] = t

        def combine(p):
            for n in range(2):
                for j in range(TT):
                    bk, fr = acc[2 * j + n]
                    t = PE.do(lambda e, bk=bk, j=j, n=n: e.matmul(
                        banks[bk][:, :], wpT[p % 2][:, j * P:(j + 1) * P], yo[p % 2][:, n * 512:(n + 1) * 512],
                        start=p == 0, stop=p == NPAIR - 1, skip_group_check=True), t_wpT[p], t_Y[p, n], fr)
                    t_acc[j, n] = t
            wpT_free[p % 2] = yo_free[p % 2] = t

        def expert_blocks(w, experts):
            kc = 4 if w == "down" else KC
            got = []
            for half in range(2):
                got.append([])
                for e in experts:
                    src = a[f"expert_w_{w}_2"][0, e].rearrange("(p k) n -> p k n", p=P)
                    got[-1].append(stream(src[:, half * kc // 2:(half + 1) * kc // 2, :]))
            return got

        t_pick, t_acc = {}, {}
        t_pick[0] = slots_of(0, pick[0], pair, t_in)
        choose(0)

        t = VE.do(lambda e: e.tensor_tensor(eg, gl, gmax.broadcast_to([P, TT, 4]), ALU.subtract), t_g)
        t1 = AC.do(lambda e: e.activation(eg, eg, ACT.Exp), t)
        t = VE.do(lambda e: e.tensor_tensor(e2, m2, m1, ALU.subtract), t_in)
        t2 = AC.do(lambda e: e.activation(e2, e2, ACT.Exp), t)
        t = VE.do(lambda e: e.tensor_reduce(gsum, eg, AXX, ALU.add), t1)
        t = VE.do(lambda e: e.reciprocal(gsum, gsum), t)
        w1, w2_ = w12[:, :, 0:1], w12[:, :, 1:2]
        t2 = VE.do(lambda e: e.tensor_scalar(w1, e2, 1.0, None, ALU.add), t2)
        t2 = VE.do(lambda e: e.reciprocal(w1, w1), t2)
        t = VE.do(lambda e: e.tensor_tensor(w1, w1, gsum, ALU.mult), t, t2)
        t = VE.do(lambda e: e.tensor_tensor(w2_, w1, e2, ALU.mult), t)
        for j in range(TT):
            t_wp = VE.do(lambda e, j=j: e.tensor_tensor(
                wpair[:, 2 * j:2 * j + 2, :], pair[:, 2 * j:2 * j + 2, :],
                w12[:, j, :].unsqueeze(2).broadcast_to([P, 2, NPAIR]), ALU.mult), t)
        t_w12 = t

        def count_over():
            t1 = VE.do(lambda e: e.tensor_scalar(isover[:, :, :], pos[:, :, :], float(CAP), None, ALU.is_ge), t_in, t_pos2)
            t1 = VE.do(lambda e: e.tensor_tensor(sel, sel, isover[:, :, :], ALU.mult), t1, PE.last())
            t1 = VE.do(lambda e: e.tensor_reduce(over[:, 0:2].unsqueeze(2), sel, AXX, ALU.add), t1)
            i, fr = take("side")
            t1 = PE.do(lambda e, i=i: e.matmul(banks[i][:, 0:2], ones[:, :], over[:, 0:2], start=True, stop=True), t1, fr)
            t1 = VE.do(lambda e, i=i: e.tensor_copy(over[:, 2:4], banks[i][:, 0:2]), t1)
            bank_free[i] = t1
            t1 = VE.do(lambda e: e.tensor_tensor(over[:, 0:1], over[:, 2:3], over[:, 3:4], ALU.add), t1)
            VE.do(lambda e: e.tensor_copy(flag[:, :], over[:, 0:1]), t1)
            for j in range(TT):
                t1 = VE.do(lambda e, j=j: e.tensor_scalar(wov[:, j, :], d12[:, j, 0, :], w1[:, j, :], None, ALU.mult), t_w12)
                t1 = VE.do(lambda e, j=j: e.scalar_tensor_tensor(
                    out=wov[:, j, :], in0=d12[:, j, 1, :], scalar=w2_[:, j, :], in1=wov[:, j, :],
                    op0=ALU.mult, op1=ALU.add), t1)
            VE.do(lambda e: e.tensor_tensor(wov[:, :, :], wov[:, :, :], isover[:, :, :], ALU.mult), t1)

        for p in range(NPAIR):
            E2 = (2 * p, 2 * p + 1)
            X, H, HT, Y = xgT[p % 2], hp[p % 2], hpT[p % 2], yo[p % 2]
            if p + 1 < NPAIR:
                t_pick[p + 1] = slots_of(p + 1, pick[(p + 1) % 2], pair, [t_in, pick_free[(p + 1) % 2]])
            t_wpick = slots_of(p, wpick[p % 2], wpair, [t_wp, wpick_free[p % 2]])
            for w in ("gate", "up"):
                bl = expert_blocks(w, E2)
                bk, fr = take("side")
                for k in range(KC):
                    half, kk = divmod(k, KC // 2)
                    for s_ in range(2):
                        slot, wt, t_w = bl[half][s_]
                        f = lambda e, bk=bk, s_=s_, k=k, kk=kk, wt=wt, X=X: e.matmul(
                            banks[bk][64 * s_:64 * s_ + 64, :], X[:, k, 64 * s_:64 * s_ + 64], wt[:, kk, :],
                            start=k == 0, stop=k == KC - 1)
                        t = (PE.do if kk == KC // 2 - 1 else PE.quiet)(f, t_w, fr, t_X[p, k // 4])
                        slot.free = t
                if w == "gate":
                    t = AC.do(lambda e, bk=bk, H=H: e.activation(H, banks[bk][:, :], ACT.Silu), t, hp_free[p % 2])
                    bank_free[bk] = t
                    tgate = t
                else:
                    t_H = VE.do(lambda e, bk=bk, H=H: e.tensor_tensor(H, banks[bk][:, :], H, ALU.mult), t, tgate)
                    bank_free[bk] = t_H
            xgT_free[p % 2] = PE.last()
            if p == 0:
                count_over()
            i, fr = take("side")
            for j in range(TT):
                f = lambda e, i=i, j=j, p=p: e.transpose(banks[i][:, j * P:(j + 1) * P], wpick[p % 2][:, j, :],
                                                         ident[:, :])
                t = (PE.do if j == TT - 1 else PE.quiet)(f, t_wpick, fr)
            wpick_free[p % 2] = t
            t_wpT[p] = AC.do(lambda e, i=i, p=p: e.activation(wpT[p % 2][:, :], banks[i][:, 0:T], ACT.Copy), t,
                             wpT_free[p % 2])
            bank_free[i] = t_wpT[p]
            if p:
                combine(p - 1)
            i, fr = take("side")
            for c in range(4):
                f = lambda e, i=i, c=c, H=H: e.transpose(banks[i][:, c * P:(c + 1) * P], H[:, c::4],
                                                         ident[:, :])
                t2 = (PE.do if c == 3 else PE.quiet)(f, t_H, fr)
            hp_free[p % 2] = t2
            t_HT = AC.do(lambda e, i=i, HT=HT: e.activation(HT, banks[i][:, :].rearrange(
                "p (k s) -> p k s", k=4), ACT.Copy), t2, hpT_free[p % 2])
            bank_free[i] = t_HT
            if p + 1 < NPAIR:
                choose(p + 1)
            bl = expert_blocks("down", E2)
            got = [take("side") for _ in range(2)]
            for k in range(4):
                half, kk = divmod(k, 2)
                for n in range(2):
                    bk, fr = got[n]
                    for s_ in range(2):
                        slot, wt, t_w = bl[half][s_]
                        f = lambda e, bk=bk, s_=s_, k=k, kk=kk, n=n, wt=wt, HT=HT: e.matmul(
                            banks[bk][64 * s_:64 * s_ + 64, :], HT[:, k, 64 * s_:64 * s_ + 64],
                            wt[:, kk, n * 512:(n + 1) * 512], start=k == 0, stop=k == 3)
                        t3 = (PE.do if kk == 1 else PE.quiet)(f, t_w, fr, t_HT)
                        slot.free = t3
            for n in range(2):
                bk = got[n][0]
                t_Y[p, n] = (AC if n else VE).do(
                    (lambda e, bk=bk, Y=Y: e.activation(Y[:, 512:1024], banks[bk][:, :], ACT.Copy)) if n else
                    (lambda e, bk=bk, Y=Y: e.tensor_copy(Y[:, 0:512], banks[bk][:, :])), t3, yo_free[p % 2])
                bank_free[bk] = t_Y[p, n]
            hpT_free[p % 2] = PE.last()
        combine(NPAIR - 1)
        for n in range(2):
            for j in range(TT):
                o = xtok2[:, j, n * 512:(n + 1) * 512]
                VE.do(lambda e, j=j, n=n, o=o: e.tensor_tensor(o, banks[acc[2 * j + n][0]][:, :], o, ALU.add),
                      t_acc[j, n])
        VE.quiet(lambda e: e.wait_ge(VE.sem, VE.count))
        AC.quiet(lambda e: e.wait_ge(t_fr[0], t_fr[1]))

        with nc.Block() as block:
            block.sync(SP.emit)
            block.scalar(AC.emit)
            block.vector(VE.emit)
            block.gpsimd(PO.emit)
            block.tensor(PE.emit)

        hidT = chainm[:, :].rearrange("p (k t) -> p k t", k=4)
        loop_sems = [nc.alloc_semaphore(f"loop{i}") for i in range(6)]
        first = loop_sems[0].num
        assert [x.num for x in loop_sems] == list(range(first, first + 6))
        n_over = nc.values_load(flag[0:1, 0:1], min_val=0, max_val=2 * T)
        with nc.If(n_over > 0):
            with nc.Fori(0, NE) as ex:
                lPE, lAC, lVE = (Queue(n, s) for n, s in zip(("pe", "act", "dve"), loop_sems[3:6]))
                W = []
                for i, (name, kc, cols) in enumerate((("gate", KC, HID), ("up", KC, HID), ("down", 4, D))):
                    w = whole[i][:, 0:kc * cols].rearrange("p (k n) -> p k n", k=kc)
                    src = a[f"expert_w_{name}_2"][0, bass.ds(ex, 1)].rearrange("o (k p) n -> p (o k) n", p=P)
                    nc.sync.dma_start(w, src).then_inc(loop_sems[i], 16)
                    W.append((w, (loop_sems[i], 16)))
                t_wc = lVE.do(lambda e: e.tensor_copy(wcol[:, :, :], wov[:, :, bass.ds(ex, 1)]))
                for m in range(2):
                    for c in range(4):
                        for k in range(KC):
                            whole = c == 3 and k == KC - 1
                            (lPE.do if whole else lPE.quiet)(lambda e, m=m, c=c, k=k: e.matmul(
                                banks[2 * m + c // 2][:, (c % 2) * T:(c % 2 + 1) * T],
                                W[m][0][:, k, c * P:(c + 1) * P], uTe[:, k, :], start=k == 0, stop=k == KC - 1),
                                W[m][1])
                t_h = None
                for b in range(2):
                    h2 = hidT[:, 2 * b:2 * b + 2, :].rearrange("p c t -> p (c t)")
                    t_s = lAC.do(lambda e, b=b, h2=h2: e.activation(h2, banks[b][:, :], ACT.Silu), (lPE.sem, 1))
                    t_h = lVE.do(lambda e, b=b, h2=h2: e.tensor_tensor(h2, banks[2 + b][:, :], h2, ALU.mult),
                                 t_s, (lPE.sem, 2))
                for j in range(TT):
                    for n in range(2):
                        for k in range(4):
                            f = lambda e, j=j, n=n, k=k: e.matmul(
                                banks[4 + 2 * j + n][:, :], hidT[:, k, j * P:(j + 1) * P],
                                W[2][0][:, k, n * 512:(n + 1) * 512], start=k == 0, stop=k == 3)
                            t = (lPE.do if k == 3 else lPE.quiet)(f, W[2][1], t_h)
                        o = xtok2[:, j, n * 512:(n + 1) * 512]
                        lVE.do(lambda e, j=j, n=n, o=o: e.scalar_tensor_tensor(
                            out=o, in0=banks[4 + 2 * j + n][:, :], scalar=wcol[:, j, :], in1=o,
                            op0=ALU.mult, op1=ALU.add), t, t_wc)
                lPE.emit(nc.tensor)
                lAC.emit(nc.scalar)
                lVE.emit(nc.vector)
                nc.vector.wait_ge(lVE.sem, lVE.count)
                nc.all_engine_barrier(sems_to_clear=range(first, first + 6))

        ss2 = small[:, 34:36]
        sq = [yo[j][:, :] for j in range(TT)]
        res = [utok[:, j, :] for j in range(TT)]
        outs = []
        tAC, tVE, tSP = (Queue(n, sem("s_tail_" + n)) for n in ("act", "dve", "sp"))
        for j in range(TT):
            o = xtok2[:, j, :]
            t = tAC.do(lambda e, j=j, o=o: e.activation(sq[j], o, ACT.Square, accum_out=ss2[:, j:j + 1]))
            t = tAC.do(lambda e, j=j: e.activation(ss2[:, j:j + 1], ss2[:, j:j + 1], ACT.Sqrt, bias=epsc[:, 0:1],
                                                   scale=1.0 / D), t)
            t = tVE.do(lambda e, j=j: e.reciprocal(ss2[:, j:j + 1], ss2[:, j:j + 1]), t)
            t = tVE.do(lambda e, j=j, o=o: e.scalar_tensor_tensor(
                out=res[j], in0=o, scalar=ss2[:, j:j + 1], in1=frow[:, :], op0=ALU.mult, op1=ALU.mult), t)
            outs.append(load(tSP, f"out{j}", out[0, j * P:(j + 1) * P, :], res[j], t))

        def store(e):
            tSP.emit(e)
            for s, v in outs:
                e.wait_ge(s, v)

        with nc.Block() as block:
            block.scalar(tAC.emit)
            block.vector(tVE.emit)
            block.sync(store)


def two_pi_parts():
    rest, parts = 2 * np.pi, []
    for bits in (9, 11):
        scale = 2.0 ** (bits - 3)
        part = np.floor(rest * scale * 2.0 ** (0 if not parts else 9)) / (scale * 2.0 ** (0 if not parts else 9))
        parts.append(float(part))
        rest -= part
    return parts + [float(np.float32(rest))]


TWO_PI_PARTS = two_pi_parts()


def constants():
    s, t = np.arange(P)[:, None], np.arange(P)[None, :]
    masks = np.zeros((P, len(LEVELS), P), np.int32)
    for i, m in enumerate(LEVELS):
        masks[:, i, :] = (s == t) if m == 1 else ((s // m == t // m) & (s % m < m // 2) & (t % m >= m // 2))
    far = 1.0e32
    q, k = np.arange(P)[:, None], np.arange(T)[None, :]
    d0 = (q - k[:, :P]).astype(np.float64)
    d1 = (q + P - k).astype(np.float64)
    dist = np.concatenate([np.where(d0 >= 0, d0, far), np.where(d1 >= 0, d1, far)], 1).astype(np.float32)
    lg = np.log(1.0 - 2.0 ** (-5.0 - np.arange(HEADS)))
    dec = np.zeros((P, HEADS, 384), np.float32)
    for h in range(HEADS):
        r0 = np.arange(T)[None, :] - s
        r1 = t - s
        r = np.concatenate([r0, r1], 1)
        dec[:, h] = np.where(r >= 0, np.exp(lg[h] * np.maximum(r, 0)), 0.0)
    theta = (np.float32(1.0) / np.power(np.float32(10000.0), np.linspace(0.0, 1.0, P, dtype=np.float32)))
    iota = np.tile(np.arange(CAP, dtype=np.float32), (P, 1))
    return {"ident": np.eye(P, dtype=np.float32), "masks": masks, "dist": dist, "decay": dec,
            "theta": theta.astype(np.float32).reshape(P, 1), "tri": (s < t).astype(np.float32), "iota": iota}


def kernel(**inputs):
    import concourse.bacc as bacc
    from concourse.bass_utils import run_bass_kernel_spmd

    nc = bacc.Bacc("TRN2", target_bir_lowering=False, num_devices=1)
    arrays, a = {}, {}
    for name, x in {**inputs, **constants()}.items():
        x = np.ascontiguousarray(x)
        arrays["in_" + name] = x
        a[name] = nc.dram_tensor("in_" + name, x.shape, mybir.dt.from_np(x.dtype), kind="ExternalInput").ap()
    out = nc.dram_tensor("out_0", (1, T, D), F32, kind="ExternalOutput").ap()
    build(nc, a, out)
    r = run_bass_kernel_spmd(nc, [arrays], core_ids=[0])
    return r.results[0]["out_0"]
```
